# Optimizing a Trainium2 kernel written in Bass

```python
import jax, jax.numpy as jnp
from jax import lax
import numpy as np

D_MODEL = 1024
BATCH = 1
SEQ = 512
DEPTH = 2

GRID_W = 64
CTX_LEN = 256
N_MIXERS = 4
ROPE_BASE = 10000.0
Q_BLOCK = 128
NORM_EPS = 1e-6
FFN_DIM = 4 * D_MODEL
ADALN_CHUNKS = 6

GQA_HEAD_DIM = 64
GQA_HEADS = D_MODEL // GQA_HEAD_DIM
GQA_KV_HEADS = GQA_HEADS // 4

RWKV_HEAD = 64
RWKV_HEADS = D_MODEL // RWKV_HEAD
RWKV_DECAY_LORA = 64
RWKV_A_LORA = 64
RWKV_G_LORA = 128
RWKV_GN_EPS = 64e-5

MLA_HEADS = 16
MLA_Q_RANK = D_MODEL // 2
MLA_KV_RANK = D_MODEL // 4
MLA_NOPE = 64
MLA_ROPE = 32
MLA_V = D_MODEL // MLA_HEADS

GLA_HEADS = 4
GLA_DK = D_MODEL // 2 // GLA_HEADS
GLA_DV = D_MODEL // GLA_HEADS
GLA_GATE_RANK = 16
GLA_TAU = 16.0
GLA_CHUNK = 64

kernel_name = 'hybrid_flow_backbone'

def rms_norm(x, g, eps=NORM_EPS):
    xf = x.astype(jnp.float32)
    y = xf * lax.rsqrt(jnp.mean(xf * xf, axis=-1, keepdims=True) + eps)
    return (y * g.astype(jnp.float32)).astype(x.dtype)

def modulate(u, shift, scale):
    return u * (1 + scale) + shift

def sq_relu_mlp(u, w_up, w_down):
    return jnp.square(jax.nn.relu(u @ w_up)) @ w_down

def grid_rope(rows, rot_dim, dtype):
    row = jnp.repeat(jnp.arange(rows), GRID_W).astype(jnp.float32)
    col = jnp.tile(jnp.arange(GRID_W), rows).astype(jnp.float32)
    n_freq = rot_dim // 4
    inv_freq = ROPE_BASE ** (-jnp.arange(n_freq, dtype=jnp.float32) / n_freq)
    ang = jnp.concatenate([row[:, None] * inv_freq, col[:, None] * inv_freq], axis=-1)
    return jnp.cos(ang).astype(dtype), jnp.sin(ang).astype(dtype)

def apply_rope(x, cos, sin):
    half = x.shape[-1] // 2
    x1, x2 = x[..., :half], x[..., half:]
    c, s = cos[:, None, :], sin[:, None, :]
    return jnp.concatenate([x1 * c - x2 * s, x1 * s + x2 * c], axis=-1)

def attend(q, k, v, scale):
    B, Tq, H, dq = q.shape
    Hk = k.shape[2]
    qg = q.reshape(B, Tq, Hk, H // Hk, dq)
    s = jnp.einsum('bqkgd,blkd->bkgql', qg, k).astype(jnp.float32) * scale
    p = jax.nn.softmax(s, axis=-1).astype(v.dtype)
    o = jnp.einsum('bkgql,blkd->bqkgd', p, v)
    return o.reshape(B, Tq, H, v.shape[-1])

def block_attention(q, k, v, scale):
    B, T, H, dq = q.shape
    qb = jnp.moveaxis(q.reshape(B, T // Q_BLOCK, Q_BLOCK, H, dq), 1, 0)
    ob = lax.map(lambda qi: attend(qi, k, v, scale), qb)
    return jnp.moveaxis(ob, 0, 1).reshape(B, T, H, v.shape[-1])

def attend_streams(q_c, k_c, v_c, q_x, k_x, v_x, scale, w_out):
    B, S = q_x.shape[:2]
    k_all = jnp.concatenate([k_c, k_x], axis=1)
    v_all = jnp.concatenate([v_c, v_x], axis=1)
    y_x = block_attention(q_x, k_all, v_all, scale).reshape(B, S, -1) @ w_out
    if q_c is None:
        return None, y_x
    y_c = block_attention(q_c, k_c, v_c, scale).reshape(B, q_c.shape[1], -1) @ w_out
    return y_c, y_x

def gqa_mixer(u_c, u_x, w_in, q_gain, k_gain, w_out, rope, with_ctx_out):
    hd = GQA_HEAD_DIM
    nq, nkv = GQA_HEADS * hd, GQA_KV_HEADS * hd

    def project(u, pos, with_q):
        B, T, _ = u.shape
        off = nq if with_q else 0
        z = u @ (w_in if with_q else w_in[:, nq:])
        k = rms_norm(z[..., off:off + nkv].reshape(B, T, GQA_KV_HEADS, hd), k_gain)
        v = z[..., off + nkv:].reshape(B, T, GQA_KV_HEADS, hd)
        if pos is not None:
            k = apply_rope(k, *pos)
        if not with_q:
            return None, k, v
        q = rms_norm(z[..., :nq].reshape(B, T, GQA_HEADS, hd), q_gain)
        if pos is not None:
            q = apply_rope(q, *pos)
        return q, k, v

    q_c, k_c, v_c = project(u_c, None, with_ctx_out)
    q_x, k_x, v_x = project(u_x, rope, True)
    return attend_streams(q_c, k_c, v_c, q_x, k_x, v_x, hd ** -0.5, w_out)

def mla_mixer(u_c, u_x, w_in, q_gain, kv_gain, w_uq, w_ukv, w_out, rope, with_ctx_out):
    H = MLA_HEADS

    def project(u, pos, with_q):
        B, T, _ = u.shape
        z = u @ (w_in if with_q else w_in[:, MLA_Q_RANK:])
        z_kv = z[..., z.shape[-1] - MLA_KV_RANK - MLA_ROPE:]
        kv = (rms_norm(z_kv[..., :MLA_KV_RANK], kv_gain) @ w_ukv).reshape(B, T, H, MLA_NOPE + MLA_V)
        k_rope = z_kv[..., MLA_KV_RANK:][:, :, None, :]
        if pos is not None:
            k_rope = apply_rope(k_rope, *pos)
        k = jnp.concatenate([kv[..., :MLA_NOPE], jnp.broadcast_to(k_rope, (B, T, H, MLA_ROPE))], axis=-1)
        v = kv[..., MLA_NOPE:]
        if not with_q:
            return None, k, v
        q = (rms_norm(z[..., :MLA_Q_RANK], q_gain) @ w_uq).reshape(B, T, H, MLA_NOPE + MLA_ROPE)
        if pos is not None:
            q = jnp.concatenate([q[..., :MLA_NOPE], apply_rope(q[..., MLA_NOPE:], *pos)], axis=-1)
        return q, k, v

    q_c, k_c, v_c = project(u_c, None, with_ctx_out)
    q_x, k_x, v_x = project(u_x, rope, True)
    return attend_streams(q_c, k_c, v_c, q_x, k_x, v_x, (MLA_NOPE + MLA_ROPE) ** -0.5, w_out)

def centred_shift(u):
    prev = jnp.pad(u[:, :-1], ((0, 0), (1, 0), (0, 0)))
    nxt = jnp.pad(u[:, 1:], ((0, 0), (0, 1), (0, 0)))
    return 0.5 * (prev + nxt)

def rwkv_side(u, mu, w_rkv, w0, w1, w2, a0, a1, a2, g1, g2, k_k, k_a, with_out):
    B, T, D = u.shape
    H, N = RWKV_HEADS, RWKV_HEAD
    xx = centred_shift(u) - u
    mix = lambda i: u + xx * mu[i]
    xw, xk, xv, xa = mix(1), mix(2), mix(3), mix(4)
    k = xk @ w_rkv[1]
    v = xv @ w_rkv[2]
    lora = lambda xin, wa, wb: jnp.einsum('nbtr,nrd->nbtd', xin, wb) if wa is None else None
    w_log = -jax.nn.softplus(-(w0[:, None, None, :] + jnp.einsum('nbtr,nrd->nbtd', jnp.tanh(jnp.einsum('btd,ndr->nbtr', xw, w1)), w2))) - 0.5
    a = jax.nn.sigmoid(a0[:, None, None, :] + jnp.einsum('nbtr,nrd->nbtd', jnp.einsum('btd,ndr->nbtr', xa, a1), a2))
    kk = (k * k_k).reshape(B, T, H, N).astype(jnp.float32)
    kk = (kk / jnp.maximum(jnp.sqrt(jnp.sum(kk * kk, axis=-1, keepdims=True)), 1e-12)).reshape(B, T, D)
    k_dir = k[None] * (1 + (a - 1) * k_a)
    decay = jnp.exp(-jnp.exp(w_log.astype(jnp.float32)))

    def lay(t):
        t = jnp.stack([t[0], jnp.flip(t[1], axis=1)]).astype(jnp.float32)
        return jnp.moveaxis(t.reshape(2, B, T, H, N), 2, 0)

    both = lambda t: jnp.stack([t, t])
    scan_in = (lay(decay), lay(k_dir), lay(both(v)), lay(both(-kk)), lay(kk[None] * a))
    if not with_out:
        return scan_in, None
    r = mix(0) @ w_rkv[0]
    g = jax.nn.sigmoid(mix(5) @ g1) @ g2
    return scan_in + (lay(both(r)),), (r, k_dir, v, g)

def rwkv_scan(scan_in, S0, with_out):
    def step(S, inp):
        w_t, k_t, v_t, a_t, b_t = inp[:5]
        sa = jnp.einsum('dbhij,dbhj->dbhi', S, a_t)
        S = S * w_t[..., None, :] + sa[..., :, None] * b_t[..., None, :] + v_t[..., :, None] * k_t[..., None, :]
        return S, (jnp.einsum('dbhij,dbhj->dbhi', S, inp[5]) if with_out else None)

    S, ys = lax.scan(step, S0, scan_in)
    if not with_out:
        return S, None
    ys = jnp.moveaxis(ys, 0, 2)
    return S, ys[0] + jnp.flip(ys[1], axis=1)

def rwkv_out(y, r, k_dir, v, g, r_k, ln_w, ln_b, w_out):
    B, T, H, N = y.shape
    mean = jnp.mean(y, axis=-1, keepdims=True)
    var = jnp.mean(jnp.square(y - mean), axis=-1, keepdims=True)
    yn = ((y - mean) * lax.rsqrt(var + RWKV_GN_EPS)).reshape(B, T, H * N) * ln_w + ln_b
    rk = jnp.sum((r[None] * k_dir).reshape(2, B, T, H, N) * r_k, axis=(0, -1))[..., None]
    yn = yn + (rk * v.reshape(B, T, H, N)).reshape(B, T, H * N)
    return (yn.astype(v.dtype) * g) @ w_out

def rwkv_mixer(u_c, u_x, mu, w_rkv, w0, w1, w2, a0, a1, a2, g1, g2, k_k, k_a, r_k, ln_w, ln_b, w_out, with_ctx_out):
    B = u_x.shape[0]
    side = lambda u, wo: rwkv_side(u, mu, w_rkv, w0, w1, w2, a0, a1, a2, g1, g2, k_k, k_a, wo)
    in_c, aux_c = side(u_c, with_ctx_out)
    S0 = jnp.zeros((2, B, RWKV_HEADS, RWKV_HEAD, RWKV_HEAD), jnp.float32)
    S_c, y_c = rwkv_scan(in_c, S0, with_ctx_out)
    in_x, aux_x = side(u_x, True)
    _, y_x = rwkv_scan(in_x, S_c, True)
    out_x = rwkv_out(y_x, *aux_x, r_k, ln_w, ln_b, w_out)
    if not with_ctx_out:
        return None, out_x
    return rwkv_out(y_c, *aux_c, r_k, ln_w, ln_b, w_out), out_x

def gla_side(u, w_in, gate_down, gate_up, gate_bias, with_out):
    B, T, _ = u.shape
    H, dk, dv = GLA_HEADS, GLA_DK, GLA_DV
    nk, nv = H * dk, H * dv
    off = nk if with_out else 0
    z = u @ (w_in if with_out else w_in[:, nk:2 * nk + nv])
    k = z[..., off:off + nk]
    v = z[..., off + nk:off + nk + nv]
    g_lin = jnp.einsum('nbtr,nrk->nbtk', jnp.einsum('btd,ndr->nbtr', u, gate_down), gate_up) + gate_bias[:, None, None, :]
    g = jax.nn.log_sigmoid(g_lin.astype(jnp.float32)) / GLA_TAU

    def lay(t, d):
        t = jnp.stack([t[0], jnp.flip(t[1], axis=1)]).astype(jnp.float32)
        return jnp.moveaxis(t.reshape(2, B, T // GLA_CHUNK, GLA_CHUNK, H, d), 2, 0)

    both = lambda t: jnp.stack([t, t])
    scan_in = (lay(both(k), dk), lay(both(v), dv), lay(g, dk))
    if not with_out:
        return scan_in, None
    q = z[..., :nk] * dk ** -0.5
    return scan_in + (lay(both(q), dk),), z[..., 2 * nk + nv:]

def gla_scan(scan_in, S0, with_out):
    C = GLA_CHUNK
    causal = jnp.tril(jnp.ones((C, C), dtype=bool))[:, :, None, None]

    def step(S, inp):
        k_c, v_c, g_c = inp[:3]
        b = jnp.cumsum(g_c, axis=2)
        b_last = b[:, :, -1]
        S_new = S * jnp.exp(b_last)[..., None] + jnp.einsum('xbshk,xbshv->xbhkv', k_c * jnp.exp(b_last[:, :, None] - b), v_c)
        if not with_out:
            return S_new, None
        q_c = inp[3]
        o = jnp.einsum('xbthk,xbhkv->xbthv', q_c * jnp.exp(b), S)
        dec = jnp.exp(jnp.where(causal, b[:, :, :, None] - b[:, :, None, :], -jnp.inf))
        att = jnp.einsum('xbtshk,xbshk->xbhts', q_c[:, :, :, None] * dec, k_c)
        o = o + jnp.einsum('xbhts,xbshv->xbthv', att, v_c)
        return S_new, o

    S, ys = lax.scan(step, S0, scan_in)
    if not with_out:
        return S, None
    n, _, B, _, H, dv = ys.shape
    ys = jnp.moveaxis(ys, 0, 2).reshape(2, B, n * C, H, dv)
    return S, ys[0] + jnp.flip(ys[1], axis=1)

def gla_out(o, gout, o_gain, w_out):
    B, T, H, dv = o.shape
    o = rms_norm(o, o_gain).reshape(B, T, H * dv).astype(gout.dtype)
    return (o * jax.nn.silu(gout)) @ w_out

def gla_mixer(u_c, u_x, w_in, gate_down, gate_up, gate_bias, o_gain, w_out, with_ctx_out):
    B = u_x.shape[0]
    in_c, gout_c = gla_side(u_c, w_in, gate_down, gate_up, gate_bias, with_ctx_out)
    S0 = jnp.zeros((2, B, GLA_HEADS, GLA_DK, GLA_DV), jnp.float32)
    S_c, o_c = gla_scan(in_c, S0, with_ctx_out)
    in_x, gout_x = gla_side(u_x, w_in, gate_down, gate_up, gate_bias, True)
    _, o_x = gla_scan(in_x, S_c, True)
    y_x = gla_out(o_x, gout_x, o_gain, w_out)
    if not with_ctx_out:
        return None, y_x
    return gla_out(o_c, gout_c, o_gain, w_out), y_x

def setup_inputs(seed: int = 0) -> dict:
    key = jax.random.key(seed)
    keys = iter(jax.random.split(key, 128))
    D = D_MODEL

    def nrm(shape, std):
        return std * jax.random.normal(next(keys), shape, jnp.float32)

    def lin(*shape):
        return nrm(shape, shape[-2] ** -0.5)

    def gain(n):
        return 1.0 + nrm((n,), 0.05)

    p = {}
    p['x'] = nrm((BATCH, SEQ, D), 1.0)
    p['c'] = nrm((BATCH, D), 1.0)
    p['ctx'] = nrm((BATCH, CTX_LEN, D), 1.0)
    p['c_ctx'] = nrm((D,), 1.0)

    def head(i):
        p[f'l{i}_ada_w'] = nrm((D, ADALN_CHUNKS * D), 0.5 * D ** -0.5)
        p[f'l{i}_ada_b'] = nrm((ADALN_CHUNKS * D,), 0.02)
        p[f'l{i}_norm1'] = gain(D)

    def tail(i):
        p[f'l{i}_norm2'] = gain(D)
        p[f'l{i}_mlp_up'] = lin(D, FFN_DIM)
        p[f'l{i}_mlp_down'] = lin(FFN_DIM, D)

    head(0)
    p['l0_w_in'] = lin(D, (GQA_HEADS + 2 * GQA_KV_HEADS) * GQA_HEAD_DIM)
    p['l0_q_gain'] = gain(GQA_HEAD_DIM)
    p['l0_k_gain'] = gain(GQA_HEAD_DIM)
    p['l0_w_out'] = lin(GQA_HEADS * GQA_HEAD_DIM, D)
    tail(0)

    head(1)
    p['l1_mu'] = jax.random.uniform(next(keys), (6, D), jnp.float32)
    p['l1_w_rkv'] = lin(3, D, D)
    p['l1_w0'] = nrm((2, D), 0.3)
    p['l1_w1'] = nrm((2, D, RWKV_DECAY_LORA), 0.5 * D ** -0.5)
    p['l1_w2'] = nrm((2, RWKV_DECAY_LORA, D), 0.5 * RWKV_DECAY_LORA ** -0.5)
    p['l1_a0'] = nrm((2, D), 0.1)
    p['l1_a1'] = nrm((2, D, RWKV_A_LORA), 0.5 * D ** -0.5)
    p['l1_a2'] = nrm((2, RWKV_A_LORA, D), 0.5 * RWKV_A_LORA ** -0.5)
    p['l1_g1'] = lin(D, RWKV_G_LORA)
    p['l1_g2'] = lin(RWKV_G_LORA, D)
    p['l1_k_k'] = 0.85 + nrm((D,), 0.05)
    p['l1_k_a'] = 1.0 + nrm((D,), 0.05)
    p['l1_r_k'] = nrm((RWKV_HEADS, RWKV_HEAD), 0.1)
    p['l1_ln_w'] = gain(D)
    p['l1_ln_b'] = nrm((D,), 0.02)
    p['l1_w_out'] = lin(D, D)
    tail(1)

    head(2)
    p['l2_w_in'] = lin(D, MLA_Q_RANK + MLA_KV_RANK + MLA_ROPE)
    p['l2_q_gain'] = gain(MLA_Q_RANK)
    p['l2_kv_gain'] = gain(MLA_KV_RANK)
    p['l2_w_uq'] = lin(MLA_Q_RANK, MLA_HEADS * (MLA_NOPE + MLA_ROPE))
    p['l2_w_ukv'] = lin(MLA_KV_RANK, MLA_HEADS * (MLA_NOPE + MLA_V))
    p['l2_w_out'] = lin(MLA_HEADS * MLA_V, D)
    tail(2)

    head(3)
    p['l3_w_in'] = lin(D, 2 * GLA_HEADS * GLA_DK + 2 * GLA_HEADS * GLA_DV)
    p['l3_gate_down'] = lin(2, D, GLA_GATE_RANK)
    p['l3_gate_up'] = lin(2, GLA_GATE_RANK, GLA_HEADS * GLA_DK)
    p['l3_gate_bias'] = nrm((2, GLA_HEADS * GLA_DK), 0.1)
    p['l3_o_gain'] = gain(GLA_DV)
    p['l3_w_out'] = lin(GLA_HEADS * GLA_DV, D)
    tail(3)

    p['final_norm'] = gain(D)
    return p

def reference(x, c, ctx, c_ctx,
              l0_ada_w, l0_ada_b, l0_norm1, l0_w_in, l0_q_gain, l0_k_gain, l0_w_out, l0_norm2, l0_mlp_up, l0_mlp_down,
              l1_ada_w, l1_ada_b, l1_norm1, l1_mu, l1_w_rkv, l1_w0, l1_w1, l1_w2, l1_a0, l1_a1, l1_a2, l1_g1, l1_g2,
              l1_k_k, l1_k_a, l1_r_k, l1_ln_w, l1_ln_b, l1_w_out, l1_norm2, l1_mlp_up, l1_mlp_down,
              l2_ada_w, l2_ada_b, l2_norm1, l2_w_in, l2_q_gain, l2_kv_gain, l2_w_uq, l2_w_ukv, l2_w_out, l2_norm2,
              l2_mlp_up, l2_mlp_down,
              l3_ada_w, l3_ada_b, l3_norm1, l3_w_in, l3_gate_down, l3_gate_up, l3_gate_bias, l3_o_gain, l3_w_out,
              l3_norm2, l3_mlp_up, l3_mlp_down,
              final_norm):
    B, S, _ = x.shape
    rows = S // GRID_W
    rope_a = grid_rope(rows, GQA_HEAD_DIM, x.dtype)
    rope_c = grid_rope(rows, MLA_ROPE, x.dtype)
    s_c = jax.nn.silu(c)
    s_cc = jax.nn.silu(c_ctx)

    layers = (
        ((l0_ada_w, l0_ada_b, l0_norm1, l0_norm2, l0_mlp_up, l0_mlp_down),
         lambda uc, ux, wo: gqa_mixer(uc, ux, l0_w_in, l0_q_gain, l0_k_gain, l0_w_out, rope_a, wo)),
        ((l1_ada_w, l1_ada_b, l1_norm1, l1_norm2, l1_mlp_up, l1_mlp_down),
         lambda uc, ux, wo: rwkv_mixer(uc, ux, l1_mu, l1_w_rkv, l1_w0, l1_w1, l1_w2, l1_a0, l1_a1, l1_a2, l1_g1, l1_g2,
                                       l1_k_k, l1_k_a, l1_r_k, l1_ln_w, l1_ln_b, l1_w_out, wo)),
        ((l2_ada_w, l2_ada_b, l2_norm1, l2_norm2, l2_mlp_up, l2_mlp_down),
         lambda uc, ux, wo: mla_mixer(uc, ux, l2_w_in, l2_q_gain, l2_kv_gain, l2_w_uq, l2_w_ukv, l2_w_out, rope_c, wo)),
        ((l3_ada_w, l3_ada_b, l3_norm1, l3_norm2, l3_mlp_up, l3_mlp_down),
         lambda uc, ux, wo: gla_mixer(uc, ux, l3_w_in, l3_gate_down, l3_gate_up, l3_gate_bias, l3_o_gain, l3_w_out, wo)),
    )

    h = ctx
    for i in range(DEPTH):
        (ada_w, ada_b, n1, n2, w_up, w_down), mixer = layers[i]
        last = i == DEPTH - 1
        mod_x = jnp.split((s_c @ ada_w + ada_b)[:, None, :], ADALN_CHUNKS, axis=-1)
        mod_c = jnp.split((s_cc @ ada_w + ada_b)[None, None, :], ADALN_CHUNKS, axis=-1)
        u_x = modulate(rms_norm(x, n1), mod_x[0], mod_x[1])
        u_c = modulate(rms_norm(h, n1), mod_c[0], mod_c[1])
        y_c, y_x = mixer(u_c, u_x, not last)
        x = x + mod_x[2] * y_x
        x = x + mod_x[5] * sq_relu_mlp(modulate(rms_norm(x, n2), mod_x[3], mod_x[4]), w_up, w_down)
        if not last:
            h = h + mod_c[2] * y_c
            h = h + mod_c[5] * sq_relu_mlp(modulate(rms_norm(h, n2), mod_c[3], mod_c[4]), w_up, w_down)
    return rms_norm(x, final_norm)


_drawn_inputs = setup_inputs


def setup_inputs(seed=0):
    import zlib

    import numpy as np

    out = dict(_drawn_inputs(seed))
    spreads = {}
    factors = {'ctx': 4.199,
     'l0_norm1': 8.0,
     'l0_q_gain': 8.0,
     'l0_k_gain': 8.0,
     'l1_norm1': 3.766,
     'l1_w0': 3.553,
     'l1_w1': 8.0,
     'l1_w2': 8.0,
     'l1_a0': 7.308,
     'l1_a1': 3.611,
     'l1_a2': 3.618,
     'l1_k_k': 200.0,
     'l1_k_a': 4.391,
     'l1_ln_w': 59.368,
     'l1_ln_b': 200.0,
     'l1_norm2': 8.0}
    for name, (base, spread) in spreads.items():
        noise = np.random.default_rng([zlib.crc32(name.encode()), seed]).standard_normal(out[name].shape)
        drawn = base * np.exp(spread * noise) if base else spread * noise
        out[name] = __import__('jax').numpy.asarray(drawn.astype(out[name].dtype))
    for name, factor in factors.items():
        out[name] = (out[name] * factor).astype(out[name].dtype)
    return out
```

```python
import math
from contextlib import ExitStack

import numpy as np

import concourse.bass as bass
from concourse import mybir

F32 = mybir.dt.float32
F32R = mybir.dt.float32r
ALU = mybir.AluOpType
ACT = mybir.ActivationFunctionType
AX = mybir.AxisListType

P = 128
D = 1024
KT = D // P
TC, TX = 256, 512
T = TC + TX
NTT = T // P
FF = 4 * D
GRID_W = 64
EPS = 1e-6
HD = 64
UC = 256
C = 64
NCH = T // C
GN_EPS = 64e-5
DEC = float(np.exp(-0.5))
SCALE = HD ** -0.5
GROUP_LOADS = 7
STREAMS = ((0, TC), (TC, T))


def const_table():
    f = np.float32
    t = {}
    t["ident"] = np.eye(P, dtype=f)
    head = np.kron(np.eye(2), np.ones((HD, HD))).astype(f)
    t["head_ones"] = head
    swap = np.zeros((P, P), f)
    for h in range(2):
        for i in range(HD):
            swap[h * HD + (i + HD // 2) % HD, h * HD + i] = 1.0
    t["swap"] = swap
    tok = np.arange(TX)
    row, col = (tok // GRID_W).astype(f), (tok % GRID_W).astype(f)
    nf = HD // 4
    inv = (f(10000.0) ** (-np.arange(nf, dtype=f) / f(nf))).astype(f)
    ang = np.concatenate([row[:, None] * inv, col[:, None] * inv], axis=-1).astype(f)
    c, s = np.cos(ang).T.astype(f), np.sin(ang).T.astype(f)
    t["rope_cos"] = np.concatenate([c, c, c, c], 0)
    t["rope_sin"] = np.concatenate([-s, s, -s, s], 0)
    i = np.arange(P)
    same = (i[:, None] // C) == (i[None, :] // C)
    for d in range(2):
        before = (i[:, None] < i[None, :]) if d == 0 else (i[:, None] > i[None, :])
        strict = (before & same).astype(f)
        incl = strict + np.eye(P, dtype=f)
        t[f"cum{d}"] = incl
        t[f"masks{d}"] = np.concatenate([strict, incl], 1)
        lv = []
        for l in range(6):
            b = 1 << l
            m = ((i[:, None] // (2 * b)) == (i[None, :] // (2 * b))) & ((i[:, None] // b) != (i[None, :] // b))
            lv.append((m & (strict.T > 0)).astype(f))
        for l in range(6):
            t[f"level{d}{l}"] = lv[l]
        t[f"level0T{d}"] = lv[0].T.copy()
    return t


PARAM = {"ada_b0": "l0_ada_b", "ada_b1": "l1_ada_b", "norm1_0": "l0_norm1", "norm2_0": "l0_norm2",
         "norm1_1": "l1_norm1", "norm2_1": "l1_norm2", "mu": "l1_mu", "k_k": "l1_k_k", "k_a": "l1_k_a",
         "r_k": "l1_r_k", "ln_w": "l1_ln_w", "ln_b": "l1_ln_b", "final": "final_norm", "a0": "l1_a0"}
ROW_LOADS = len(PARAM) + 2 + 4

TABLE = const_table()
OFFSET, _at = {}, 0
for _n, _a in TABLE.items():
    OFFSET[_n] = (_at, _a.shape[1])
    _at += _a.shape[1]
TABLE_W = _at
ATTN_NAMES = ["rope_cos", "rope_sin"]
CORE_FIRST = OFFSET["cum0"][0]
CORE_W = TABLE_W - CORE_FIRST

ROWS_A = {"ada_b0": 0, "ada_b1": 48, "norm1_0": 96, "norm2_0": 104, "norm1_1": 112, "norm2_1": 120}
ROWS_B = {"mu": 0, "k_k": 48, "k_a": 56, "r_k": 64, "ln_w": 72, "ln_b": 80, "final": 88, "a0": 96}
ROWS_C = {"c": 0, "c_ctx": 8}

U_IN, U_OUT0, U_MLP0 = 0, 6, 10
U_RKV, U_LORA, U_OUT1, U_MLP1 = 42, 54, 56, 60
UNITS = 92

FOUR = (0, 1, 2, 3, 6, 7, 8, 9, 54)
LANDED = [sum(2 if v in FOUR else 1 for v in range(u % 2, u + 1, 2)) for u in range(UNITS)]


def build(nc, a, out):
    stack = ExitStack()
    with stack:
        def sem(name):
            return stack.enter_context(nc.semaphore(name))

        def keep(name, shape, dt=F32):
            return stack.enter_context(nc.sbuf_tensor(name, shape, dt))

        def place(name, kib, shape, dt=F32):
            with ExitStack() as s:
                if kib:
                    s.enter_context(nc.sbuf_tensor(name + "_below", [P, int(kib * 256)], F32))
                return s.enter_context(nc.sbuf_tensor(name, shape, dt))

        X = keep("X", [P, KT, T])
        RAW = keep("RAW", [P, 2, KT, UC])
        WH = keep("WH", [P, 2, KT, UC], F32R)
        WL = keep("WL", [P, 2, KT, UC], F32R)
        CK = keep("CK", [P, 384])
        PAR = keep("PAR", [P, 384])
        MOD = keep("MOD", [P, 2, 48, 2])
        SV = keep("SV", [P, KT, 2])
        EPSC = keep("EPSC", [P, 3])
        AB = keep("AB", [P, KT, 2])
        QKG = keep("QKG", [P, 2])
        ONES = keep("ONES", [P, P])
        A0H = keep("A0H", [P, 16])
        KA1 = keep("KA1", [P, KT])
        IDN, HEAD1, SWAP = CK[:, 0:128], CK[:, 128:256], CK[:, 256:384]
        PS = stack.enter_context(nc.psum_tensor("PS", [P, 4096], F32))

        XT = place("XT", 64, [P, NTT, D])
        ROWS = place("ROWS", 88, [P, 3, P])
        ADA0 = place("ADA0", 0, [P, 4, KT, 512])
        AH = place("AH", 0, [P, KT, T], F32R)
        AL = place("AL", 24, [P, KT, T], F32R)
        QKV = place("QKV", 48, [P, 12, T])
        SQ = place("SQ", 96, [P, 2, T])
        TN = place("TN", 102, [P, 2, T])
        RS = place("RS", 108, [P, T])
        ADW = place("ADW", 119, [P, KT, UC])
        HQ = place("HQ", 0, [P, 2, T])
        HR = place("HR", 6, [P, 2, T])
        HN = place("HN", 12, [P, 2, T])
        HC = place("HC", 18, [P, 2, TX])
        ROPE = place("ROPE", 84, [P, 2, TX])
        OT = place("OT", 0, [P, KT, T])
        KH2 = place("KH2", 24, [P, 2, T], F32R)
        KL2 = place("KL2", 30, [P, 2, T], F32R)
        VS = place("VS", 36, [P, 4, NTT, P], F32R)
        QS = place("QS", 84, [P, 2, T], F32R)
        PB = place("PB", 90, [P, 2, T])
        PTH = place("PTH", 96, [P, NTT, 256], F32R)
        PTL = place("PTL", 102, [P, NTT, 256], F32R)
        OA = place("OA", 108, [P, 256])
        OB = place("OB", 109, [P, 256])
        SMS = place("SMS", 110, [P, 16])
        BH = place("BH", 48, [P, KT, T], F32R)
        BL = place("BL", 72, [P, KT, T], F32R)
        HRL = place("HRL", 96, [P, 2, T])
        HSQ = place("HSQ", 102, [P, 2, T])

        U = place("U", 48, [P, KT, T])
        XX = place("XX", 72, [P, KT, T])
        MX = place("MX", 96, [P, 2, T])
        STG = place("STG", 102, [P, 4, T])
        LW = place("LW", 121.5, [P, T])
        LA = place("LA", 124.5, [P, T])
        LG = place("LG", 127.5, [P, TX])
        SCR = nc.dram_tensor("rwkv_scratch", [3, KT, P, T], F32, kind="Internal").ap()
        CT = place("CT", 0, [P, CORE_W])
        KG = place("KG", 10, [P, T])
        VG = place("VG", 13, [P, T])
        RG = place("RG", 16, [P, TX])
        W2G = place("W2G", 18, [P, P])
        A2G = place("A2G", 18.5, [P, P])
        G2G = place("G2G", 19, [P, P])
        W0G = place("W0G", 19.5, [1, 2, P])
        KK = place("KK", 20.5, [P, T])
        WI = place("WI", 23.5, [P, T])
        LV = place("LV", 23.5, [P, NTT, P])
        SG = place("SG", 26.5, [P, NTT, P])
        BT = place("BT", 26.5, [P, T])
        AA = place("AA", 29.5, [P, T])
        TB = place("TB", 32.5, [P, T])
        KD = place("KD", 35.5, [P, T])
        AR = place("AR", 38.5, [P, NTT, 2, P])
        WP = [place(f"WP{d}", 44.5 + 3.25 * d, [P, NCH, C + 1]) for d in range(2)]
        RKS = place("RKS", 51, [P, TX])
        BKT = place("BKT", 53, [P, NTT, 2, P])
        VT = place("VT", 59, [P, NTT, P])
        LK = place("LK", 62, [P, 12, 2, 2 * P])
        XI = place("XI", 86, [P, 12, P])
        XIT = place("XIT", 92, [P, 12, P])
        UM = place("UM", 98, [P, 2, 4, P])
        OG = place("OG", 102, [P, KT, TX])
        YA = place("YA", 118, [P, TX])
        RH = place("RH", 120, [P, P])
        SA = place("SA", 120.5, [P, P])
        YB = place("YB", 86, [P, TX])
        SS = place("SS", 121, [P, 2, HD])
        SW = place("SW", 98, [P, HD])
        YC = place("YC", 23.5, [P, TX])
        YQ = place("YQ", 26.5, [P, TX])
        YR = place("YR", 29.5, [P, TX])
        YT = place("YT", 32.5, [P, TX])
        OUTT = place("OUTT", 0, [P, 4, D])

        def bank(b):
            return PS[:, b * 512:(b + 1) * 512]

        def pair(b):
            return PS[:, b * 512:b * 512 + 1024]

        def tile_ps(b):
            return PS[:, b * 512 + 256:b * 512 + 1024]

        def col(block, row, n=1):
            return PAR[:, block * 128 + row:block * 128 + row + n]

        ld_const, ld_rows, ld_x, ld_rope = sem("ld_const"), sem("ld_rows"), sem("ld_x"), sem("ld_rope")
        ld_ada0 = [sem(f"ld_ada0_{i}") for i in range(4)]
        raw_landed = [sem("raw_landed0"), sem("raw_landed1")]
        w_high = sem("w_high")
        w_split = sem("w_split")
        w_used = sem("w_used")
        evac_act, evac_dve = sem("evac_act"), sem("evac_dve")
        ada_landed, ada_used, ada_read = sem("ada_landed"), sem("ada_used"), sem("ada_read")
        par_t, par_ready, sv_ready, silu_a = sem("par_t"), sem("par_ready"), sem("sv_ready"), sem("silu_a")
        sv_step = sem("sv_step")
        ones_ready = sem("ones_ready")
        xt_done, xv_act, xv_dve = sem("xt_done"), sem("xv_act"), sem("xv_dve")
        ada0_done, mod_ready = sem("ada0_done"), sem("mod_ready")
        n_sq, n_squsd = sem("norm_squared"), sem("norm_square_used")
        n_ln, n_rs, n_ab, n_t, n_h, n_u = (sem("norm_ln"), sem("norm_rs"), sem("norm_ab"), sem("norm_scaled"),
                                          sem("norm_high"), sem("norm_low"))
        hn_sq, hn_stat, hn_ln, hn_rs, hn_q, hn_sw, hn_c, hn_s, hn_done = [
            sem("hn_" + x) for x in ("sq", "stat", "ln", "rs", "q", "swap", "cos", "sin", "done")]
        v_t, v_high, v_low = sem("v_transposed"), sem("v_high"), sem("v_low")
        k_high, k_low, q_high, q_low = sem("k_high"), sem("k_low"), sem("q_high"), sem("q_low")
        s_done, m_done, nm_done, e_done, r_done = (sem("scores"), sem("row_max"), sem("neg_max"), sem("exps"),
                                                   sem("recip"))
        t_done, pth, ptl, pv_done, oa_done, ob_done, o_done = [
            sem(x) for x in ("p_transposed", "pt_high", "pt_low", "pv", "o_upper", "o_sum", "o_scaled")]
        ot_high, ot_low = sem("ot_high"), sem("ot_low")
        h_relu, h_sq, h_high, h_low = (sem("hid_relu"), sem("hid_sq"), sem("hid_high"), sem("hid_low"))
        out_ready, stored = sem("out_ready"), sem("stored")

        xx_step, xx_ready = sem("xx_step"), sem("xx_ready")
        mx_made, mx_high, mx_low, mx_used = sem("mix_made"), sem("mix_high"), sem("mix_low"), sem("mix_used")
        stg_stored = [sem("stage_stored0"), sem("stage_stored1")]
        lora_done, lora_ready, lg_tanh = sem("lora_done"), sem("lora_ready"), sem("lg_tanh")
        consts1, ar_zero = sem("layer1_constants"), sem("ar_zero")
        g_loaded = sem("group_loaded")
        kk_raw, kk_sq, kk_sum, kk_max, kk_ln, kk_rn, kk_ready = [
            sem("kk_" + x) for x in ("raw", "sq", "sum", "max", "ln", "rn", "ready")]
        vt_done, vt_ready = sem("vt_done"), sem("vt_ready")
        z_done, sg_tanh, sg_ready, cum_done = sem("z_done"), sem("sg_tanh"), sem("sg_ready"), sem("cum_done")
        wp_ready, wi_ready, a_done, a_tanh, a_ready = (sem("wp_ready"), sem("wi_ready"), sem("a_done"), sem("a_tanh"),
                                                       sem("a_ready"))
        ar_ready, bt_raw, bt_ready, kd_rate, kd_dir, rks_ready, kd_ready = [
            sem(x) for x in ("ar_ready", "bt_raw", "bt_ready", "kd_rate", "kd_dir", "rks_ready", "kd_ready")]
        tb_done, tb_ready = sem("tb_done"), sem("tb_ready")
        mat_done, mat_ready, lab_done, xi_raw, xi_init, xit_raw, xit_init = [
            sem(x) for x in ("mat_done", "mat_ready", "lab_done", "xi_raw", "xi_init", "xit_raw", "xit_init")]
        u_done, um_ready, inv_done, xi_ready, xit_ready = [
            sem(x) for x in ("u_done", "um_ready", "inv_done", "xi_ready", "xit_ready")]
        rhs_done, rh_ready, sa_done, sa_ready, st_done, sw_ready, st_ready, y_done, y_state, y_ready, \
            lv_done, lv_ready = [
            sem(x) for x in ("rhs_done", "rh_ready", "sa_done", "sa_ready", "state_done", "state_decayed",
                             "state_ready", "y_done", "y_state", "y_ready", "lv_done", "lv_ready")]
        gn_sum, gn_mean, gn_centred, gn_sq, gn_var, gn_ln, gn_rn, gn_scaled, gn_rk, gn_rksum, gn_rkv, gn_affine, gn_gate, \
            og_ready = [sem(x) for x in ("gn_sum", "gn_mean", "gn_centred", "gn_sq", "gn_var", "gn_ln", "gn_rn", "gn_scaled",
                                         "gn_rk", "gn_rksum", "gn_rkv", "gn_affine", "gn_gate", "og_ready")]
        f_done, f_read = sem("final_transposed"), sem("final_read")

        def w_view(w):
            return w.rearrange("(k p) n -> p k n", p=P)

        def load_unit(e, u, s, parts):
            e.wait_ge(w_split, u + 1)
            for dst, src in parts:
                e.dma_start(dst, src).then_inc(raw_landed[s], 16)

        def plain(w, c, s):
            v = w_view(w)
            return [(RAW[:, s, 4 * h:4 * h + 4, :], v[:, 4 * h:4 * h + 4, bass.ds(c, UC)]) for h in range(2)]

        def act_split(e, u, s, landed):
            e.wait_ge(raw_landed[s], 32 * landed)
            e.wait_ge(w_used, u + 1)
            e.activation(WH[:, s], RAW[:, s], ACT.Copy).then_inc(w_high, 1)

        def pool_split(e, u, s):
            e.wait_ge(w_high, u + 1)
            e.tensor_tensor(WL[:, s], RAW[:, s], WH[:, s], ALU.subtract).then_inc(w_split, 1)

        def pe_unit(e, u, s, rh, rl, streams=(0, 1), ntiles=(0, 1), k_ready=None, k_used=None, done=w_used):
            e.wait_ge(w_split, u + 3)
            e.wait_ge(evac_act, u + 1)
            e.wait_ge(evac_dve, u + 1)
            mm = None
            for k in range(KT):
                if k_ready:
                    k_ready(e, k)
                for n in ntiles:
                    for st in streams:
                        lo, hi = STREAMS[st]
                        dst = tile_ps(4 * s + 2 * n)[:, lo:hi]
                        for i, (w, r) in enumerate(((WH, rh), (WL, rh), (WH, rl))):
                            mm = e.matmul(dst, w[:, s, k, n * P:(n + 1) * P], r[:, k, lo:hi],
                                          start=(k == 0 and i == 0), stop=(k == KT - 1 and i == 2),
                                          skip_group_check=True)
                if k_used is not None and k < KT - 1:
                    mm.then_inc(k_used, 1)
            mm.then_inc(done, 1)

        def pe_ada(e, n_landed, dst_bank, dst_col, unit=None):
            if unit is not None:
                e.wait_ge(evac_act, unit + 1)
                e.wait_ge(evac_dve, unit + 1)
            e.wait_ge(ada_landed, 16 * n_landed)
            e.wait_ge(ada_read, n_landed)
            for n in range(2):
                for k in range(KT):
                    mm = e.matmul(bank(dst_bank)[:, dst_col + 2 * n:dst_col + 2 * n + 2],
                                  ADW[:, k, n * P:(n + 1) * P], SV[:, k, :],
                                  start=(k == 0), stop=(k == KT - 1), skip_group_check=True)
            mm.then_inc(ada_used, 1)

        def dve_ada(e, n, layer, tile, src_bank, src_col):
            e.wait_ge(ada_used, n + 2)
            e.tensor_tensor(MOD[:, layer, bass.ds(tile, 2), :],
                            bank(src_bank)[:, src_col:src_col + 4].rearrange("p (n v) -> p n v", v=2),
                            PAR[:, bass.ds(48 * layer + tile, 2)].unsqueeze(2).to_broadcast([P, 2, 2]),
                            ALU.add).then_inc(ada_read, 1)

        def load_ada(e, n, layer, c):
            e.wait_ge(ada_used, n + 1)
            e.dma_start(ADW[:, :, :], w_view(a[f"l{layer}_ada_w"])[:, :, bass.ds(c, UC)]).then_inc(ada_landed, 16)

        def norm_ab(e, i, layer, half):
            g = col(0, ROWS_A[f"norm{half + 1}_{layer}"], KT)
            sc = MOD[:, layer, 24 * half + 8:24 * half + 16, :]
            e.scalar_tensor_tensor(out=AB[:, :, :], in0=sc, scalar=1.0,
                                   in1=g.unsqueeze(2).to_broadcast([P, KT, 2]), op0=ALU.add,
                                   op1=ALU.mult).then_inc(n_ab, 1)

        def norm_act_stats(e, i, lo):
            for k in range(KT):
                if k >= 2:
                    e.wait_ge(n_squsd, KT * i + k - 1)
                e.activation(SQ[:, k % 2, lo:], X[:, k, lo:], ACT.Square).then_inc(n_sq, 1)
            e.wait_ge(n_squsd, KT * (i + 1))
            e.activation(RS[:, lo:], tile_ps(0)[:, lo:], ACT.Ln, bias=EPSC[:, 0:1], scale=1.0 / D).then_inc(n_ln, 1)
            e.wait_ge(n_ln, i + 1)
            e.activation(RS[:, lo:], RS[:, lo:], ACT.Exp, scale=-0.5).then_inc(n_rs, 1)

        def norm_pe_stats(e, i, lo):
            for k in range(KT):
                e.wait_ge(n_sq, KT * i + k + 1)
                for st_lo, st_hi in STREAMS:
                    if st_lo >= lo:
                        mm = e.matmul(tile_ps(0)[:, st_lo:st_hi], ONES[:, :], SQ[:, k % 2, st_lo:st_hi],
                                      start=(k == 0), stop=(k == KT - 1), skip_group_check=True)
                mm.then_inc(n_squsd, 1)

        def norm_act_high(e, i, layer, half, lo, dst):
            for k in range(KT):
                e.wait_ge(n_t, KT * i + k + 1)
                for st, (a0, a1) in enumerate(STREAMS):
                    if a0 >= lo:
                        ins = e.activation(dst[:, k, a0:a1], TN[:, k % 2, a0:a1], ACT.Identity,
                                           bias=MOD[:, layer, 24 * half + k, 1 - st:2 - st])
                ins.then_inc(n_h, 1)

        def norm_dve(e, i, layer, half, lo, low):
            norm_ab(e, i, layer, half)
            e.wait_ge(n_ab, i + 1)
            e.wait_ge(n_rs, i + 1)
            for k in range(KT + 1):
                if k < KT:
                    if k >= 2:
                        e.wait_ge(n_h, KT * i + k - 1)
                        if low is not None:
                            e.wait_ge(n_u, KT * low + k - 1)
                    for st, (a0, a1) in enumerate(STREAMS):
                        if a0 >= lo:
                            ins = e.scalar_tensor_tensor(out=TN[:, k % 2, a0:a1], in0=X[:, k, a0:a1],
                                                         scalar=AB[:, k, 1 - st:2 - st], in1=RS[:, a0:a1],
                                                         op0=ALU.mult, op1=ALU.mult)
                    ins.then_inc(n_t, 1)
                if k >= 1 and low is not None:
                    e.wait_ge(n_h, KT * i + k)
                    for st, (a0, a1) in enumerate(STREAMS):
                        if a0 >= lo:
                            ins = e.scalar_tensor_tensor(out=AL[:, k - 1, a0:a1], in0=TN[:, (k - 1) % 2, a0:a1],
                                                         scalar=MOD[:, layer, 24 * half + k - 1, 1 - st:2 - st],
                                                         in1=AH[:, k - 1, a0:a1], op0=ALU.add, op1=ALU.subtract)
                    ins.then_inc(n_u, 1)

        def after_norm(n):
            def wait(e, k):
                e.wait_ge(n_u, KT * n + k + 1)
            return wait

        def mlp_up_act(e, u, s, tile, count, lo, landed):
            act_split(e, u + 1, 1 - s, landed)
            e.wait_ge(w_used, u + 3)
            for n in range(2):
                e.activation(HRL[:, n, lo:], tile_ps(4 * s + 2 * n)[:, lo:], ACT.Relu).then_inc(h_relu, 1)
            e.wait_ge(h_relu, count + 2)
            e.sem_inc(evac_act, 1)
            for n in range(2):
                e.wait_ge(h_sq, count + n + 1)
                e.activation(BH[:, bass.ds(tile + n, 1), lo:].rearrange("p a t -> p (a t)"), HSQ[:, n, lo:],
                             ACT.Copy).then_inc(h_high, 1)

        def mlp_up_dve(e, u, tile, count, lo, ada=None):
            for n in range(2):
                e.wait_ge(h_relu, count + n + 1)
                e.wait_ge(h_low, count + n + 1)
                e.tensor_tensor(HSQ[:, n, lo:], HRL[:, n, lo:], HRL[:, n, lo:], ALU.mult).then_inc(h_sq, 1)
            if ada is not None:
                dve_ada(e, *ada)
                e.wait_ge(ada_read, ada[0] + 2)
            e.wait_ge(evac_dve, u + 2)
            e.sem_inc(evac_dve, 1)
            for n in range(2):
                e.wait_ge(h_high, count + n + 1)
                row = bass.ds(tile + n, 1)
                e.tensor_tensor(BL[:, row, lo:].rearrange("p a t -> p (a t)"), HSQ[:, n, lo:],
                                BH[:, row, lo:].rearrange("p a t -> p (a t)"), ALU.subtract).then_inc(h_low, 1)

        def add_act(e, u, s, landed):
            if landed is not None:
                act_split(e, u + 1, 1 - s, landed)
            e.sem_inc(evac_act, 1)

        def add_dve(e, u, s, tile, layer, chunk, lo, ada=None):
            e.wait_ge(w_used, u + 3)
            if ada is not None:
                dve_ada(e, *ada)
            for n in range(2):
                for st, (a0, a1) in enumerate(STREAMS):
                    if a0 >= lo:
                        x = X[:, bass.ds(tile + n, 1), a0:a1].rearrange("p a t -> p (a t)")
                        gate = MOD[:, layer, bass.ds(8 * chunk + tile + n, 1), 1 - st:2 - st].rearrange("p a t -> p (a t)")
                        ins = e.scalar_tensor_tensor(out=x, in0=tile_ps(4 * s + 2 * n)[:, a0:a1], scalar=gate, in1=x,
                                                     op0=ALU.mult, op1=ALU.add)
            ins.then_inc(evac_dve, 1)

        def job(n):
            j, r = divmod(n, 6)
            return j, r, (TC if r < 2 else T)

        def attn_pe(e, g, p):
            for n in range(13):
                if n < 12:
                    j, r, nk = job(n)
                    if n == 0:
                        e.wait_ge(q_low, 2 * g + 2)
                    e.wait_ge(e_done, 12 * g + n + 1)
                    for a0, a1 in ((0, min(nk, 512)), (512, nk)):
                        if a1 > a0:
                            for i, kk in enumerate((KH2, KL2)):
                                mm = e.matmul(pair(2 * (n % 2))[:, a0:a1], QS[:, j, r * P:(r + 1) * P], kk[:, j, a0:a1],
                                              start=(i == 0), stop=(i == 1), skip_group_check=True)
                    mm.then_inc(s_done, 1)
                if n:
                    m = n - 1
                    j, r, nk = job(m)
                    e.wait_ge(e_done, 12 * g + m + 3)
                    e.wait_ge(ptl, 12 * g + m + 1)
                    for l in range(nk // P):
                        mm = e.transpose(pair(4)[:, l * P:(l + 1) * P], PB[:, m % 2, l * P:(l + 1) * P], IDN)
                    mm.then_inc(t_done, 1)
                    if m % 2:
                        q = m // 2
                        e.wait_ge(o_done, 6 * g + q + 1)
                        e.wait_ge(r_done, 12 * g + m + 1)
                        for b in range(2):
                            rs = 12 + (m - 1 + b) % 4
                            e.matmul(bank(6)[:, 256 + b * P:256 + (b + 1) * P], SMS[:, rs:rs + 1].to_broadcast([P, P]), IDN,
                                     start=True, stop=True, skip_group_check=True)
                        e.wait_ge(ptl, 12 * g + m + 2)
                        for i, pt in enumerate((PTH, PTL)):
                            for l in range(nk // P):
                                mm = e.matmul(bank(6)[:, 0:256], VS[:, 2 * p + j, l, :], pt[:, l, :], start=(i == 0 and l == 0),
                                              stop=(i == 1 and l == nk // P - 1), skip_group_check=True)
                        mm.then_inc(pv_done, 1)
                if n == 6:
                    pe_ada(e, 2 * g + 1, 7, 0)
            pe_ada(e, 2 * g + 2, 7, 0)

        def attn_act(e, g):
            e.wait_ge(s_done, 12 * g + 1)
            for j in range(2):
                e.activation(QS[64 * j:64 * j + 64, j, :], QKV[64 * j:64 * j + 64, bass.ds(g, 1), :].rearrange("p a t -> p (a t)"),
                             ACT.Copy).then_inc(q_high, 1)

            def output(q):
                j = q // 3
                e.wait_ge(pv_done, 6 * g + q + 1)
                e.wait_ge(ob_done, 6 * g + q + 1)
                e.activation(OA[64 * j:64 * j + 64, :], bank(6)[64 - 64 * j:128 - 64 * j, 0:256], ACT.Copy).then_inc(oa_done, 1)

            for n in range(13):
                if n < 12:
                    j, r, nk = job(n)
                    e.wait_ge(nm_done, 12 * g + n + 1)
                    e.wait_ge(t_done, 12 * g + n + 1)
                    e.activation(PB[:, n % 2, 0:nk], pair(2 * (n % 2))[:, 0:nk], ACT.Exp, bias=SMS[:, 4 + n % 4:5 + n % 4],
                                 scale=SCALE, accum_out=SMS[:, 8 + n % 4:9 + n % 4]).then_inc(e_done, 1)
                if n:
                    m = n - 1
                    j, r, nk = job(m)
                    e.wait_ge(t_done, 12 * g + m + 3)
                    e.activation(PTH[:, 0:nk // P, (m % 2) * P:(m % 2 + 1) * P],
                                 pair(4)[:, 0:nk].rearrange("p (l q) -> p l q", q=P), ACT.Copy).then_inc(pth, 1)
                    if m >= 2 and m % 2 == 0:
                        output(m // 2 - 1)
            output(5)

        def attn_dve(e, g):
            e.wait_ge(q_high, 2 * g + 2)
            for j in range(2):
                e.tensor_tensor(QS[64 - 64 * j:128 - 64 * j, j, :], QKV[64 * j:64 * j + 64, bass.ds(g, 1), :].rearrange("p a t -> p (a t)"),
                                QS[64 * j:64 * j + 64, j, :], ALU.subtract).then_inc(q_low, 1)

            def output(q):
                j, b = divmod(q, 3)
                h = slice(64 * j, 64 * j + 64)
                e.wait_ge(oa_done, 6 * g + q + 1)
                e.tensor_tensor(OB[h, :], bank(6)[h, 0:256], OA[h, :], ALU.add).then_inc(ob_done, 1)
                e.wait_ge(ob_done, 6 * g + q + 2)
                e.tensor_tensor(OT[h, bass.ds(g, 1), b * 256:(b + 1) * 256].rearrange("p a t -> p (a t)"),
                                bank(6)[h, 256:512], OB[h, :], ALU.mult).then_inc(o_done, 1)

            for n in range(13):
                if n < 12:
                    j, r, nk = job(n)
                    e.wait_ge(s_done, 12 * g + n + 2)
                    e.tensor_reduce(SMS[:, n % 4:n % 4 + 1], pair(2 * (n % 2))[:, 0:nk], AX.X, ALU.max).then_inc(m_done, 1)
                    e.wait_ge(m_done, 12 * g + n + 1)
                    e.tensor_scalar(SMS[:, 4 + n % 4:5 + n % 4], SMS[:, n % 4:n % 4 + 1], -SCALE, None, ALU.mult)\
                     .then_inc(nm_done, 1)
                if n:
                    m = n - 1
                    j, r, nk = job(m)
                    e.wait_ge(e_done, 12 * g + m + 3)
                    e.reciprocal(SMS[:, 12 + m % 4:13 + m % 4], SMS[:, 8 + m % 4:9 + m % 4]).then_inc(r_done, 1)
                    e.wait_ge(pth, 12 * g + m + 1)
                    cols = slice((m % 2) * P, (m % 2 + 1) * P)
                    e.tensor_tensor(PTL[:, 0:nk // P, cols], pair(4)[:, 0:nk].rearrange("p (l q) -> p l q", q=P),
                                    PTH[:, 0:nk // P, cols], ALU.subtract).then_inc(ptl, 1)
                    if m >= 2 and m % 2 == 0:
                        output(m // 2 - 1)
                if n == 7:
                    dve_ada(e, 2 * g, 0, 16 + 4 * g, 7, 0)
            output(5)
            dve_ada(e, 2 * g + 1, 0, 18 + 4 * g, 7, 0)

        MIXES = ((2, 0), (3, 0), (0, TC), (1, 0), (4, 0), (5, TC))

        def mix_used(e, n, k):
            if n < 0:
                return
            if k < KT - 1:
                e.wait_ge(mx_used, 7 * (min(4 * n + 3, 11) + max(0, n - 2)) + k + 1)
            elif n == 3:
                e.wait_ge(lora_done, 1)
            else:
                e.wait_ge(w_used, (U_RKV + 4 * n + 3 if n < 3 else U_LORA) + 3)

        def mix_ready(n):
            def wait(e, k):
                e.wait_ge(mx_low, KT * n + k + 1)
            return wait

        def mix_act(e, n):
            lo = MIXES[n][1]
            for k in range(KT):
                e.wait_ge(mx_made, KT * n + k + 1)
                mix_used(e, n - 1, k)
                e.activation(AH[:, k, lo:], MX[:, k % 2, lo:], ACT.Copy).then_inc(mx_high, 1)

        def mix_dve(e, n):
            row, lo = MIXES[n]
            for k in range(KT + 1):
                if k < KT:
                    if n + k >= 2 or n:
                        e.wait_ge(mx_high, KT * n + k - 1)
                        e.wait_ge(mx_low, KT * n + k - 1)
                    if n == 0:
                        e.wait_ge(xx_ready, k + 1)
                    e.scalar_tensor_tensor(out=MX[:, k % 2, lo:], in0=XX[:, k, lo:], scalar=col(1, 8 * row + k),
                                           in1=U[:, k, lo:], op0=ALU.mult, op1=ALU.add).then_inc(mx_made, 1)
                if k:
                    e.wait_ge(mx_high, KT * n + k)
                    mix_used(e, n - 1, k - 1)
                    e.tensor_tensor(AL[:, k - 1, lo:], MX[:, (k - 1) % 2, lo:], AH[:, k - 1, lo:],
                                    ALU.subtract).then_inc(mx_low, 1)

        def stage(e, j, n, evac):
            s = j % 2
            e.wait_ge(w_used, U_RKV + j + 3)
            if j >= 2:
                e.wait_ge(stg_stored[s], 32 * (j // 2))
            dst, src = STG[:, 2 * s + n, :], tile_ps(4 * s + 2 * n)
            if n == 0:
                e.activation(dst, src, ACT.Copy).then_inc(evac, 1)
            else:
                e.tensor_copy(dst, src).then_inc(evac, 1)

        ORDER = (tuple(range(NCH)), tuple(range(TC // C))[::-1] + tuple(range(TC // C, NCH))[::-1])
        NX = TX // C

        def table(name):
            first, width = OFFSET[name]
            return CT[:, first - CORE_FIRST:first - CORE_FIRST + width]

        def wp_inclusive(d):
            return WP[d][:, :, 1 - d:1 - d + C]

        def wp_exclusive(d):
            return WP[d][:, :, d:d + C]

        def chunks(ap):
            return ap.rearrange("p (c t) -> p c t", t=C)

        def pe_group(e, g):
            e.wait_ge(kk_sq, g + 1)
            for a0, a1 in STREAMS:
                mm = e.matmul(tile_ps(0)[:, a0:a1], HEAD1, TB[:, a0:a1], start=True, stop=True, skip_group_check=True)
            mm.then_inc(kk_sum, 1)
            for m in range(NTT):
                mm = e.transpose(pair(2)[:, m * P:(m + 1) * P], VG[:, m * P:(m + 1) * P], IDN)
            mm.then_inc(vt_done, 1)

        def act_group(e, g):
            e.wait_ge(kk_raw, g + 1)
            e.activation(TB[:, :], KK[:, :], ACT.Square).then_inc(kk_sq, 1)
            e.wait_ge(kk_max, g + 1)
            e.activation(TB[:, :], TB[:, :], ACT.Ln, scale=65536.0).then_inc(kk_ln, 1)
            e.wait_ge(kk_ln, g + 1)
            e.activation(TB[:, :], TB[:, :], ACT.Exp, scale=-0.5, bias=EPSC[:, 2:3]).then_inc(kk_rn, 1)
            e.wait_ge(vt_done, g + 1)
            e.activation(VT[:, :, :].rearrange("p m c -> p (m c)"), pair(2)[:, 0:T], ACT.Copy).then_inc(vt_ready, 1)

        def dve_group(e, g):
            e.wait_ge(g_loaded, GROUP_LOADS * 16 * (g + 1) + 16)
            e.tensor_scalar(KK[:, :], KG[:, :], PAR[:, bass.ds(P + ROWS_B["k_k"] + g, 1)], None, ALU.mult).then_inc(kk_raw, 1)
            e.wait_ge(kk_sum, g + 1)
            e.tensor_scalar(TB[:, :], tile_ps(0), 1e-24, None, ALU.max).then_inc(kk_max, 1)
            e.wait_ge(kk_rn, g + 1)
            e.tensor_tensor(KK[:, :], KK[:, :], TB[:, :], ALU.mult).then_inc(kk_ready, 1)

        def pe_build(e, g, d):
            q = 2 * g + d
            r = slice(64 * d, 64 * d + 64)
            e.wait_ge(vt_ready, g + 1)
            e.wait_ge(kk_max, g + 1)
            for m in range(NTT):
                e.matmul(pair(0)[:, m * P:(m + 1) * P], LW[r, m * P:(m + 1) * P], W2G[r, :], start=True, stop=False,
                         skip_group_check=True)
                mm = e.matmul(pair(0)[:, m * P:(m + 1) * P], ONES[0:1, :], W0G[0:1, d, :], start=False, stop=True,
                              skip_group_check=True)
            mm.then_inc(z_done, 1)
            e.wait_ge(y_ready, q + 1)
            for a0, a1 in STREAMS:
                mm = e.matmul(tile_ps(4)[:, a0:a1], A2G[r, :], LA[r, a0:a1], start=True, stop=True, skip_group_check=True)
            mm.then_inc(a_done, 1)
            e.wait_ge(sg_ready, q + 1)
            for m in range(NTT):
                mm = e.matmul(pair(2)[:, m * P:(m + 1) * P], SG[:, m, :], table(f"cum{d}"), start=True, stop=True,
                              skip_group_check=True)
            mm.then_inc(cum_done, 1)
            e.wait_ge(bt_ready, q + 1)
            e.wait_ge(kd_ready, q + 1)
            for m in range(NTT):
                for i, src in enumerate((BT, KD)):
                    mm = e.transpose(PS[:, (2 * m + i) * P:(2 * m + i + 1) * P], src[:, m * P:(m + 1) * P], IDN)
            mm.then_inc(tb_done, 1)
            e.wait_ge(ar_ready, 2 * q + 2)
            for u in range(12):
                m, h = divmod(u, 2)
                c = slice(64 * h, 64 * h + 64)
                if u >= 2:
                    e.wait_ge(mat_ready, 12 * q + u - 1)
                for i, src in enumerate((BT, KD)):
                    mm = e.matmul(bank(3 + u % 2)[:, 256 * i:256 * i + 256], src[c, m * P:(m + 1) * P],
                                  AR[c, m, :, :].rearrange("p a t -> p (a t)"), start=True, stop=True, skip_group_check=True)
                mm.then_inc(mat_done, 1)
                if u in (4, 8):
                    e.wait_ge(xi_raw, 3 * q + u // 4)
                mm = e.matmul(bank(5 + h)[:, (m % 2) * P:(m % 2 + 1) * P], AR[c, m, 0, :],
                              BT[c, m * P:(m + 1) * P], start=True, stop=True, skip_group_check=True)
                if u % 4 == 3:
                    mm.then_inc(lab_done, 1)
            e.wait_ge(tb_ready, q + 1)
            e.wait_ge(mat_ready, 12 * q + 12)
            e.wait_ge(xi_raw, 3 * q + 3)
            for u in range(12):
                m, h = divmod(u, 2)
                mm = e.matmul(pair(6)[:, u * HD:(u + 1) * HD], LK[:, u, 1, 0:P], VT[:, m, 64 * h:64 * h + 64], start=True,
                              stop=True, skip_group_check=True)
            mm.then_inc(lv_done, 1)
            for n in range(16):
                if n < 15:
                    if n < 3:
                        e.wait_ge(xi_init, 3 * q + n + 1)
                    else:
                        e.wait_ge(xi_ready, 12 * q + n - 2)
                    if n >= 2:
                        e.wait_ge(um_ready, 15 * q + n - 1)
                    for i in range(4):
                        u = 4 * (n % 3) + i
                        mm = e.matmul(bank(n % 2)[:, i * P:(i + 1) * P], LK[:, u, 0, 0:P], XI[:, u, :], start=True,
                                      stop=True, skip_group_check=True)
                    mm.then_inc(u_done, 1)
                if n:
                    v = n - 1
                    e.wait_ge(um_ready, 15 * q + v + 1)
                    if v < 3:
                        e.wait_ge(xit_init, 3 * q + v + 1)
                    if v >= 2:
                        e.wait_ge(xit_ready, 15 * q + v - 1)
                        if v < 12:
                            e.wait_ge(xi_ready, 12 * q + v - 1)
                    for i in range(4):
                        u = 4 * (v % 3) + i
                        cols = slice(i * P, (i + 1) * P)
                        if v < 12:
                            e.matmul(bank(2 + v % 2)[:, cols], XIT[:, u, :], UM[:, v % 2, i, :], start=True, stop=True,
                                     skip_group_check=True)
                        mm = e.matmul(bank(4 + v % 2)[:, cols], UM[:, v % 2, i, :], XIT[:, u, :], start=True, stop=True,
                                      skip_group_check=True)
                    mm.then_inc(inv_done, 1)

        def act_build(e, g, d):
            q = 2 * g + d
            e.wait_ge(z_done, q + 1)
            e.activation(SG[:, :, :].rearrange("p m c -> p (m c)"), pair(0)[:, 0:T], ACT.Tanh, scale=0.5).then_inc(sg_tanh, 1)
            e.wait_ge(a_done, q + 1)
            e.activation(AA[:, :], tile_ps(4), ACT.Tanh, bias=A0H[:, bass.ds(8 * d + g, 1)], scale=0.5).then_inc(a_tanh, 1)
            e.wait_ge(cum_done, q + 1)
            e.activation(wp_inclusive(d), chunks(pair(2)[:, 0:T]), ACT.Exp, scale=-DEC).then_inc(wp_ready, 1)
            e.activation(WI[:, :], pair(2)[:, 0:T], ACT.Exp, scale=DEC).then_inc(wi_ready, 1)
            if d == 0:
                e.wait_ge(kd_dir, q + 1)
                e.activation(RKS[:, :], TB[:, TC:], ACT.Copy).then_inc(rks_ready, 1)
            e.wait_ge(tb_done, q + 1)
            e.activation(BKT[:, :, :, :].rearrange("p m a c -> p (m a c)"), PS[:, 0:2 * T], ACT.Copy).then_inc(tb_ready, 1)
            e.wait_ge(lv_done, q + 1)
            e.activation(LV[:, :, :].rearrange("p m c -> p (m c)"), pair(6)[:, 0:T], ACT.Copy).then_inc(lv_ready, 1)

        def pool_build(e, g, d):
            q = 2 * g + d
            if d:
                e.wait_ge(kd_dir, q + 1)
                e.wait_ge(rks_ready, q)
                e.tensor_tensor(RKS[:, :], RKS[:, :], TB[:, TC:], ALU.add).then_inc(rks_ready, 1)
            for b in range(3):
                e.wait_ge(mat_ready, 12 * q + 4 * b + 4)
                e.tensor_tensor(XIT[:, 4 * b:4 * b + 4, :], LK[:, 4 * b:4 * b + 4, 0, 0:P],
                                table(f"level0T{d}").unsqueeze(1).to_broadcast([P, 4, P]), ALU.mult).then_inc(xit_raw, 1)
                e.wait_ge(xit_raw, 3 * q + b + 1)
                e.tensor_tensor(XIT[:, 4 * b:4 * b + 4, :], XIT[:, 4 * b:4 * b + 4, :],
                                IDN.unsqueeze(1).to_broadcast([P, 4, P]), ALU.add).then_inc(xit_init, 1)

        def dve_build(e, g, d):
            q = 2 * g + d
            e.wait_ge(sg_tanh, q + 1)
            e.tensor_scalar(SG[:, :, :], SG[:, :, :], 0.5, 0.5, ALU.mult, ALU.add).then_inc(sg_ready, 1)
            e.wait_ge(a_tanh, q + 1)
            e.tensor_scalar(AA[:, :], AA[:, :], 0.5, 0.5, ALU.mult, ALU.add).then_inc(a_ready, 1)
            if d == 0:
                e.wait_ge(kk_ready, g + 1)
            else:
                e.wait_ge(rks_ready, q)
            e.wait_ge(a_ready, q + 1)
            e.tensor_scalar(TB[:, :], AA[:, :], PAR[:, bass.ds(P + ROWS_B["k_a"] + g, 1)], KA1[:, bass.ds(g, 1)], ALU.mult,
                            ALU.add).then_inc(kd_rate, 1)
            e.wait_ge(kd_rate, q + 1)
            e.tensor_tensor(TB[:, :], TB[:, :], KG[:, :], ALU.mult).then_inc(kd_dir, 1)
            e.wait_ge(cum_done, q + 1)
            e.tensor_tensor(BT[:, :], KK[:, :], AA[:, :], ALU.mult).then_inc(bt_raw, 1)
            e.wait_ge(wi_ready, q + 1)
            e.wait_ge(bt_raw, q + 1)
            e.tensor_tensor(BT[:, :], BT[:, :], WI[:, :], ALU.mult).then_inc(bt_ready, 1)
            e.wait_ge(kd_dir, q + 1)
            e.tensor_tensor(KD[:, :], TB[:, :], WI[:, :], ALU.mult).then_inc(kd_ready, 1)
            e.wait_ge(wp_ready, q + 1)
            e.scalar_tensor_tensor(out=AR[:, :, 0, :].rearrange("p m (c t) -> p m c t", t=C),
                                   in0=KK[:, :].rearrange("p (m c t) -> p m c t", c=2, t=C), scalar=-1.0,
                                   in1=wp_exclusive(d).rearrange("p (m c) t -> p m c t", c=2), op0=ALU.mult,
                                   op1=ALU.mult).then_inc(ar_ready, 1)
            e.tensor_tensor(AR[:, 2:, 1, :].rearrange("p m (c t) -> p m c t", t=C),
                            RG[:, :].rearrange("p (m c t) -> p m c t", c=2, t=C),
                            wp_inclusive(d)[:, TC // C:, :].rearrange("p (m c) t -> p m c t", c=2),
                            ALU.mult).then_inc(ar_ready, 1)
            for u in range(12):
                e.wait_ge(mat_done, 12 * q + u + 1)
                e.tensor_tensor(LK[:, u, :, :], bank(3 + u % 2).rearrange("p (i t) -> p i t", i=2),
                                table(f"masks{d}").unsqueeze(1).to_broadcast([P, 2, 2 * P]), ALU.mult).then_inc(mat_ready, 1)
                if u % 4 == 3:
                    b = u // 4
                    four = slice(4 * b, 4 * b + 4)
                    e.wait_ge(lab_done, 3 * q + b + 1)
                    e.tensor_tensor(XI[:, four, :].rearrange("p (m h) t -> p m h t", h=2),
                                    pair(5).rearrange("p (h m t) -> p m h t", h=2, t=P)[:, 0:2],
                                    table(f"level{d}0").unsqueeze(1).unsqueeze(1).to_broadcast([P, 2, 2, P]),
                                    ALU.mult).then_inc(xi_raw, 1)
                    e.wait_ge(xi_raw, 3 * q + b + 1)
                    e.tensor_tensor(XI[:, four, :], XI[:, four, :], IDN.unsqueeze(1).to_broadcast([P, 4, P]),
                                    ALU.add).then_inc(xi_init, 1)
            for n in range(16):
                if n < 15:
                    e.wait_ge(u_done, 15 * q + n + 1)
                    e.tensor_tensor(UM[:, n % 2, :, :], bank(n % 2).rearrange("p (i t) -> p i t", i=4),
                                    table(f"level{d}{1 + n // 3}").unsqueeze(1).to_broadcast([P, 4, P]),
                                    ALU.mult).then_inc(um_ready, 1)
                if n:
                    v = n - 1
                    four = slice(4 * (v % 3), 4 * (v % 3) + 4)
                    e.wait_ge(inv_done, 15 * q + v + 1)
                    if v < 3:
                        e.wait_ge(xit_init, 3 * q + v + 1)
                    else:
                        e.wait_ge(xit_ready, 15 * q + v - 2)
                    if v < 12:
                        e.wait_ge(*((xi_init, 3 * q + v + 1) if v < 3 else (xi_ready, 12 * q + v - 2)))
                        e.tensor_tensor(XI[:, four, :], XI[:, four, :], bank(2 + v % 2).rearrange("p (i t) -> p i t", i=4),
                                        ALU.add).then_inc(xi_ready, 1)
                    e.tensor_tensor(XIT[:, four, :], XIT[:, four, :], bank(4 + v % 2).rearrange("p (i t) -> p i t", i=4),
                                    ALU.add).then_inc(xit_ready, 1)

        def pe_chain(e, g, d):
            q = 2 * g + d
            heads = (slice(0, 64), slice(64, 128))
            e.wait_ge(xit_ready, 15 * q + 15)
            for m in range(TC // P, NTT):
                for h, k in enumerate(heads):
                    e.matmul(bank(4)[k, m * P - TC:(m + 1) * P - TC], VT[:, m, k], LK[:, 2 * m + h, 1, P:],
                             start=(m == TC // P), stop=False, skip_group_check=True)
            e.wait_ge(lv_ready, q + 1)
            e.nop(nofuse=True)
            for j, c in enumerate(ORDER[d]):
                m, cp = divmod(c, 2)
                t = slice(64 * cp, 64 * cp + 64)
                if j:
                    e.wait_ge(st_ready, 11 * q + j)
                    e.nop(nofuse=True)
                    for h, k in enumerate(heads):
                        mm = e.matmul(bank(6 + h)[t, 0:HD], AR[k, m, 0, t], SS[k, j % 2, :], start=True, stop=True,
                                      skip_group_check=True)
                    mm.then_inc(rhs_done, 1)
                if j < NCH - 1:
                    for h, k in enumerate(heads):
                        e.matmul(bank(2 + j % 2)[k, 0:HD], BKT[t, m, 1, k], VT[t, m, k], start=True, stop=False,
                                 skip_group_check=True)
                if j >= NCH - NX:
                    for h, k in enumerate(heads):
                        mm = e.matmul(bank(5)[k, c * C - TC:(c + 1) * C - TC], SS[k, j % 2, :], AR[k, m, 1, t], start=True,
                                      stop=True, skip_group_check=True)
                if j:
                    e.wait_ge(rh_ready, 11 * q + j)
                    e.nop(nofuse=True)
                for h, k in enumerate(heads):
                    mm = e.matmul(bank(6)[t, P + 64 * h:P + 64 * h + 64], XIT[t, 2 * m + h, t],
                                  RH[t, k] if j else LV[t, m, k], start=True, stop=True, skip_group_check=True)
                mm.then_inc(sa_done, 1)
                e.wait_ge(sa_ready, 12 * q + j + 1)
                e.nop(nofuse=True)
                if j < NCH - 1:
                    for h, k in enumerate(heads):
                        mm = e.matmul(bank(2 + j % 2)[k, 0:HD], BKT[t, m, 0, k], SA[t, k], start=False, stop=True,
                                      skip_group_check=True)
                    mm.then_inc(st_done, 1)
                if j >= NCH - NX:
                    for h, k in enumerate(heads):
                        mm = e.matmul(bank(4)[k, c * C - TC:(c + 1) * C - TC], SA[t, k],
                                      LK[t, 2 * m + h, 0, P + 64 * cp:P + 64 * cp + 64], start=False, stop=True,
                                      skip_group_check=True)
            mm.then_inc(y_done, 1)

        def act_chain(e, g, d):
            q = 2 * g + d
            e.wait_ge(y_done, q + 1)
            e.activation((YA, YB)[d][:, :], bank(5), ACT.Copy).then_inc(y_state, 1)

        def dve_chain(e, g, d):
            q = 2 * g + d
            for j, c in enumerate(ORDER[d]):
                m, cp = divmod(c, 2)
                t = slice(64 * cp, 64 * cp + 64)
                total = WP[d][:, c, (C, 0)[d]:(C, 0)[d] + 1]
                if j:
                    e.wait_ge(rhs_done, 11 * q + j)
                    e.tensor_tensor(RH[t, :].rearrange("p (h v) -> p h v", h=2),
                                    pair(6).rearrange("p (h v) -> p h v", h=2)[t, :, 0:HD],
                                    LV[t, m, :].rearrange("p (h v) -> p h v", h=2), ALU.add).then_inc(rh_ready, 1)
                if 0 < j < NCH - 1:
                    e.wait_ge(st_ready, 11 * q + j)
                    e.tensor_scalar(SW[:, :], SS[:, j % 2, :], total, None, ALU.mult).then_inc(sw_ready, 1)
                e.wait_ge(sa_done, 12 * q + j + 1)
                e.tensor_copy(SA[t, :], bank(6)[t, P:2 * P]).then_inc(sa_ready, 1)
                if j < NCH - 1:
                    e.wait_ge(st_done, 11 * q + j + 1)
                    if j:
                        e.wait_ge(sw_ready, 10 * q + j)
                        e.scalar_tensor_tensor(out=SS[:, (j + 1) % 2, :], in0=bank(2 + j % 2)[:, 0:HD], scalar=total,
                                               in1=SW[:, :], op0=ALU.mult, op1=ALU.add).then_inc(st_ready, 1)
                    else:
                        e.tensor_scalar(SS[:, 1, :], bank(2)[:, 0:HD], total, None, ALU.mult).then_inc(st_ready, 1)
            y = (YA, YB)[d]
            e.wait_ge(y_state, q + 1)
            e.tensor_tensor(y[:, :], y[:, :], bank(4), ALU.add).then_inc(y_ready, 1)

        def pe_finish(e, g):
            e.wait_ge(gn_sum, g + 1)
            e.matmul(bank(0), HEAD1, YC[:, :], start=True, stop=True).then_inc(gn_mean, 1)
            e.wait_ge(gn_rk, g + 1)
            e.matmul(bank(1), HEAD1, YT[:, :], start=True, stop=True).then_inc(gn_rksum, 1)
            e.matmul(bank(3), G2G[:, :], LG[:, :], start=True, stop=True).then_inc(gn_gate, 1)
            e.wait_ge(gn_sq, g + 1)
            e.matmul(bank(2), HEAD1, YQ[:, :], start=True, stop=True).then_inc(gn_var, 1)

        def act_finish(e, g):
            e.wait_ge(gn_centred, g + 1)
            e.activation(YQ[:, :], YC[:, :], ACT.Square).then_inc(gn_sq, 1)
            e.wait_ge(gn_var, g + 1)
            e.activation(YR[:, :], bank(2), ACT.Ln, bias=EPSC[:, 1:2], scale=1.0 / HD).then_inc(gn_ln, 1)
            e.wait_ge(gn_ln, g + 1)
            e.activation(YR[:, :], YR[:, :], ACT.Exp, scale=-0.5).then_inc(gn_rn, 1)

        def dve_finish(e, g):
            def par(name):
                return PAR[:, bass.ds(P + ROWS_B[name] + g, 1)]

            e.wait_ge(y_ready, 2 * g + 3)
            e.tensor_tensor(YC[:, :], YA[:, :], YB[:, :], ALU.add).then_inc(gn_sum, 1)
            e.wait_ge(rks_ready, 2 * g + 2)
            e.scalar_tensor_tensor(out=YT[:, :], in0=RKS[:, :], scalar=par("r_k"), in1=RG[:, :], op0=ALU.mult,
                                   op1=ALU.mult).then_inc(gn_rk, 1)
            e.wait_ge(gn_mean, g + 1)
            e.wait_ge(gn_sum, g + 1)
            e.scalar_tensor_tensor(out=YC[:, :], in0=bank(0), scalar=-1.0 / HD, in1=YC[:, :], op0=ALU.mult,
                                   op1=ALU.add).then_inc(gn_centred, 1)
            e.wait_ge(gn_rksum, g + 1)
            e.tensor_tensor(YT[:, :], bank(1), VG[:, TC:], ALU.mult).then_inc(gn_rkv, 1)
            e.wait_ge(gn_rn, g + 1)
            e.wait_ge(gn_centred, g + 1)
            e.scalar_tensor_tensor(out=YC[:, :], in0=YC[:, :], scalar=par("ln_w"), in1=YR[:, :], op0=ALU.mult,
                                   op1=ALU.mult).then_inc(gn_scaled, 1)
            e.wait_ge(gn_scaled, g + 1)
            e.wait_ge(gn_rkv, g + 1)
            e.scalar_tensor_tensor(out=YC[:, :], in0=YC[:, :], scalar=par("ln_b"), in1=YT[:, :], op0=ALU.add,
                                   op1=ALU.add).then_inc(gn_affine, 1)
            e.wait_ge(gn_affine, g + 1)
            e.wait_ge(gn_gate, g + 1)
            e.tensor_tensor(OG[:, bass.ds(g, 1), :].rearrange("p a t -> p (a t)"), bank(3), YC[:, :], ALU.mult)\
             .then_inc(og_ready, 1)

        block = stack.enter_context(nc.Block())

        @block.sync
        def _(sp):
            sp.dma_start(CK[:, :], a["table"][:, 0:384]).then_inc(ld_const, 16)
            for n, r in list(ROWS_A.items()):
                v = a[PARAM[n]].rearrange("(r c) -> r c", c=P)
                sp.dma_start(ROWS[r:r + v.shape[0], 0, :], v).then_inc(ld_rows, 16)
            for n, r in list(ROWS_C.items()):
                v = a[n].rearrange("b (r c) -> (b r) c", c=P) if n == "c" else a[n].rearrange("(r c) -> r c", c=P)
                sp.dma_start(ROWS[r:r + 8, 2, :], v).then_inc(ld_rows, 16)
            for n, r in list(ROWS_B.items()):
                v = a[PARAM[n]]
                form = {"mu": "i (r c) -> (i r) c", "a0": "i (r c) -> (i r) c", "r_k": "(r h) c -> r (h c)"}
                v = v.rearrange(form.get(n, "(r c) -> r c"), **({"h": 2} if n == "r_k" else {"c": P}))
                sp.dma_start(ROWS[r:r + v.shape[0], 1, :], v).then_inc(ld_rows, 16)
            for h in range(2):
                sp.dma_start(QKG[64 * h:64 * h + 64, 0:1], a["l0_q_gain"].unsqueeze(1)).then_inc(ld_rows, 16)
                sp.dma_start(QKG[64 * h:64 * h + 64, 1:2], a["l0_k_gain"].unsqueeze(1)).then_inc(ld_rows, 16)
            for m in range(NTT):
                src = a["ctx"][0, m * P:(m + 1) * P, :] if m < 2 else a["x"][0, (m - 2) * P:(m - 1) * P, :]
                sp.dma_start(XT[:, m, :], src).then_inc(ld_x, 16)
            for i in range(4):
                sp.dma_start(ADA0[:, i], w_view(a["l0_ada_w"])[:, :, i * 512:(i + 1) * 512]).then_inc(ld_ada0[i], 16)
            with sp.Fori(0, 2) as i:
                for s in range(2):
                    load_unit(sp, U_IN + 2 * i + s, s,
                              [(RAW[:, s, :, 128 * r + 64 * h:128 * r + 64 * h + 64],
                                w_view(a["l0_w_in"])[:, :, bass.ds(512 * i + 256 * h + 128 * s + 64 * r, 64)])
                               for r in range(2) for h in range(2)])
            for s in range(2):
                load_unit(sp, U_IN + 4 + s, s, plain(a["l0_w_in"], D + UC * s, s))
            sp.wait_ge(ada0_done, 1)
            sp.wait_ge(xt_done, 12)
            sp.dma_start(ROPE[:, :, :].rearrange("p a b -> p (a b)"), a["table"][:, OFFSET["rope_cos"][0]:OFFSET["rope_cos"][0] + 2 * TX]).then_inc(ld_rope, 16)
            def load_out0(u):
                load_unit(sp, U_OUT0 + u, u % 2,
                          [(RAW[64 * h:64 * h + 64, u % 2, 4 * g:4 * g + 4, :],
                            a["l0_w_out"].rearrange("(g a r d) n -> g a d r n", g=2, a=2, r=4)[g, h][:, :, u * UC:(u + 1) * UC])
                           for h in range(2) for g in range(2)])

            load_out0(0)
            load_out0(1)
            with sp.Fori(0, 8) as g:
                for c in range(2):
                    load_ada(sp, 2 * g + c, 0, 2048 + 512 * g + 256 * c)
            load_out0(2)
            load_out0(3)
            with sp.Fori(0, 4) as c:
                with sp.Fori(0, 2) as i:
                    for s in range(2):
                        load_unit(sp, U_MLP0 + 8 * c + 2 * i + s, s, plain(a["l0_mlp_up"], 1024 * c + 512 * i + 256 * s, s))
                        load_ada(sp, 16 + 6 * c + 2 * i + s, 1, (6 * c + 2 * i + s) * UC)
                with sp.Fori(0, 2) as i:
                    for s in range(2):
                        v = a["l0_mlp_down"][bass.ds(1024 * c, 1024), :]
                        load_unit(sp, U_MLP0 + 8 * c + 4 + 2 * i + s, s, plain(v, 512 * i + 256 * s, s))
                    load_ada(sp, 16 + 6 * c + 4 + i, 1, (6 * c + 4 + i) * UC)
            def load_rkv(j, w):
                load_unit(sp, U_RKV + j, j % 2, plain(a["l1_w_rkv"][w], UC * (j % 4), j % 2))

            def load_lora():
                load_unit(sp, U_LORA, 0, [(RAW[:, 0, :, 64 * (2 * i + d):64 * (2 * i + d) + 64], w_view(a[n][d]))
                                          for i, n in enumerate(("l1_w1", "l1_a1")) for d in range(2)])

            def load_gate():
                v = w_view(a["l1_g1"])
                load_unit(sp, U_LORA + 1, 1, [(RAW[:, 1, 4 * h:4 * h + 4, 0:P], v[:, 4 * h:4 * h + 4, :]) for h in range(2)])

            for j in range(2):
                load_rkv(j, 1)
            for j in range(12):
                if j < 10:
                    load_rkv(j + 2, (1, 2, 0)[(j + 2) // 4])
                elif j == 10:
                    load_lora()
                else:
                    load_gate()
                sp.wait_ge(evac_act, U_RKV + j + 3)
                sp.wait_ge(evac_dve, U_RKV + j + 3)
                for n in range(2):
                    sp.dma_start(SCR[j // 4, 2 * (j % 4) + n], STG[:, 2 * (j % 2) + n, :]).then_inc(stg_stored[j % 2], 16)
            for s in range(2):
                load_unit(sp, U_OUT1 + s, s, plain(a["l1_w_out"], UC * s, s))
            for s in range(2):
                sp.wait_ge(stg_stored[s], 32 * 6)
            sp.wait_ge(w_used, U_LORA + 4)
            sp.dma_start(CT[:, :], a["table"][:, CORE_FIRST:]).then_inc(g_loaded, 16)
            with sp.Fori(0, KT) as g:
                sp.wait_ge(og_ready, g + 1)
                cols = bass.ds(P * g, P)
                for dst, src in ((KG, SCR[0]), (VG, SCR[1])):
                    sp.dma_start(dst[:, :], src[bass.ds(g, 1)].rearrange("a p t -> p (a t)")).then_inc(g_loaded, 16)
                sp.dma_start(RG[:, :], SCR[2, bass.ds(g, 1), :, TC:].rearrange("a p t -> p (a t)")).then_inc(g_loaded, 16)
                sp.dma_start(W2G[:, :], a["l1_w2"].rearrange("d r c -> (d r) c")[:, cols]).then_inc(g_loaded, 16)
                sp.dma_start(A2G[:, :], a["l1_a2"].rearrange("d r c -> (d r) c")[:, cols]).then_inc(g_loaded, 16)
                sp.dma_start(G2G[:, :], a["l1_g2"][:, cols]).then_inc(g_loaded, 16)
                sp.dma_start(W0G[:, :, :], a["l1_w0"][:, cols].unsqueeze(0)).then_inc(g_loaded, 16)
            for s in range(2):
                load_unit(sp, U_OUT1 + 2 + s, s, plain(a["l1_w_out"], UC * (2 + s), s))
            with sp.Fori(0, 4) as c:
                with sp.Fori(0, 2) as i:
                    for s in range(2):
                        load_unit(sp, U_MLP1 + 8 * c + 2 * i + s, s, plain(a["l1_mlp_up"], 1024 * c + 512 * i + 256 * s, s))
                with sp.Fori(0, 2) as i:
                    for s in range(2):
                        v = a["l1_mlp_down"][bass.ds(1024 * c, 1024), :]
                        load_unit(sp, U_MLP1 + 8 * c + 4 + 2 * i + s, s, plain(v, 512 * i + 256 * s, s))
            for i in range(2):
                sp.wait_ge(f_read, 4 * i + 4)
                sp.dma_start(out[0].rearrange("(m p) c -> p m c", p=P)[:, :, 512 * i:512 * i + 512],
                             OUTT[:, :, 512 * i:512 * i + 512]).then_inc(stored, 16)
            sp.wait_ge(stored, 32)

        @block.gpsimd
        def _(pool):
            pool.memset(ONES[:, :], 1.0).then_inc(ones_ready, 1)
            for j, v in enumerate((EPS, GN_EPS, 8 * math.log(2))):
                pool.memset(EPSC[:, j:j + 1], v).then_inc(ones_ready, 1)
            pool.sem_inc(w_split, 2)
            with pool.Fori(0, U_OUT0 // 2) as i:
                for s in range(2):
                    pool_split(pool, 2 * i + s, s)
            pool.wait_ge(ld_rope, 16)

            def rope_cos(idx, s):
                pool.wait_ge(hn_q, idx + 1)
                pool.tensor_tensor(HC[:, s, :], HN[:, s, TC:], ROPE[:, 0, :], ALU.mult).then_inc(hn_c, 1)

            with pool.Fori(0, 5) as i:
                for s in range(2):
                    rope_cos(2 * i + s, s)
            with pool.Fori(U_OUT0 // 2, U_OUT1 // 2) as i:
                for s in range(2):
                    pool_split(pool, 2 * i + s, s)
            pool_split(pool, U_OUT1, 0)
            pool.wait_ge(w_used, U_LORA + 4)
            pool.memset(AR[:, 0:TC // P, 1, :], 0.0).then_inc(ar_zero, 1)
            pool.memset(WP[0][:, :, 0:1], 1.0).then_inc(ar_zero, 1)
            pool.memset(WP[1][:, :, C:C + 1], 1.0).then_inc(ar_zero, 1)
            with pool.Fori(0, KT) as g:
                for d in range(2):
                    pool_build(pool, g, d)
            pool_split(pool, U_OUT1 + 1, 1)
            with pool.Fori(U_OUT1 // 2 + 1, UNITS // 2) as i:
                for s in range(2):
                    pool_split(pool, 2 * i + s, s)

        @block.scalar
        def _(act):
            act.wait_ge(par_ready, 3)
            act.activation(SV[:, :, :].rearrange("p k v -> p v k"), PAR[:, 256:272].rearrange("p (v k) -> p v k", v=2),
                           ACT.Exp, scale=-1.0).then_inc(silu_a, 1)
            act.sem_inc(evac_act, 2)
            for i in range(NTT):
                act.wait_ge(xt_done, 2 * i + 2)
                act.activation(X[:, 4:8, i * P:(i + 1) * P], bank((2 * i + 1) % 4).rearrange("p (k t) -> p k t", k=4),
                               ACT.Copy).then_inc(xv_act, 1)
            act.wait_ge(ones_ready, 4)
            act.wait_ge(xv_dve, NTT)
            act.wait_ge(xv_act, NTT)
            norm_act_stats(act, 0, 0)
            act.wait_ge(mod_ready, 1)
            norm_act_high(act, 0, 0, 0, 0, AH)
            act_split(act, 0, 0, LANDED[0])
            for i in range(3):
                for s in range(2):
                    u = 2 * i + s
                    act_split(act, u + 1, 1 - s, LANDED[u + 1])
                    act.wait_ge(w_used, u + 3)
                    act.activation(QKV[:, bass.ds(2 * u, 1), :].rearrange("p a t -> p (a t)"), tile_ps(4 * s),
                                   ACT.Copy).then_inc(evac_act, 1)
            def head_norm(tiles, idx):
                for s in range(2):
                    act.wait_ge(hn_done, idx + s + 1)
                    act.activation(HQ[:, s, :], tiles[s], ACT.Square).then_inc(hn_sq, 1)
                for s in range(2):
                    act.wait_ge(hn_stat, idx + s + 1)
                    act.activation(HR[:, s, :], tile_ps(2 * s), ACT.Ln, bias=EPSC[:, 0:1], scale=1.0 / HD).then_inc(hn_ln, 1)
                    act.wait_ge(hn_ln, idx + s + 1)
                    act.activation(HR[:, s, :], HR[:, s, :], ACT.Exp, scale=-0.5).then_inc(hn_rs, 1)

            act.wait_ge(evac_act, U_OUT0 + 2)
            act.wait_ge(evac_dve, U_OUT0 + 2)
            with act.Fori(0, 5) as i:
                head_norm([QKV[:, bass.ds(2 * i + s, 1), :].rearrange("p a t -> p (a t)") for s in range(2)], 2 * i)
            for p in range(2):
                act.wait_ge(v_t, p + 1)
                act.activation(VS[:, 2 * p:2 * p + 2, :, 0:HD].rearrange("p j l d -> p l j d"),
                               PS[:, 3072:3072 + T].rearrange("p (l j d) -> p l j d", l=NTT, j=2), ACT.Copy).then_inc(v_high, 1)
            act.wait_ge(hn_done, 12)
            for p in range(2):
                if p:
                    act.wait_ge(t_done, 48 + 2)
                for j in range(2):
                    for h in range(2):
                        act.activation(KH2[64 * h:64 * h + 64, j, :], QKV[64 * j:64 * j + 64, 8 + p, :],
                                       ACT.Copy).then_inc(k_high, 1)
                if not p:
                    act.sem_inc(e_done, 2)
                with act.Fori(4 * p, 4 * p + 4) as g:
                    attn_act(act, g)
            act.wait_ge(o_done, 49)
            for k in range(KT):
                act.activation(BH[:, k, :], OT[:, k, :], ACT.Copy).then_inc(ot_high, 1)
            for i in range(2):
                for s in range(2):
                    add_act(act, U_OUT0 + 2 * i + s, s, LANDED[U_OUT0 + 2 * i + s + 1])
            act.wait_ge(evac_dve, U_MLP0 + 2)
            norm_act_stats(act, 1, 0)
            norm_act_high(act, 1, 0, 1, 0, AH)
            with act.Fori(0, 4) as c:
                with act.Fori(0, 2) as i:
                    for s in range(2):
                        u = U_MLP0 + 8 * c + 2 * i + s
                        mlp_up_act(act, u, s, 4 * i + 2 * s, 8 * c + 4 * i + 2 * s, 0, LANDED[U_MLP0] + 4 * c + i + s)
                with act.Fori(0, 2) as i:
                    for s in range(2):
                        add_act(act, U_MLP0 + 8 * c + 4 + 2 * i + s, s, LANDED[U_MLP0] + 4 * c + 2 + i + s)
            act.wait_ge(evac_dve, U_RKV + 2)
            norm_act_stats(act, 2, 0)
            norm_act_high(act, 2, 1, 0, 0, U)
            mix_act(act, 0)
            for j in range(12):
                if j % 4 == 3:
                    mix_act(act, j // 4 + 1)
                act_split(act, U_RKV + j + 1, (j + 1) % 2, LANDED[U_RKV + j + 1])
                stage(act, j, 0, evac_act)
            act_split(act, U_LORA + 1, 1, LANDED[U_LORA + 1])
            mix_act(act, 4)
            mix_act(act, 5)
            act.wait_ge(w_used, U_LORA + 3)
            act.activation(LW[:, :], tile_ps(0), ACT.Tanh).then_inc(evac_act, 1)
            act_split(act, U_OUT1, 0, LANDED[U_OUT1])
            act.wait_ge(w_used, U_LORA + 4)
            act.activation(LG[:, :], tile_ps(4)[:, TC:], ACT.Tanh, scale=0.5).then_inc(lg_tanh, 1)
            act.wait_ge(lg_tanh, 1)
            act.sem_inc(evac_act, 1)
            act.sem_inc(y_ready, 1)
            act.wait_ge(ar_zero, 3)
            act.wait_ge(consts1, 2)
            with act.Fori(0, KT) as g:
                act_group(act, g)
                for d in range(2):
                    act_build(act, g, d)
                    act_chain(act, g, d)
                act_finish(act, g)
            act.wait_ge(og_ready, KT + 1)
            for k in range(KT):
                act.activation(AH[:, k, TC:], OG[:, k, :], ACT.Copy).then_inc(ot_high, 1)
            for j in range(4):
                add_act(act, U_OUT1 + j, j % 2, LANDED[U_OUT1 + j + 1])
            act.wait_ge(evac_dve, U_MLP1 + 2)
            norm_act_stats(act, 3, TC)
            norm_act_high(act, 3, 1, 1, TC, AH)

            def mlp_act(c, whole):
                with act.Fori(0, 2) as i:
                    for s in range(2):
                        mlp_up_act(act, U_MLP1 + 8 * c + 2 * i + s, s, 4 * i + 2 * s, 32 + 8 * c + 4 * i + 2 * s, TC,
                                   LANDED[U_MLP1 + 1 + s] + 4 * c + i)
                with act.Fori(0, 2 if whole else 1) as i:
                    for s in range(2):
                        add_act(act, U_MLP1 + 8 * c + 4 + 2 * i + s, s, LANDED[U_MLP1 + 1 + s] + 4 * c + 2 + i)

            with act.Fori(0, 3) as c:
                mlp_act(c, True)
            mlp_act(3, False)
            add_act(act, UNITS - 2, 0, LANDED[UNITS - 1])
            add_act(act, UNITS - 1, 1, None)
            act.wait_ge(evac_dve, UNITS + 2)
            norm_act_stats(act, 4, TC)
            for k in range(KT):
                act.wait_ge(f_done, k + 1)
                act.activation(OUTT[:, :, k * P:(k + 1) * P], bank(2 + k % 4).rearrange("p (m c) -> p m c", c=P),
                               ACT.Copy).then_inc(f_read, 1)

        @block.tensor
        def _(pe):
            pe.sem_inc(w_used, 2)
            pe.sem_inc(ada_used, 1)
            pe.wait_ge(ld_const, 16)
            pe.wait_ge(ld_rows, 16 * ROW_LOADS)
            for b in range(3):
                n = (P, 112, 16)[b]
                pe.transpose(bank(7)[:, b * P:b * P + n], ROWS[0:n, b, :], IDN[0:n, 0:n]).then_inc(par_t, 1)
            pe.wait_ge(ld_x, 16 * NTT)
            for i in range(2 * NTT):
                if i >= 4:
                    pe.wait_ge((xv_dve, xv_act)[i % 2], i // 2 - 1)
                for k in range(4):
                    kk = 4 * (i % 2) + k
                    mm = pe.transpose(bank(i % 4)[:, k * P:(k + 1) * P], XT[:, i // 2, kk * P:(kk + 1) * P], IDN)
                mm.then_inc(xt_done, 1)
            pe.wait_ge(sv_ready, 1)
            for i in range(4):
                pe.wait_ge(ld_ada0[i], 16)
                for n in range(4):
                    for k in range(KT):
                        mm = pe.matmul(bank(4)[:, 8 * i + 2 * n:8 * i + 2 * n + 2], ADA0[:, i, k, n * P:(n + 1) * P],
                                       SV[:, k, :], start=(k == 0), stop=(k == KT - 1), skip_group_check=True)
            mm.then_inc(ada0_done, 1)
            pe.wait_ge(ones_ready, 4)
            pe.wait_ge(xv_act, NTT)
            pe.wait_ge(xv_dve, NTT)
            norm_pe_stats(pe, 0, 0)
            with pe.Fori(0, 3) as i:
                for s in range(2):
                    pe_unit(pe, 2 * i + s, s, AH, AL, k_ready=after_norm(0))
            pe.wait_ge(evac_act, U_OUT0 + 2)
            pe.wait_ge(evac_dve, U_OUT0 + 2)

            def head_norm(idx):
                for s in range(2):
                    pe.wait_ge(hn_sq, idx + s + 1)
                    for a0, a1 in STREAMS:
                        mm = pe.matmul(tile_ps(2 * s)[:, a0:a1], HEAD1, HQ[:, s, a0:a1], start=True, stop=True,
                                       skip_group_check=True)
                    mm.then_inc(hn_stat, 1)
                for s in range(2):
                    pe.wait_ge(hn_q, idx + s + 1)
                    pe.matmul(bank(4 + s), SWAP, HN[:, s, TC:], start=True, stop=True).then_inc(hn_sw, 1)

            with pe.Fori(0, 5) as i:
                head_norm(2 * i)
            for p in range(2):
                if p:
                    pe.wait_ge(v_low, 1)
                for l in range(NTT):
                    mm = pe.transpose(PS[:, 3072 + l * P:3072 + (l + 1) * P], QKV[:, 10 + p, l * P:(l + 1) * P], IDN)
                mm.then_inc(v_t, 1)
            pe.wait_ge(hn_done, 12)
            pe.wait_ge(v_low, 2)
            pe.sem_inc(t_done, 2)
            pe.sem_inc(s_done, 1)
            for p in range(2):
                pe.wait_ge(k_low, 4 * p + 4)
                with pe.Fori(4 * p, 4 * p + 4) as g:
                    attn_pe(pe, g, p)
            pe.wait_ge(o_done, 49)

            def ot_ready(e, k):
                e.wait_ge(ot_low, k + 1)

            with pe.Fori(0, 2) as i:
                for s in range(2):
                    pe_unit(pe, U_OUT0 + 2 * i + s, s, BH, BL, k_ready=ot_ready)
            pe.wait_ge(evac_dve, U_MLP0 + 2)
            norm_pe_stats(pe, 1, 0)
            pe.wait_ge(n_ln, 2)
            with pe.Fori(0, 4) as c:
                with pe.Fori(0, 2) as i:
                    for s in range(2):
                        pe_ada(pe, 17 + 6 * c + 2 * i + s, 4 * s, 0, U_MLP0 + 8 * c + 2 * i + s)
                        pe_unit(pe, U_MLP0 + 8 * c + 2 * i + s, s, AH, AL, k_ready=after_norm(1))

                def hidden_ready(e, k):
                    e.wait_ge(h_low, 8 * c + k + 3)

                with pe.Fori(0, 2) as i:
                    pe_ada(pe, 17 + 6 * c + 4 + i, 0, 0, U_MLP0 + 8 * c + 4 + 2 * i)
                    for s in range(2):
                        pe_unit(pe, U_MLP0 + 8 * c + 4 + 2 * i + s, s, BH, BL, k_ready=hidden_ready)
            pe.wait_ge(evac_act, U_RKV + 2)
            pe.wait_ge(evac_dve, U_RKV + 2)
            norm_pe_stats(pe, 2, 0)
            pe.wait_ge(n_ln, 3)
            for n in range(2):
                for i in range(4):
                    pe_unit(pe, U_RKV + 4 * n + i, i % 2, AH, AL, k_ready=mix_ready(n), k_used=mx_used)
            for i in range(4):
                pe_unit(pe, U_RKV + 8 + i, i % 2, AH, AL, streams=(1,), k_ready=mix_ready(2), k_used=mx_used)
            pe_unit(pe, U_LORA, 0, AH, AL, ntiles=(0,), k_ready=mix_ready(3), k_used=mx_used, done=lora_done)
            pe_unit(pe, U_LORA, 0, AH, AL, ntiles=(1,), k_ready=mix_ready(4), k_used=mx_used)
            pe_unit(pe, U_LORA + 1, 1, AH, AL, streams=(1,), ntiles=(0,), k_ready=mix_ready(5))
            pe.wait_ge(lora_ready, 1)
            pe.wait_ge(evac_act, U_OUT1 + 2)
            pe.wait_ge(evac_dve, U_OUT1 + 2)
            pe.wait_ge(ar_zero, 3)
            with pe.Fori(0, KT) as g:
                pe_group(pe, g)
                for d in range(2):
                    pe_build(pe, g, d)
                    pe_chain(pe, g, d)
                pe_finish(pe, g)
            pe.wait_ge(og_ready, KT + 1)

            def og_split(e, k):
                e.wait_ge(ot_low, KT + k + 1)

            with pe.Fori(0, 2) as i:
                for s in range(2):
                    pe_unit(pe, U_OUT1 + 2 * i + s, s, AH, AL, streams=(1,), k_ready=og_split)
            pe.wait_ge(evac_act, U_MLP1 + 2)
            pe.wait_ge(evac_dve, U_MLP1 + 2)
            norm_pe_stats(pe, 3, TC)
            pe.wait_ge(n_ln, 4)
            with pe.Fori(0, 4) as c:
                with pe.Fori(0, 2) as i:
                    for s in range(2):
                        pe_unit(pe, U_MLP1 + 8 * c + 2 * i + s, s, AH, AL, streams=(1,), k_ready=after_norm(2))

                def hidden1_ready(e, k):
                    e.wait_ge(h_low, 32 + 8 * c + k + 3)

                with pe.Fori(0, 2) as i:
                    for s in range(2):
                        pe_unit(pe, U_MLP1 + 8 * c + 4 + 2 * i + s, s, BH, BL, streams=(1,), k_ready=hidden1_ready)
            pe.wait_ge(evac_act, UNITS + 2)
            pe.wait_ge(evac_dve, UNITS + 2)
            norm_pe_stats(pe, 4, TC)
            for k in range(KT):
                pe.wait_ge(n_t, KT * 4 + k + 1)
                if k >= 4:
                    pe.wait_ge(f_read, k - 3)
                for m in range(4):
                    mm = pe.transpose(bank(2 + k % 4)[:, m * P:(m + 1) * P], TN[:, k % 2, TC + m * P:TC + (m + 1) * P], IDN)
                mm.then_inc(f_done, 1)

        @block.vector
        def _(dve):
            dve.sem_inc(evac_dve, 2)
            dve.sem_inc(ada_read, 1)
            dve.sem_inc(hn_done, 2)
            dve.sem_inc(h_low, 2)
            dve.wait_ge(par_t, 3)
            dve.tensor_copy(PAR[:, 0:240], bank(7)[:, 0:240]).then_inc(par_ready, 1)
            dve.tensor_copy(PAR[:, 256:272], bank(7)[:, 256:272]).then_inc(par_ready, 2)
            dve.wait_ge(silu_a, 1)
            dve.tensor_scalar(SV[:, :, :], SV[:, :, :], 1.0, None, ALU.add).then_inc(sv_step, 1)
            dve.wait_ge(sv_step, 1)
            dve.reciprocal(SV[:, :, :], SV[:, :, :]).then_inc(sv_step, 1)
            dve.wait_ge(sv_step, 2)
            dve.tensor_tensor(SV[:, :, :], SV[:, :, :], PAR[:, 256:272].rearrange("p (v k) -> p k v", v=2),
                              ALU.mult).then_inc(sv_ready, 1)
            dve.wait_ge(par_ready, 3)
            dve.tensor_scalar(A0H[:, :], col(1, ROWS_B["a0"], 16), 0.5, None, ALU.mult).then_inc(consts1, 1)
            dve.tensor_scalar(KA1[:, :], col(1, ROWS_B["k_a"], KT), -1.0, 1.0, ALU.mult, ALU.add).then_inc(consts1, 1)
            for i in range(NTT):
                dve.wait_ge(xt_done, 2 * i + 1)
                dve.tensor_copy(X[:, 0:4, i * P:(i + 1) * P], bank((2 * i) % 4).rearrange("p (k t) -> p k t", k=4))\
                   .then_inc(xv_dve, 1)
            dve.wait_ge(ada0_done, 1)
            dve.tensor_tensor(MOD[:, 0, 0:16, :], bank(4)[:, 0:32].rearrange("p (n v) -> p n v", v=2),
                              PAR[:, 0:16].unsqueeze(2).to_broadcast([P, 16, 2]), ALU.add).then_inc(mod_ready, 1)
            dve.wait_ge(mod_ready, 1)
            dve.wait_ge(xv_act, NTT)
            dve.wait_ge(xv_dve, NTT)
            norm_dve(dve, 0, 0, 0, 0, 0)
            with dve.Fori(0, 3) as i:
                for s in range(2):
                    u = 2 * i + s
                    dve.wait_ge(w_used, u + 3)
                    dve.tensor_copy(QKV[:, bass.ds(2 * u + 1, 1), :].rearrange("p a t -> p (a t)"), tile_ps(4 * s + 2))\
                       .then_inc(evac_dve, 1)
            dve.wait_ge(evac_act, U_OUT0 + 2)
            dve.wait_ge(evac_dve, U_OUT0 + 2)

            def head_norm(tiles, idx, gain):
                for s in range(2):
                    dve.wait_ge(hn_rs, idx + s + 1)
                    dve.scalar_tensor_tensor(out=HN[:, s, :], in0=tiles[s], scalar=QKG[:, gain:gain + 1],
                                             in1=HR[:, s, :], op0=ALU.mult, op1=ALU.mult).then_inc(hn_q, 1)
                for s in range(2):
                    dve.wait_ge(hn_sw, idx + s + 1)
                    dve.tensor_tensor(HQ[:, s, 0:TX], bank(4 + s), ROPE[:, 1, :], ALU.mult).then_inc(hn_s, 1)
                    dve.tensor_copy(tiles[s][:, 0:TC], HN[:, s, 0:TC])
                    dve.wait_ge(hn_s, idx + s + 1)
                    dve.wait_ge(hn_c, idx + s + 1)
                    dve.tensor_tensor(tiles[s][:, TC:], HC[:, s, :], HQ[:, s, 0:TX], ALU.add).then_inc(hn_done, 1)

            dve.wait_ge(ld_rope, 16)
            with dve.Fori(0, 4) as i:
                head_norm([QKV[:, bass.ds(2 * i + s, 1), :].rearrange("p a t -> p (a t)") for s in range(2)], 2 * i, 0)
            head_norm([QKV[:, 8 + s, :] for s in range(2)], 8, 1)
            dve.sem_inc(ptl, 1)
            dve.sem_inc(ob_done, 1)
            dve.sem_inc(o_done, 1)
            for p in range(2):
                dve.wait_ge(v_high, p + 1)
                dve.tensor_tensor(VS[:, 2 * p:2 * p + 2, :, HD:].rearrange("p j l d -> p l j d"),
                                  PS[:, 3072:3072 + T].rearrange("p (l j d) -> p l j d", l=NTT, j=2),
                                  VS[:, 2 * p:2 * p + 2, :, 0:HD].rearrange("p j l d -> p l j d"),
                                  ALU.subtract).then_inc(v_low, 1)
            dve.wait_ge(hn_done, 12)
            for p in range(2):
                dve.wait_ge(k_high, 4 * p + 4)
                for j in range(2):
                    for h in range(2):
                        dve.tensor_tensor(KL2[64 * h:64 * h + 64, j, :], QKV[64 * j:64 * j + 64, 8 + p, :],
                                          KH2[64 * j:64 * j + 64, j, :], ALU.subtract).then_inc(k_low, 1)
                with dve.Fori(4 * p, 4 * p + 4) as g:
                    attn_dve(dve, g)
            dve.wait_ge(o_done, 49)
            for k in range(KT):
                dve.wait_ge(ot_high, k + 1)
                dve.tensor_tensor(BL[:, k, :], OT[:, k, :], BH[:, k, :], ALU.subtract).then_inc(ot_low, 1)
            with dve.Fori(0, 2) as i:
                for s in range(2):
                    add_dve(dve, U_OUT0 + 2 * i + s, s, 4 * i + 2 * s, 0, 2, 0)
            dve.wait_ge(evac_dve, U_MLP0 + 2)
            norm_dve(dve, 1, 0, 1, 0, 1)
            with dve.Fori(0, 4) as c:
                with dve.Fori(0, 2) as i:
                    for s in range(2):
                        mlp_up_dve(dve, U_MLP0 + 8 * c + 2 * i + s, 4 * i + 2 * s, 8 * c + 4 * i + 2 * s, 0,
                                   (16 + 6 * c + 2 * i + s, 1, 2 * (6 * c + 2 * i + s), 4 * s, 0))
                with dve.Fori(0, 2) as i:
                    for s in range(2):
                        add_dve(dve, U_MLP0 + 8 * c + 4 + 2 * i + s, s, 4 * i + 2 * s, 0, 5, 0,
                                None if s else (16 + 6 * c + 4 + i, 1, 2 * (6 * c + 4 + i), 0, 0))
            dve.wait_ge(evac_dve, U_RKV + 2)
            norm_dve(dve, 2, 1, 0, 0, None)
            dve.wait_ge(n_h, KT * 3)
            dve.tensor_copy(XX[:, :, 0:TC + 1:TC], U[:, :, 1:TC + 2:TC]).then_inc(xx_step, 1)
            dve.tensor_copy(XX[:, :, TC - 1:T:TX], U[:, :, TC - 2:T - 1:TX]).then_inc(xx_step, 1)
            for k in range(KT):
                for a0, a1 in STREAMS:
                    dve.tensor_tensor(XX[:, k, a0 + 1:a1 - 1], U[:, k, a0:a1 - 2], U[:, k, a0 + 2:a1], ALU.add)\
                       .then_inc(xx_step, 1)
                dve.wait_ge(xx_step, 2 * k + 4)
                dve.scalar_tensor_tensor(out=XX[:, k, :], in0=XX[:, k, :], scalar=0.5, in1=U[:, k, :], op0=ALU.mult,
                                         op1=ALU.subtract).then_inc(xx_ready, 1)
            mix_dve(dve, 0)
            for j in range(12):
                if j % 4 == 3:
                    mix_dve(dve, j // 4 + 1)
                stage(dve, j, 1, evac_dve)
            mix_dve(dve, 4)
            mix_dve(dve, 5)
            dve.wait_ge(w_used, U_LORA + 3)
            dve.tensor_copy(LA[:, :], tile_ps(2)).then_inc(evac_dve, 1)
            dve.wait_ge(lg_tanh, 1)
            dve.tensor_scalar(LG[:, :], LG[:, :], 0.5, 0.5, ALU.mult, ALU.add).then_inc(lora_ready, 1)
            dve.sem_inc(evac_dve, 1)
            dve.sem_inc(og_ready, 1)
            dve.wait_ge(ar_zero, 3)
            dve.wait_ge(consts1, 2)
            with dve.Fori(0, KT) as g:
                dve_group(dve, g)
                for d in range(2):
                    dve_build(dve, g, d)
                    dve_chain(dve, g, d)
                dve_finish(dve, g)
            for k in range(KT):
                dve.wait_ge(ot_high, KT + k + 1)
                dve.tensor_tensor(AL[:, k, TC:], OG[:, k, :], AH[:, k, TC:], ALU.subtract).then_inc(ot_low, 1)
            with dve.Fori(0, 2) as i:
                for s in range(2):
                    add_dve(dve, U_OUT1 + 2 * i + s, s, 4 * i + 2 * s, 1, 2, TC)
            dve.wait_ge(evac_dve, U_MLP1 + 2)
            norm_dve(dve, 3, 1, 1, TC, 2)
            with dve.Fori(0, 4) as c:
                with dve.Fori(0, 2) as i:
                    for s in range(2):
                        mlp_up_dve(dve, U_MLP1 + 8 * c + 2 * i + s, 4 * i + 2 * s, 32 + 8 * c + 4 * i + 2 * s, TC)
                with dve.Fori(0, 2) as i:
                    for s in range(2):
                        add_dve(dve, U_MLP1 + 8 * c + 4 + 2 * i + s, s, 4 * i + 2 * s, 1, 5, TC)
            dve.wait_ge(evac_dve, UNITS + 2)
            dve.wait_ge(n_rs, 5)
            for k in range(KT):
                if k >= 2:
                    dve.wait_ge(f_done, k - 1)
                dve.scalar_tensor_tensor(out=TN[:, k % 2, TC:], in0=X[:, k, TC:], scalar=col(1, ROWS_B["final"] + k),
                                         in1=RS[:, TC:], op0=ALU.mult, op1=ALU.mult).then_inc(n_t, 1)


_INS = ["x", "c", "ctx", "c_ctx", "l0_ada_w", "l0_ada_b", "l0_norm1", "l0_w_in", "l0_q_gain", "l0_k_gain", "l0_w_out",
        "l0_norm2", "l0_mlp_up", "l0_mlp_down", "l1_ada_w", "l1_ada_b", "l1_norm1", "l1_mu", "l1_w_rkv", "l1_w0",
        "l1_w1", "l1_w2", "l1_a0", "l1_a1", "l1_a2", "l1_g1", "l1_g2", "l1_k_k", "l1_k_a", "l1_r_k", "l1_ln_w",
        "l1_ln_b", "l1_w_out", "l1_norm2", "l1_mlp_up", "l1_mlp_down", "final_norm"]


def kernel(**inputs):
    import numpy as _np
    import concourse.bacc as _bacc
    from concourse import mybir as _mybir
    from concourse.bass_utils import run_bass_kernel_spmd as _run

    nc = _bacc.Bacc("TRN2", target_bir_lowering=False, num_devices=1)
    arrays = {name: _np.ascontiguousarray(inputs[name]) for name in _INS}
    arrays["table"] = _np.ascontiguousarray(_np.concatenate(list(TABLE.values()), 1))
    args = {name: nc.dram_tensor(name, v.shape, _mybir.dt.from_np(v.dtype), kind="ExternalInput").ap()
            for name, v in arrays.items()}
    out = nc.dram_tensor("out", (1, TX, D), _mybir.dt.float32, kind="ExternalOutput").ap()
    build(nc, args, out)
    r = _run(nc, [arrays], core_ids=[0])
    return r.results[0]["out"]
```

```python
import math
from contextlib import ExitStack

import numpy as np

import concourse.bass as bass
from concourse import mybir

F32 = mybir.dt.float32
F32R = mybir.dt.float32r
ALU = mybir.AluOpType
ACT = mybir.ActivationFunctionType
AX = mybir.AxisListType

P = 128
D = 1024
KT = D // P
TC, TX = 256, 512
T = TC + TX
NTT = T // P
FF = 4 * D
GRID_W = 64
EPS = 1e-6
HD = 64
UC = 256
C = 64
NCH = T // C
GN_EPS = 64e-5
DEC = float(np.exp(-0.5))
SCALE = HD ** -0.5
RING = 48
GROUP_LOADS = 7
STREAMS = ((0, TC), (TC, T))


def const_table():
    f = np.float32
    t = {}
    t["ident"] = np.eye(P, dtype=f)
    head = np.kron(np.eye(2), np.ones((HD, HD))).astype(f)
    t["head_ones"] = head
    swap = np.zeros((P, P), f)
    for h in range(2):
        for i in range(HD):
            swap[h * HD + (i + HD // 2) % HD, h * HD + i] = 1.0
    t["swap"] = swap
    tok = np.arange(TX)
    row, col = (tok // GRID_W).astype(f), (tok % GRID_W).astype(f)
    nf = HD // 4
    inv = (f(10000.0) ** (-np.arange(nf, dtype=f) / f(nf))).astype(f)
    ang = np.concatenate([row[:, None] * inv, col[:, None] * inv], axis=-1).astype(f)
    c, s = np.cos(ang).T.astype(f), np.sin(ang).T.astype(f)
    t["rope_cos"] = np.concatenate([c, c, c, c], 0)
    t["rope_sin"] = np.concatenate([-s, s, -s, s], 0)
    i = np.arange(P)
    same = (i[:, None] // C) == (i[None, :] // C)
    for d in range(2):
        before = (i[:, None] < i[None, :]) if d == 0 else (i[:, None] > i[None, :])
        strict = (before & same).astype(f)
        incl = strict + np.eye(P, dtype=f)
        t[f"cum{d}"] = incl
        t[f"masks{d}"] = np.concatenate([strict, incl], 1)
        lv = []
        for l in range(6):
            b = 1 << l
            m = ((i[:, None] // (2 * b)) == (i[None, :] // (2 * b))) & ((i[:, None] // b) != (i[None, :] // b))
            lv.append((m & (strict.T > 0)).astype(f) + np.eye(P, dtype=f))
        for l in range(6):
            t[f"level{d}{l}"] = lv[l]
    return t


PARAM = {"ada_b0": "l0_ada_b", "ada_b1": "l1_ada_b", "norm1_0": "l0_norm1", "norm2_0": "l0_norm2",
         "norm1_1": "l1_norm1", "norm2_1": "l1_norm2", "mu": "l1_mu", "k_k": "l1_k_k", "k_a": "l1_k_a",
         "r_k": "l1_r_k", "ln_w": "l1_ln_w", "ln_b": "l1_ln_b", "final": "final_norm", "a0": "l1_a0"}
ROW_LOADS = len(PARAM) + 2 + 4

TABLE = const_table()
OFFSET, _at = {}, 0
for _n, _a in TABLE.items():
    OFFSET[_n] = (_at, _a.shape[1])
    _at += _a.shape[1]
TABLE_W = _at
ATTN_NAMES = ["rope_cos", "rope_sin"]
CORE_FIRST = OFFSET["cum0"][0]
CORE_W = TABLE_W - CORE_FIRST

ROWS_A = {"ada_b0": 0, "ada_b1": 48, "norm1_0": 96, "norm2_0": 104, "norm1_1": 112, "norm2_1": 120}
ROWS_B = {"mu": 0, "k_k": 48, "k_a": 56, "r_k": 64, "ln_w": 72, "ln_b": 80, "final": 88, "a0": 96}
ROWS_C = {"c": 0, "c_ctx": 8}

U_IN, U_OUT0, U_MLP0 = 0, 6, 10
U_RKV, U_LORA, U_OUT1, U_MLP1 = 42, 54, 56, 60
UNITS = 92

FOUR = (0, 1, 2, 3, 6, 7, 8, 9, 54)
LANDED = [sum(2 if v in FOUR else 1 for v in range(u % 2, u + 1, 2)) for u in range(UNITS)]


def build(nc, a, out):
    stack = ExitStack()
    with stack:
        def sem(name):
            return stack.enter_context(nc.semaphore(name))

        def keep(name, shape, dt=F32):
            return stack.enter_context(nc.sbuf_tensor(name, shape, dt))

        def place(name, kib, shape, dt=F32):
            with ExitStack() as s:
                if kib > -RING:
                    s.enter_context(nc.sbuf_tensor(name + "_below", [P, int((kib + RING) * 256)], F32))
                return s.enter_context(nc.sbuf_tensor(name, shape, dt))

        X = keep("X", [P, KT, T])
        CK = keep("CK", [P, 384])
        PAR = keep("PAR", [P, 384])
        MOD = keep("MOD", [P, 2, 48, 2])
        SV = keep("SV", [P, KT, 2])
        EPSC = keep("EPSC", [P, 3])
        AB = keep("AB", [P, KT, 2])
        QKG = keep("QKG", [P, 2])
        ONES = keep("ONES", [P, P])
        A0H = keep("A0H", [P, 16])
        KA1 = keep("KA1", [P, KT])
        IDN, HEAD1, SWAP = CK[:, 0:128], CK[:, 128:256], CK[:, 256:384]
        PS = stack.enter_context(nc.psum_tensor("PS", [P, 4096], F32))

        RAW = place("RAW", -48, [P, 2, KT, UC])
        WH = place("WH", -32, [P, 2, KT, UC], F32R)
        WL = place("WL", -16, [P, 2, KT, UC], F32R)
        XT = place("XT", 64, [P, NTT, D])
        ROWS = place("ROWS", 88, [P, 3, P])
        ADA0 = place("ADA0", 0, [P, 4, KT, 512])
        AH = place("AH", 0, [P, KT, T], F32R)
        AL = place("AL", 24, [P, KT, T], F32R)
        QKV = place("QKV", 48, [P, 12, T])
        SQ = place("SQ", 96, [P, 2, T])
        TN = place("TN", 102, [P, 2, T])
        RS = place("RS", 108, [P, T])
        ADW = place("ADW", 119, [P, KT, UC])
        HQ = place("HQ", 0, [P, 2, T])
        HR = place("HR", 6, [P, 2, T])
        HN = place("HN", 12, [P, 2, T])
        HC = place("HC", 18, [P, 2, TX])
        ROPE = place("ROPE", 84, [P, 2, TX])
        OT = place("OT", 0, [P, KT, T])
        KH2 = place("KH2", 24, [P, 2, T], F32R)
        KL2 = place("KL2", 30, [P, 2, T], F32R)
        VS = place("VS", 36, [P, 4, NTT, P], F32R)
        QS = place("QS", 84, [P, 2, T], F32R)
        PB = place("PB", 90, [P, 2, T])
        PTH = place("PTH", 96, [P, NTT, 256], F32R)
        PTL = place("PTL", 102, [P, NTT, 256], F32R)
        OA = place("OA", 108, [P, 256])
        OB = place("OB", 109, [P, 256])
        SMS = place("SMS", 110, [P, 16])
        BH = place("BH", 48, [P, KT, T], F32R)
        BL = place("BL", 72, [P, KT, T], F32R)
        HRL = place("HRL", 96, [P, 2, T])
        HSQ = place("HSQ", 102, [P, 2, T])

        U = place("U", 48, [P, KT, T])
        XX = place("XX", 72, [P, KT, T])
        MX = place("MX", 96, [P, 2, T])
        STG = place("STG", 102, [P, 4, T])
        LW = place("LW", 121.5, [P, T])
        LA = place("LA", 124.5, [P, T])
        LG = place("LG", 127.5, [P, TX])
        SCR = nc.dram_tensor("rwkv_scratch", [3, KT, P, T], F32, kind="Internal").ap()
        core_at = [-RING]

        def core(name, shape, dt=F32):
            t = place(name, core_at[0], shape, dt)
            core_at[0] += -(-math.prod(shape[1:]) // 64) / 4
            return t

        def two(name, shape, dt=F32):
            return [core(f"{name}{i}", shape, dt) for i in range(2)]

        CT = core("CT", [P, CORE_W])
        KG = core("KG", [P, T])
        VG, RG = two("VG", [P, T]), two("RG", [P, TX])
        W2G, A2G, G2G = core("W2G", [P, P]), core("A2G", [P, P]), two("G2G", [P, P])
        W0G = core("W0G", [1, 2, P])
        KK = core("KK", [P, T])
        un_at = core_at[0]
        WI = core("WI", [P, T])
        SG = core("SG", [P, NTT, P])
        UM = place("UM", un_at, [P, 2, 4, P])
        kd_at = core_at[0]
        AA = core("AA", [P, T])
        KD = place("KD", kd_at, [P, T])
        TB = core("TB", [P, T])
        BT = core("BT", [P, T])
        LTA = core("LTA", [P, 12, P])
        XI = core("XI", [P, 12, P])
        XIT = core("XIT", [P, 12, P])
        RKS = core("RKS", [P, TX])
        VT = two("VT", [P, NTT, P])
        AZ = two("AZ", [P, NTT, 2, P])
        RZ = two("RZ", [P, TX // P, 2, P])
        WP = two("WP", [P, NCH, C + 1])
        BKT = two("BKT", [P, NTT, 2, P])
        LKA = two("LKA", [P, 12, P])
        TRR = two("TRR", [P, 8, 2, P])
        XIF = two("XIF", [P, 12, P])
        LV = two("LV", [P, NTT, P])
        OG = core("OG", [P, KT, TX // 2])
        YC, YQ, YT = [core(n, [P, TX]) for n in ("YC", "YQ", "YT")]
        RH, SA = core("RH", [P, P]), core("SA", [P, P])
        SS, SW = core("SS", [P, 2, HD]), core("SW", [P, HD])
        assert core_at[0] <= 121.5, core_at
        OUTT = place("OUTT", 0, [P, 4, D])

        def bank(b):
            return PS[:, b * 512:(b + 1) * 512]

        def pair(b):
            return PS[:, b * 512:b * 512 + 1024]

        def tile_ps(b):
            return PS[:, b * 512 + 256:b * 512 + 1024]

        def col(block, row, n=1):
            return PAR[:, block * 128 + row:block * 128 + row + n]

        ld_const, ld_rows, ld_x, ld_rope = sem("ld_const"), sem("ld_rows"), sem("ld_x"), sem("ld_rope")
        ld_ada0 = [sem(f"ld_ada0_{i}") for i in range(4)]
        raw_landed = [sem("raw_landed0"), sem("raw_landed1")]
        w_high = sem("w_high")
        w_split = sem("w_split")
        w_used = sem("w_used")
        evac_act, evac_dve = sem("evac_act"), sem("evac_dve")
        ada_landed, ada_used, ada_read = sem("ada_landed"), sem("ada_used"), sem("ada_read")
        par_t, par_ready, sv_ready, silu_a = sem("par_t"), sem("par_ready"), sem("sv_ready"), sem("silu_a")
        sv_step = sem("sv_step")
        ones_ready = sem("ones_ready")
        xt_done, xv_act, xv_dve = sem("xt_done"), sem("xv_act"), sem("xv_dve")
        ada0_done, mod_ready = sem("ada0_done"), sem("mod_ready")
        n_sq, n_squsd = sem("norm_squared"), sem("norm_square_used")
        n_ln, n_rs, n_ab, n_t, n_h, n_u = (sem("norm_ln"), sem("norm_rs"), sem("norm_ab"), sem("norm_scaled"),
                                          sem("norm_high"), sem("norm_low"))
        hn_sq, hn_stat, hn_ln, hn_rs, hn_q, hn_sw, hn_c, hn_s, hn_done = [
            sem("hn_" + x) for x in ("sq", "stat", "ln", "rs", "q", "swap", "cos", "sin", "done")]
        v_t, v_high, v_low = sem("v_transposed"), sem("v_high"), sem("v_low")
        k_high, k_low, q_high, q_low = sem("k_high"), sem("k_low"), sem("q_high"), sem("q_low")
        s_done, m_done, nm_done, e_done, r_done = (sem("scores"), sem("row_max"), sem("neg_max"), sem("exps"),
                                                   sem("recip"))
        t_done, pth, ptl, pv_done, oa_done, ob_done, o_done = [
            sem(x) for x in ("p_transposed", "pt_high", "pt_low", "pv", "o_upper", "o_sum", "o_scaled")]
        t_first, pth_first, ptl_first = sem("p_transposed_first"), sem("pt_high_first"), sem("pt_low_first")
        ot_high, ot_low = sem("ot_high"), sem("ot_low")
        h_relu, h_sq, h_high, h_low = (sem("hid_relu"), sem("hid_sq"), sem("hid_high"), sem("hid_low"))
        out_ready, stored = sem("out_ready"), sem("stored")

        xx_step, xx_ready = sem("xx_step"), sem("xx_ready")
        mx_made, mx_high, mx_low, mx_used = sem("mix_made"), sem("mix_high"), sem("mix_low"), sem("mix_used")
        stg_stored = [sem("stage_stored0"), sem("stage_stored1")]
        lora_done, lora_ready, lg_tanh = sem("lora_done"), sem("lora_ready"), sem("lg_tanh")
        consts1, pads_ready = sem("layer1_constants"), sem("pads_ready")
        g_loaded = sem("group_loaded")
        kk_raw, kk_sq, kk_sum, kk_max, kk_ln, kk_rn, kk_ready = [
            sem("kk_" + x) for x in ("raw", "sq", "sum", "max", "ln", "rn", "ready")]
        vt_done, vt_ready = sem("vt_done"), sem("vt_ready")
        z_done, sg_tanh, sg_ready, cum_done = sem("z_done"), sem("sg_tanh"), sem("sg_ready"), sem("cum_done")
        wp_ready, wi_ready, a_done, a_tanh, a_ready = (sem("wp_ready"), sem("wi_ready"), sem("a_done"), sem("a_tanh"),
                                                       sem("a_ready"))
        az_ready, rz_ready, bt_raw, bt_ready, kd_rate, kd_dir, rks_ready, kd_ready = [
            sem(x) for x in ("az_ready", "rz_ready", "bt_raw", "bt_ready", "kd_rate", "kd_dir", "rks_ready", "kd_ready")]
        tb_done, tb_ready = sem("tb_done"), sem("tb_ready")
        mat_done, mat_ready, lta_ready, xit_init = [
            sem(x) for x in ("mat_done", "mat_ready", "lta_ready", "xit_init")]
        u_done, um_ready, xi_done, inv_done, xi_ready, xit_ready = [
            sem(x) for x in ("u_done", "um_ready", "xi_done", "inv_done", "xi_ready", "xit_ready")]
        rhs_done, rh_ready, sa_done, sa_ready, st_done, sw_ready, st_ready, y_done, \
            lv_done, lv_ready = [
            sem(x) for x in ("rhs_done", "rh_ready", "sa_done", "sa_ready", "state_done", "state_decayed",
                             "state_ready", "y_done", "lv_done", "lv_ready")]
        gn_sum, gn_mean, gn_centred, gn_sq, gn_var, gn_ln, gn_rn, gn_scaled, gn_rk, gn_rksum, gn_rkv, gn_affine, gn_gate, \
            og_ready = [sem(x) for x in ("gn_sum", "gn_mean", "gn_centred", "gn_sq", "gn_var", "gn_ln", "gn_rn", "gn_scaled",
                                         "gn_rk", "gn_rksum", "gn_rkv", "gn_affine", "gn_gate", "og_ready")]
        f_done, f_read = sem("final_transposed"), sem("final_read")

        def w_view(w):
            return w.rearrange("(k p) n -> p k n", p=P)

        def load_unit(e, u, s, parts):
            e.wait_ge(w_split, u + 1)
            for dst, src in parts:
                e.dma_start(dst, src).then_inc(raw_landed[s], 16)

        def plain(w, c, s):
            v = w_view(w)
            return [(RAW[:, s, 4 * h:4 * h + 4, :], v[:, 4 * h:4 * h + 4, bass.ds(c, UC)]) for h in range(2)]

        def act_split(e, u, s, landed):
            e.wait_ge(raw_landed[s], 32 * landed)
            e.wait_ge(w_used, u + 1)
            e.activation(WH[:, s], RAW[:, s], ACT.Copy).then_inc(w_high, 1)

        def pool_split(e, u, s):
            e.wait_ge(w_high, u + 1)
            e.tensor_tensor(WL[:, s], RAW[:, s], WH[:, s], ALU.subtract).then_inc(w_split, 1)

        def pe_unit(e, u, s, rh, rl, streams=(0, 1), ntiles=(0, 1), k_ready=None, k_used=None, done=w_used):
            e.wait_ge(w_split, u + 3)
            e.wait_ge(evac_act, u + 1)
            e.wait_ge(evac_dve, u + 1)
            mm = None
            for k in range(KT):
                if k_ready:
                    k_ready(e, k)
                for n in ntiles:
                    for st in streams:
                        lo, hi = STREAMS[st]
                        dst = tile_ps(4 * s + 2 * n)[:, lo:hi]
                        for i, (w, r) in enumerate(((WH, rh), (WL, rh), (WH, rl))):
                            mm = e.matmul(dst, w[:, s, k, n * P:(n + 1) * P], r[:, k, lo:hi],
                                          start=(k == 0 and i == 0), stop=(k == KT - 1 and i == 2),
                                          skip_group_check=True)
                if k_used is not None and k < KT - 1:
                    mm.then_inc(k_used, 1)
            mm.then_inc(done, 1)

        def pe_ada(e, n):
            e.wait_ge(ada_landed, 16 * (n + 1))
            e.wait_ge(ada_read, n + 1)
            for h in range(2):
                for k in range(KT):
                    mm = e.matmul(bank(7)[:, 2 * h:2 * h + 2], ADW[:, k, h * P:(h + 1) * P], SV[:, k, :],
                                  start=(k == 0), stop=(k == KT - 1), skip_group_check=True)
            mm.then_inc(ada_used, 1)

        def dve_ada(e, n):
            e.wait_ge(ada_used, n + 2)
            e.tensor_tensor(MOD[:, :, :, :].rearrange("p l c v -> p (l c) v")[:, bass.ds(2 * n + 16, 2), :],
                            bank(7)[:, 0:4].rearrange("p (n v) -> p n v", v=2),
                            PAR[:, bass.ds(2 * n + 16, 2)].unsqueeze(2).to_broadcast([P, 2, 2]),
                            ALU.add).then_inc(ada_read, 1)

        def load_ada(e, n, layer, c):
            e.wait_ge(ada_used, n + 1)
            e.dma_start(ADW[:, :, :], w_view(a[f"l{layer}_ada_w"])[:, :, bass.ds(c, UC)]).then_inc(ada_landed, 16)

        def norm_ab(e, i, layer, half):
            g = col(0, ROWS_A[f"norm{half + 1}_{layer}"], KT)
            sc = MOD[:, layer, 24 * half + 8:24 * half + 16, :]
            e.scalar_tensor_tensor(out=AB[:, :, :], in0=sc, scalar=1.0,
                                   in1=g.unsqueeze(2).to_broadcast([P, KT, 2]), op0=ALU.add,
                                   op1=ALU.mult).then_inc(n_ab, 1)

        def norm_act_stats(e, i, lo):
            for k in range(KT):
                if k >= 2:
                    e.wait_ge(n_squsd, KT * i + k - 1)
                e.activation(SQ[:, k % 2, lo:], X[:, k, lo:], ACT.Square).then_inc(n_sq, 1)
            e.wait_ge(n_squsd, KT * (i + 1))
            e.activation(RS[:, lo:], tile_ps(0)[:, lo:], ACT.Ln, bias=EPSC[:, 0:1], scale=1.0 / D).then_inc(n_ln, 1)
            e.wait_ge(n_ln, i + 1)
            e.activation(RS[:, lo:], RS[:, lo:], ACT.Exp, scale=-0.5).then_inc(n_rs, 1)

        def norm_pe_stats(e, i, lo):
            for k in range(KT):
                e.wait_ge(n_sq, KT * i + k + 1)
                for st_lo, st_hi in STREAMS:
                    if st_lo >= lo:
                        mm = e.matmul(tile_ps(0)[:, st_lo:st_hi], ONES[:, :], SQ[:, k % 2, st_lo:st_hi],
                                      start=(k == 0), stop=(k == KT - 1), skip_group_check=True)
                mm.then_inc(n_squsd, 1)

        def norm_act_high(e, i, layer, half, lo, dst):
            for k in range(KT):
                e.wait_ge(n_t, KT * i + k + 1)
                for st, (a0, a1) in enumerate(STREAMS):
                    if a0 >= lo:
                        ins = e.activation(dst[:, k, a0:a1], TN[:, k % 2, a0:a1], ACT.Identity,
                                           bias=MOD[:, layer, 24 * half + k, 1 - st:2 - st])
                ins.then_inc(n_h, 1)

        def norm_dve(e, i, layer, half, lo, low):
            norm_ab(e, i, layer, half)
            e.wait_ge(n_ab, i + 1)
            e.wait_ge(n_rs, i + 1)
            for k in range(KT + 1):
                if k < KT:
                    if k >= 2:
                        e.wait_ge(n_h, KT * i + k - 1)
                        if low is not None:
                            e.wait_ge(n_u, KT * low + k - 1)
                    for st, (a0, a1) in enumerate(STREAMS):
                        if a0 >= lo:
                            ins = e.scalar_tensor_tensor(out=TN[:, k % 2, a0:a1], in0=X[:, k, a0:a1],
                                                         scalar=AB[:, k, 1 - st:2 - st], in1=RS[:, a0:a1],
                                                         op0=ALU.mult, op1=ALU.mult)
                    ins.then_inc(n_t, 1)
                if k >= 1 and low is not None:
                    e.wait_ge(n_h, KT * i + k)
                    for st, (a0, a1) in enumerate(STREAMS):
                        if a0 >= lo:
                            ins = e.scalar_tensor_tensor(out=AL[:, k - 1, a0:a1], in0=TN[:, (k - 1) % 2, a0:a1],
                                                         scalar=MOD[:, layer, 24 * half + k - 1, 1 - st:2 - st],
                                                         in1=AH[:, k - 1, a0:a1], op0=ALU.add, op1=ALU.subtract)
                    ins.then_inc(n_u, 1)

        def after_norm(n):
            def wait(e, k):
                e.wait_ge(n_u, KT * n + k + 1)
            return wait

        def mlp_up_act(e, u, s, tile, count, lo, landed):
            act_split(e, u + 1, 1 - s, landed)
            e.wait_ge(w_used, u + 3)
            for n in range(2):
                e.activation(HRL[:, n, lo:], tile_ps(4 * s + 2 * n)[:, lo:], ACT.Relu).then_inc(h_relu, 1)
            e.wait_ge(h_relu, count + 2)
            e.sem_inc(evac_act, 1)
            for n in range(2):
                e.wait_ge(h_sq, count + n + 1)
                e.activation(BH[:, bass.ds(tile + n, 1), lo:].rearrange("p a t -> p (a t)"), HSQ[:, n, lo:],
                             ACT.Copy).then_inc(h_high, 1)

        def mlp_up_dve(e, u, tile, count, lo):
            for n in range(2):
                e.wait_ge(h_relu, count + n + 1)
                e.wait_ge(h_low, count + n + 1)
                e.tensor_tensor(HSQ[:, n, lo:], HRL[:, n, lo:], HRL[:, n, lo:], ALU.mult).then_inc(h_sq, 1)
            e.wait_ge(evac_dve, u + 2)
            e.sem_inc(evac_dve, 1)
            for n in range(2):
                e.wait_ge(h_high, count + n + 1)
                row = bass.ds(tile + n, 1)
                e.tensor_tensor(BL[:, row, lo:].rearrange("p a t -> p (a t)"), HSQ[:, n, lo:],
                                BH[:, row, lo:].rearrange("p a t -> p (a t)"), ALU.subtract).then_inc(h_low, 1)

        def add_act(e, u, s, landed):
            if landed is not None:
                act_split(e, u + 1, 1 - s, landed)
            e.sem_inc(evac_act, 1)

        def add_dve(e, u, s, tile, layer, chunk, lo):
            e.wait_ge(w_used, u + 3)
            for n in range(2):
                for st, (a0, a1) in enumerate(STREAMS):
                    if a0 >= lo:
                        x = X[:, bass.ds(tile + n, 1), a0:a1].rearrange("p a t -> p (a t)")
                        gate = MOD[:, layer, bass.ds(8 * chunk + tile + n, 1), 1 - st:2 - st].rearrange("p a t -> p (a t)")
                        ins = e.scalar_tensor_tensor(out=x, in0=tile_ps(4 * s + 2 * n)[:, a0:a1], scalar=gate, in1=x,
                                                     op0=ALU.mult, op1=ALU.add)
            ins.then_inc(evac_dve, 1)

        ADA_AT = (0, 3, 6, 9, 13)

        def job(n):
            j, r = divmod(n, 6)
            return j, r, (TC if r < 2 else T)

        def first(g, n):
            j, r = divmod(n % 12, 6)
            return 8 * g + 4 * j + r - 2 if n >= 0 else 8 * g - 1

        def attn_pe(e, g, p):
            def transposes(m, l0, l1):
                for l in range(l0, l1):
                    mm = e.transpose(pair(4)[:, l * P:(l + 1) * P], PB[:, m % 2, l * P:(l + 1) * P], IDN)
                return mm

            def values(m):
                j, r, nk = job(m)
                q = m // 2
                e.wait_ge(o_done, 6 * g + q + 1)
                e.wait_ge(r_done, 12 * g + m + 1)
                for b in range(2):
                    rs = 12 + (m - 1 + b) % 4
                    e.matmul(bank(6)[:, 256 + b * P:256 + (b + 1) * P], SMS[:, rs:rs + 1].to_broadcast([P, P]), IDN,
                             start=True, stop=True, skip_group_check=True)
                e.wait_ge(ptl, 12 * g + m + 2)
                for i, pt in enumerate((PTH, PTL)):
                    for l in range(nk // P):
                        mm = e.matmul(bank(6)[:, 0:256], VS[:, 2 * p + j, l, :], pt[:, l, :], start=(i == 0 and l == 0),
                                      stop=(i == 1 and l == nk // P - 1), skip_group_check=True)
                mm.then_inc(pv_done, 1)

            for n in range(14):
                if n < 12:
                    j, r, nk = job(n)
                    if r == 0:
                        e.wait_ge(q_low, 2 * g + j + 1)
                    e.wait_ge(e_done, 12 * g + n + 1)
                    for a0, a1 in ((0, min(nk, 512)), (512, nk)):
                        if a1 > a0:
                            for i, kk in enumerate((KH2, KL2)):
                                mm = e.matmul(pair(2 * (n % 2))[:, a0:a1], QS[:, j, r * P:(r + 1) * P], kk[:, j, a0:a1],
                                              start=(i == 0), stop=(i == 1), skip_group_check=True)
                    mm.then_inc(s_done, 1)
                if 1 <= n < 13:
                    m = n - 1
                    j, r, nk = job(m)
                    e.wait_ge(e_done, 12 * g + m + 3)
                    if job(m - 1)[1] < 2 and m:
                        e.wait_ge(ptl, 12 * g + m + 1)
                    else:
                        e.wait_ge(ptl_first, first(g, m - 1) + 2)
                    mm = transposes(m, 0, min(nk // P, 4))
                    if nk > TC:
                        mm.then_inc(t_first, 1)
                    else:
                        mm.then_inc(t_done, 1)
                if n >= 3 and n % 2:
                    values(n - 2)
                if 1 <= n < 13 and nk > TC:
                    e.wait_ge(ptl, 12 * g + m + 1)
                    transposes(m, 4, NTT).then_inc(t_done, 1)
                if n in ADA_AT:
                    pe_ada(e, 5 * g + ADA_AT.index(n))

        def split_high(e, g, j, n_scores):
            e.wait_ge(s_done, n_scores + 1)
            e.activation(QS[64 * j:64 * j + 64, j, :], QKV[64 * j:64 * j + 64, bass.ds(g, 1), :].rearrange("p a t -> p (a t)"),
                         ACT.Copy).then_inc(q_high, 1)

        def split_low(e, g, j):
            e.wait_ge(q_high, 2 * g + j + 1)
            e.tensor_tensor(QS[64 - 64 * j:128 - 64 * j, j, :], QKV[64 * j:64 * j + 64, bass.ds(g, 1), :].rearrange("p a t -> p (a t)"),
                            QS[64 * j:64 * j + 64, j, :], ALU.subtract).then_inc(q_low, 1)

        def attn_act(e, g):
            def output(q):
                j = q // 3
                e.wait_ge(pv_done, 6 * g + q + 1)
                e.wait_ge(ob_done, 6 * g + q + 1)
                e.activation(OA[64 * j:64 * j + 64, :], bank(6)[64 - 64 * j:128 - 64 * j, 0:256], ACT.Copy).then_inc(oa_done, 1)

            for n in range(13):
                if n < 12:
                    j, r, nk = job(n)
                    e.wait_ge(nm_done, 12 * g + n + 1)
                    e.wait_ge(t_done, 12 * g + n + 1)
                    e.activation(PB[:, n % 2, 0:nk], pair(2 * (n % 2))[:, 0:nk], ACT.Exp, bias=SMS[:, 4 + n % 4:5 + n % 4],
                                 scale=SCALE, accum_out=SMS[:, 8 + n % 4:9 + n % 4]).then_inc(e_done, 1)
                if n:
                    m = n - 1
                    j, r, nk = job(m)
                    if m >= 2 and m % 2 == 0:
                        e.wait_ge(pv_done, 6 * g + m // 2)
                    if nk > TC:
                        e.wait_ge(t_first, first(g, m) + 1)
                        e.activation(PTH[:, 0:4, (m % 2) * P:(m % 2 + 1) * P],
                                     bank(4).rearrange("p (l q) -> p l q", q=P), ACT.Copy).then_inc(pth_first, 1)
                    e.wait_ge(t_done, 12 * g + m + 3)
                    l0 = 4 if nk > TC else 0
                    e.activation(PTH[:, l0:nk // P, (m % 2) * P:(m % 2 + 1) * P],
                                 pair(4)[:, l0 * P:nk].rearrange("p (l q) -> p l q", q=P), ACT.Copy).then_inc(pth, 1)
                    if m >= 2 and m % 2 == 0:
                        output(m // 2 - 1)
                if n == 1:
                    split_high(e, g, 1, 12 * g)
                if n == 8:
                    split_high(e, g + 1, 0, 12 * g + 6)
            output(5)

        def attn_dve(e, g):
            def output(q):
                j, b = divmod(q, 3)
                h = slice(64 * j, 64 * j + 64)
                e.wait_ge(oa_done, 6 * g + q + 1)
                e.tensor_tensor(OB[h, :], bank(6)[h, 0:256], OA[h, :], ALU.add).then_inc(ob_done, 1)
                e.wait_ge(ob_done, 6 * g + q + 2)
                e.tensor_tensor(OT[h, bass.ds(g, 1), b * 256:(b + 1) * 256].rearrange("p a t -> p (a t)"),
                                bank(6)[h, 256:512], OB[h, :], ALU.mult).then_inc(o_done, 1)

            for n in range(13):
                if n < 12:
                    j, r, nk = job(n)
                    e.wait_ge(s_done, 12 * g + n + 2)
                    e.tensor_reduce(SMS[:, n % 4:n % 4 + 1], pair(2 * (n % 2))[:, 0:nk], AX.X, ALU.max).then_inc(m_done, 1)
                    e.wait_ge(m_done, 12 * g + n + 1)
                    e.tensor_scalar(SMS[:, 4 + n % 4:5 + n % 4], SMS[:, n % 4:n % 4 + 1], -SCALE, None, ALU.mult)\
                     .then_inc(nm_done, 1)
                if n:
                    m = n - 1
                    j, r, nk = job(m)
                    e.wait_ge(e_done, 12 * g + m + 3)
                    e.reciprocal(SMS[:, 12 + m % 4:13 + m % 4], SMS[:, 8 + m % 4:9 + m % 4]).then_inc(r_done, 1)
                    cols = slice((m % 2) * P, (m % 2 + 1) * P)
                    l0 = 4 if nk > TC else 0
                    if nk > TC:
                        e.wait_ge(pth_first, first(g, m) + 1)
                        e.tensor_tensor(PTL[:, 0:4, cols], bank(4).rearrange("p (l q) -> p l q", q=P), PTH[:, 0:4, cols],
                                        ALU.subtract).then_inc(ptl_first, 1)
                    e.wait_ge(pth, 12 * g + m + 1)
                    e.tensor_tensor(PTL[:, l0:nk // P, cols], pair(4)[:, l0 * P:nk].rearrange("p (l q) -> p l q", q=P),
                                    PTH[:, l0:nk // P, cols], ALU.subtract).then_inc(ptl, 1)
                    if m >= 2 and m % 2 == 0:
                        output(m // 2 - 1)
                if n - 1 in ADA_AT:
                    dve_ada(e, 5 * g + ADA_AT.index(n - 1))
                if n == 2:
                    split_low(e, g, 1)
                if n == 9:
                    split_low(e, g + 1, 0)
            output(5)
            dve_ada(e, 5 * g + 4)

        MIXES = ((2, 0), (3, 0), (0, TC), (1, 0), (4, 0), (5, TC))

        def mix_used(e, n, k):
            if n < 0:
                return
            if k < KT - 1:
                e.wait_ge(mx_used, 7 * (min(4 * n + 3, 11) + max(0, n - 2)) + k + 1)
            elif n == 3:
                e.wait_ge(lora_done, 1)
            else:
                e.wait_ge(w_used, (U_RKV + 4 * n + 3 if n < 3 else U_LORA) + 3)

        def mix_ready(n):
            def wait(e, k):
                e.wait_ge(mx_low, KT * n + k + 1)
            return wait

        def mix_act(e, n):
            lo = MIXES[n][1]
            for k in range(KT):
                e.wait_ge(mx_made, KT * n + k + 1)
                mix_used(e, n - 1, k)
                e.activation(AH[:, k, lo:], MX[:, k % 2, lo:], ACT.Copy).then_inc(mx_high, 1)

        def mix_dve(e, n):
            row, lo = MIXES[n]
            for k in range(KT + 1):
                if k < KT:
                    if n + k >= 2 or n:
                        e.wait_ge(mx_high, KT * n + k - 1)
                        e.wait_ge(mx_low, KT * n + k - 1)
                    if n == 0:
                        e.wait_ge(xx_ready, k + 1)
                    e.scalar_tensor_tensor(out=MX[:, k % 2, lo:], in0=XX[:, k, lo:], scalar=col(1, 8 * row + k),
                                           in1=U[:, k, lo:], op0=ALU.mult, op1=ALU.add).then_inc(mx_made, 1)
                if k:
                    e.wait_ge(mx_high, KT * n + k)
                    mix_used(e, n - 1, k - 1)
                    e.tensor_tensor(AL[:, k - 1, lo:], MX[:, (k - 1) % 2, lo:], AH[:, k - 1, lo:],
                                    ALU.subtract).then_inc(mx_low, 1)

        def stage(e, j, n, evac):
            s = j % 2
            e.wait_ge(w_used, U_RKV + j + 3)
            if j >= 2:
                e.wait_ge(stg_stored[s], 32 * (j // 2))
            dst, src = STG[:, 2 * s + n, :], tile_ps(4 * s + 2 * n)
            if n == 0:
                e.activation(dst, src, ACT.Copy).then_inc(evac, 1)
            else:
                e.tensor_copy(dst, src).then_inc(evac, 1)

        ORDER = (tuple(range(NCH)), tuple(range(TC // C))[::-1] + tuple(range(TC // C, NCH))[::-1])
        NX = TX // C

        def table(name):
            first, width = OFFSET[name]
            return CT[:, first - CORE_FIRST:first - CORE_FIRST + width]

        def wp_inclusive(d):
            return WP[d][:, :, 1 - d:1 - d + C]

        def wp_exclusive(d):
            return WP[d][:, :, d:d + C]

        def chunks(ap):
            return ap.rearrange("p (c t) -> p c t", t=C)

        HEADS = (slice(0, 64), slice(64, 128))

        def slots(e, chain, build):
            def turn(g, last):
                for n in range(4):
                    gp, d = divmod(n, 2)
                    steps = chain(e, g + gp, d, gp)
                    if n < 3 or not last:
                        build(e, g + (n + 1) // 2, (n + 1) % 2, (n + 1) // 2 % 2, steps)
                    for _ in steps:
                        pass

            with e.Fori(0, KT // 2 - 1) as i:
                turn(2 * i, False)
            turn(KT - 2, True)

        def step(steps):
            if steps is not None:
                next(steps, None)

        def mat_bank(u):
            return (3, 4, 0, 1)[u % 4]

        def pe_build(e, g, d, gp, steps):
            q = 2 * g + d
            r = slice(64 * d, 64 * d + 64)
            e.wait_ge(g_loaded, GROUP_LOADS * 16 * (g + 1) + 16)
            if steps is not None:
                e.wait_ge(um_ready, 18 * q)
                e.wait_ge(xi_ready, 12 * q)
                e.wait_ge(xit_ready, 15 * q)
            for m in range(NTT):
                e.matmul(pair(0)[:, m * P:(m + 1) * P], LW[r, m * P:(m + 1) * P], W2G[r, :], start=True, stop=False,
                         skip_group_check=True)
                mm = e.matmul(pair(0)[:, m * P:(m + 1) * P], ONES[0:1, :], W0G[0:1, d, :], start=False, stop=True,
                              skip_group_check=True)
            mm.then_inc(z_done, 1)
            step(steps)
            for a0, a1 in STREAMS:
                mm = e.matmul(tile_ps(2)[:, a0:a1], A2G[r, :], LA[r, a0:a1], start=True, stop=True, skip_group_check=True)
            mm.then_inc(a_done, 1)
            step(steps)
            e.wait_ge(sg_ready, q + 1)
            for m in range(NTT):
                mm = e.matmul(pair(0)[:, m * P:(m + 1) * P], SG[:, m, :], table(f"cum{d}"), start=True, stop=True,
                              skip_group_check=True)
            mm.then_inc(cum_done, 1)
            step(steps)
            if d == 0:
                e.wait_ge(a_tanh, q + 1)
                e.wait_ge(kk_sq, g + 1)
                for a0, a1 in STREAMS:
                    mm = e.matmul(tile_ps(2)[:, a0:a1], HEAD1, TB[:, a0:a1], start=True, stop=True, skip_group_check=True)
                mm.then_inc(kk_sum, 1)
            step(steps)
            if d == 0:
                e.wait_ge(kk_max, g + 1)
                for m in range(NTT):
                    mm = e.transpose(pair(3)[:, m * P:(m + 1) * P], VG[gp][:, m * P:(m + 1) * P], IDN)
                mm.then_inc(vt_done, 1)
            step(steps)
            step(steps)
            e.wait_ge(bt_ready, q + 1)
            e.wait_ge(kd_ready, q + 1)
            for m in range(NTT):
                for i, src in enumerate((BT, KD)):
                    mm = e.transpose(PS[:, (2 * m + i) * P:(2 * m + i + 1) * P], src[:, m * P:(m + 1) * P], IDN)
            mm.then_inc(tb_done, 1)
            step(steps)
            e.wait_ge(az_ready, 2 * q + 2)
            e.wait_ge(vt_ready, g + 1)

            def times_v(u):
                m, h = divmod(u, 2)
                if u == 8:
                    e.wait_ge(lv_ready, 2 * q + 1)
                mm = e.matmul(bank(2)[:, u % 8 * HD:(u % 8 + 1) * HD], LKA[d][:, u, :], VT[gp][:, m, HEADS[h]], start=True,
                              stop=True, skip_group_check=True)
                if u in (7, 11):
                    mm.then_inc(lv_done, 1)

            for u in range(12):
                m, i = divmod(u, 2)
                src = (BT, KD)[i]
                if u == 2:
                    e.wait_ge(tb_ready, q + 1)
                if u == 4:
                    e.wait_ge(rz_ready, 2 * q + 2)
                if u >= 4:
                    e.wait_ge(mat_ready, 12 * q + u - 3)
                for n, rhs in enumerate((AZ[d][:, m], RZ[d][:, m - 2]) if m >= TC // P else (AZ[d][:, m],)):
                    mm = e.matmul(bank(mat_bank(u))[:, 256 * n:256 * n + 256], src[:, m * P:(m + 1) * P],
                                  rhs.rearrange("p h t -> p (h t)"), start=True, stop=True, skip_group_check=True)
                mm.then_inc(mat_done, 1)
                if u >= 3:
                    e.wait_ge(mat_ready, 12 * q + u - 1)
                    times_v(u - 3)
                step(steps)
            e.wait_ge(mat_ready, 12 * q + 12)
            for u in (9, 10, 11):
                times_v(u)
            step(steps)
            for n in range(19):
                if n < 18:
                    if n >= 2:
                        e.wait_ge(um_ready, 18 * q + n - 1)
                    if n < 3:
                        e.wait_ge(lta_ready, 3 * q + n + 1)
                    elif n >= 6:
                        e.wait_ge(xi_ready, 12 * q + n - 5)
                    for i in range(4):
                        u = 4 * (n % 3) + i
                        mm = e.matmul(bank(n % 2)[:, i * P:(i + 1) * P], LTA[:, u, :], XI[:, u, :] if n >= 3 else IDN,
                                      start=True, stop=True, skip_group_check=True)
                    mm.then_inc(u_done, 1)
                if n >= 4:
                    v = n - 1
                    b = v % 3
                    e.wait_ge(um_ready, 18 * q + v + 1)
                    if v < 6:
                        e.wait_ge(xit_init, 3 * q + b + 1)
                    if v == 3:
                        e.wait_ge(lv_ready, 2 * q + 2)
                    if v >= 5:
                        e.wait_ge(xit_ready, 15 * q + v - 4)
                    if 4 <= v < 15:
                        e.wait_ge(xi_ready, 12 * q + v - 3)
                    if v < 15:
                        for i in range(4):
                            mm = e.matmul(bank(2)[:, i * P:(i + 1) * P], XIT[:, 4 * b + i, :], UM[:, v % 2, i, :], start=True,
                                          stop=True, skip_group_check=True)
                        mm.then_inc(xi_done, 1)
                    for i in range(4):
                        mm = e.matmul(bank(3 + v % 2)[:, i * P:(i + 1) * P], UM[:, v % 2, i, :], XIT[:, 4 * b + i, :],
                                      start=True, stop=True, skip_group_check=True)
                    mm.then_inc(inv_done, 1)
                step(steps)

        def act_build(e, g, d, gp, steps):
            q = 2 * g + d
            e.wait_ge(z_done, q + 1)
            e.activation(SG[:, :, :].rearrange("p m c -> p (m c)"), pair(0)[:, 0:T], ACT.Tanh, scale=0.5).then_inc(sg_tanh, 1)
            step(steps)
            e.wait_ge(a_done, q + 1)
            e.activation(AA[:, :], tile_ps(2), ACT.Tanh, bias=A0H[:, bass.ds(8 * d + g, 1)], scale=0.5).then_inc(a_tanh, 1)
            step(steps)
            if d == 0:
                e.wait_ge(kk_raw, g + 1)
                e.activation(TB[:, :], KK[:, :], ACT.Square).then_inc(kk_sq, 1)
            e.wait_ge(cum_done, q + 1)
            e.activation(wp_inclusive(d), chunks(pair(0)[:, 0:T]), ACT.Exp, scale=-DEC).then_inc(wp_ready, 1)
            e.activation(WI[:, :], pair(0)[:, 0:T], ACT.Exp, scale=DEC).then_inc(wi_ready, 1)
            step(steps)
            if d == 0:
                e.wait_ge(kk_max, g + 1)
                e.activation(TB[:, :], TB[:, :], ACT.Ln, scale=65536.0).then_inc(kk_ln, 1)
                e.wait_ge(kk_ln, g + 1)
                e.activation(TB[:, :], TB[:, :], ACT.Exp, scale=-0.5, bias=EPSC[:, 2:3]).then_inc(kk_rn, 1)
            step(steps)
            if d == 0:
                e.wait_ge(vt_done, g + 1)
                e.activation(VT[gp][:, :, :].rearrange("p m c -> p (m c)"), pair(3)[:, 0:T], ACT.Copy).then_inc(vt_ready, 1)
            step(steps)
            if d == 0:
                e.wait_ge(kd_dir, q + 2)
                if steps is not None:
                    e.wait_ge(gn_rk, g)
                e.activation(RKS[:, :], TB[:, TC:], ACT.Copy).then_inc(rks_ready, 1)
            step(steps)
            e.wait_ge(tb_done, q + 1)
            e.activation(BKT[d][:, :, :, :].rearrange("p m a c -> p (m a c)"), PS[:, 0:2 * T], ACT.Copy).then_inc(tb_ready, 1)
            for _ in range(11):
                step(steps)
            e.wait_ge(lv_done, 2 * q + 1)
            e.activation(LV[d][:, 0:4, :].rearrange("p m c -> p (m c)"), bank(2), ACT.Copy).then_inc(lv_ready, 1)
            for _ in range(2):
                step(steps)
            e.wait_ge(lv_done, 2 * q + 2)
            e.activation(LV[d][:, 4:6, :].rearrange("p m c -> p (m c)"), bank(2)[:, 0:256], ACT.Copy).then_inc(lv_ready, 1)
            step(steps)
            for n in range(19):
                if n >= 4:
                    v = n - 1
                    four = slice(4 * (v % 3), 4 * (v % 3) + 4)
                    if v < 15:
                        e.wait_ge(xi_done, 12 * q + v - 2)
                        e.activation(XI[:, four, :].rearrange("p u t -> p (u t)"), bank(2), ACT.Copy).then_inc(xi_ready, 1)
                    e.wait_ge(inv_done, 15 * q + v - 2)
                    e.activation((XIT if v < 15 else XIF[d])[:, four, :].rearrange("p u t -> p (u t)"), bank(3 + v % 2),
                                 ACT.Copy).then_inc(xit_ready, 1)
                step(steps)

        def pool_build(e, g, d):
            q = 2 * g + d
            if d:
                e.wait_ge(kd_dir, q + 2)
                e.wait_ge(rks_ready, q)
                e.tensor_tensor(RKS[:, :], RKS[:, :], TB[:, TC:], ALU.add).then_inc(rks_ready, 1)
            for b in range(3):
                four = slice(4 * b, 4 * b + 4)
                e.wait_ge(mat_ready, 12 * q + 4 * b + 4)
                e.tensor_tensor(LTA[:, four, :], LTA[:, four, :], IDN.unsqueeze(1).to_broadcast([P, 4, P]),
                                ALU.add).then_inc(lta_ready, 1)
                e.wait_ge(lta_ready, 3 * q + b + 1)
                e.tensor_tensor(XIT[:, four, :], LTA[:, four, :],
                                table(f"level{1 - d}0").unsqueeze(1).to_broadcast([P, 4, P]), ALU.mult).then_inc(xit_init, 1)

        def dve_build(e, g, d, gp, steps):
            q = 2 * g + d
            masks = table(f"masks{d}")
            strict, inclusive = masks[:, 0:P], masks[:, P:]
            if d == 0:
                e.wait_ge(g_loaded, GROUP_LOADS * 16 * (g + 1) + 16)
                e.tensor_scalar(KK[:, :], KG[:, :], PAR[:, bass.ds(P + ROWS_B["k_k"] + g, 1)], None, ALU.mult).then_inc(kk_raw, 1)
            e.wait_ge(sg_tanh, q + 1)
            e.tensor_scalar(SG[:, :, :], SG[:, :, :], 0.5, 0.5, ALU.mult, ALU.add).then_inc(sg_ready, 1)
            step(steps)
            e.wait_ge(a_tanh, q + 1)
            e.tensor_scalar(AA[:, :], AA[:, :], 0.5, 0.5, ALU.mult, ALU.add).then_inc(a_ready, 1)
            step(steps)
            step(steps)
            if d == 0:
                e.wait_ge(kk_sum, g + 1)
                e.tensor_scalar(TB[:, :], tile_ps(2), 1e-24, None, ALU.max).then_inc(kk_max, 1)
            step(steps)
            if d == 0:
                e.wait_ge(kk_rn, g + 1)
                e.tensor_tensor(KK[:, :], KK[:, :], TB[:, :], ALU.mult).then_inc(kk_ready, 1)
                e.wait_ge(kk_ready, g + 1)
            e.wait_ge(a_ready, q + 1)
            e.tensor_scalar(TB[:, :], AA[:, :], PAR[:, bass.ds(P + ROWS_B["k_a"] + g, 1)], KA1[:, bass.ds(g, 1)], ALU.mult,
                            ALU.add).then_inc(kd_rate, 1)
            e.tensor_tensor(BT[:, :], KK[:, :], AA[:, :], ALU.mult).then_inc(bt_raw, 1)
            e.wait_ge(kd_rate, q + 1)
            e.tensor_tensor(TB[:, :], TB[:, :], KG[:, :], ALU.mult).then_inc(kd_dir, 1)
            step(steps)
            e.wait_ge(wi_ready, q + 1)
            e.wait_ge(bt_raw, q + 1)
            e.tensor_tensor(BT[:, :], BT[:, :], WI[:, :], ALU.mult).then_inc(bt_ready, 1)
            e.wait_ge(kd_dir, q + 2)
            e.tensor_tensor(KD[:, :], TB[:, :], WI[:, :], ALU.mult).then_inc(kd_ready, 1)
            step(steps)
            for h, k in enumerate(HEADS):
                e.scalar_tensor_tensor(out=AZ[d][k, :, h, :].rearrange("p m (c t) -> p m c t", t=C),
                                       in0=KK[k, :].rearrange("p (m c t) -> p m c t", c=2, t=C), scalar=-1.0,
                                       in1=wp_exclusive(d)[k].rearrange("p (m c) t -> p m c t", c=2), op0=ALU.mult,
                                       op1=ALU.mult).then_inc(az_ready, 1)
            for h, k in enumerate(HEADS):
                e.tensor_tensor(RZ[d][k, :, h, :].rearrange("p m (c t) -> p m c t", t=C),
                                RG[gp][k, :].rearrange("p (m c t) -> p m c t", c=2, t=C),
                                wp_inclusive(d)[k, TC // C:, :].rearrange("p (m c) t -> p m c t", c=2),
                                ALU.mult).then_inc(rz_ready, 1)
            step(steps)
            for u in range(12):
                m, i = divmod(u, 2)
                e.wait_ge(mat_done, 12 * q + u + 1)
                ps = bank(mat_bank(u)).rearrange("p (a h t) -> p a h t", a=2, h=2)
                if m >= TC // P:
                    e.tensor_tensor(TRR[d][:, 2 * m - 4:2 * m - 2, i, :], ps[:, 1],
                                    inclusive.unsqueeze(1).to_broadcast([P, 2, P]), ALU.mult)
                e.tensor_tensor((LTA, LKA[d])[i][:, 2 * m:2 * m + 2, :], ps[:, 0],
                                strict.unsqueeze(1).to_broadcast([P, 2, P]), ALU.mult).then_inc(mat_ready, 1)
                step(steps)
            step(steps)
            for n in range(19):
                if n < 18:
                    b = n % 3
                    dst = UM[:, n % 2, :, :] if n >= 3 else XI[:, 4 * b:4 * b + 4, :]
                    e.wait_ge(u_done, 18 * q + n + 1)
                    e.tensor_tensor(dst, bank(n % 2).rearrange("p (i t) -> p i t", i=4),
                                    table(f"level{d}{n // 3}").unsqueeze(1).to_broadcast([P, 4, P]),
                                    ALU.mult).then_inc(um_ready, 1)
                step(steps)

        def pe_chain(e, g, d, gp):
            q = 2 * g + d
            e.wait_ge(xit_ready, 15 * q + 15)
            e.wait_ge(lv_ready, 2 * q + 2)
            if d == 0:
                e.wait_ge(og_ready, g + 2)
                e.wait_ge(gn_sum, g + 1)
            for m in range(TC // P, NTT):
                for h, k in enumerate(HEADS):
                    mm = e.matmul(bank(7)[k, m * P - TC:(m + 1) * P - TC], VT[gp][:, m, k], TRR[d][:, 2 * m + h - 4, 1, :],
                                  start=(d == 0 and m == TC // P), stop=False, skip_group_check=True)
            for j, c in enumerate(ORDER[d]):
                m, cp = divmod(c, 2)
                t = slice(64 * cp, 64 * cp + 64)
                out_cols = slice(c * C - TC, (c + 1) * C - TC)
                if j:
                    e.wait_ge(st_ready, 11 * q + j)
                    e.nop(nofuse=True)
                    for h, k in enumerate(HEADS):
                        mm = e.matmul(bank(5 + h)[t, 0:HD], AZ[d][k, m, h, t], SS[k, j % 2, :], start=True, stop=True,
                                      skip_group_check=True)
                    mm.then_inc(rhs_done, 1)
                if j >= NCH - NX:
                    for h, k in enumerate(HEADS):
                        e.matmul(bank(7)[k, out_cols], SS[k, j % 2, :], RZ[d][k, m - 2, h, t], start=False, stop=False,
                                 skip_group_check=True)
                yield
                if j:
                    e.wait_ge(rh_ready, 11 * q + j)
                    e.nop(nofuse=True)
                for h, k in enumerate(HEADS):
                    mm = e.matmul(bank(5)[t, P + 64 * h:P + 64 * h + 64], XIF[d][t, 2 * m + h, t],
                                  RH[t, k] if j else LV[d][t, m, k], start=True, stop=True, skip_group_check=True)
                mm.then_inc(sa_done, 1)
                if j < NCH - 1:
                    for k in HEADS:
                        e.matmul(bank(6)[k, P:P + HD], BKT[d][t, m, 1, k], VT[gp][t, m, k], start=True, stop=False,
                                 skip_group_check=True)
                yield
                e.wait_ge(sa_ready, 12 * q + j + 1)
                e.nop(nofuse=True)
                if j >= NCH - NX:
                    for h, k in enumerate(HEADS):
                        mm = e.matmul(bank(7)[k, out_cols], SA[t, k], TRR[d][t, 2 * m + h - 4, 0, t], start=False,
                                      stop=(d == 1), skip_group_check=True)
                    if j == NCH - 1 and d == 1:
                        mm.then_inc(y_done, 1)
                if j < NCH - 1:
                    for k in HEADS:
                        mm = e.matmul(bank(6)[k, P:P + HD], BKT[d][t, m, 0, k], SA[t, k], start=False, stop=True,
                                      skip_group_check=True)
                    mm.then_inc(st_done, 1)
                yield
            if d == 1:
                e.wait_ge(gn_rk, g + 1)
                e.matmul(bank(6), HEAD1, YT[:, :], start=True, stop=True).then_inc(gn_rksum, 1)
                yield
                e.wait_ge(gn_sum, g + 2)
                e.matmul(bank(5), HEAD1, YC[:, :], start=True, stop=True).then_inc(gn_mean, 1)
                yield
                e.wait_ge(gn_rkv, g + 1)
                e.matmul(bank(6), G2G[gp][:, :], LG[:, :], start=True, stop=True).then_inc(gn_gate, 1)
                yield
                e.wait_ge(gn_sq, g + 1)
                e.matmul(bank(5), HEAD1, YQ[:, :], start=True, stop=True).then_inc(gn_var, 1)

        def act_chain(e, g, d, gp):
            for _ in range(3 * NCH):
                yield
            if d == 1:
                yield
                yield
                e.wait_ge(gn_centred, g + 1)
                e.activation(YQ[:, :], YC[:, :], ACT.Square).then_inc(gn_sq, 1)
                yield
                e.wait_ge(gn_var, g + 1)
                e.activation(YQ[:, :], bank(5), ACT.Ln, bias=EPSC[:, 1:2], scale=1.0 / HD).then_inc(gn_ln, 1)
                e.wait_ge(gn_ln, g + 1)
                e.activation(YQ[:, :], YQ[:, :], ACT.Exp, scale=-0.5).then_inc(gn_rn, 1)

        def dve_chain(e, g, d, gp):
            def par(name):
                return PAR[:, bass.ds(P + ROWS_B[name] + g, 1)]

            q = 2 * g + d
            if d == 1:
                e.wait_ge(rks_ready, 2 * g + 2)
                e.scalar_tensor_tensor(out=YT[:, :], in0=RKS[:, :], scalar=par("r_k"), in1=RG[gp][:, :], op0=ALU.mult,
                                       op1=ALU.mult).then_inc(gn_rk, 1)
            for j, c in enumerate(ORDER[d]):
                m, cp = divmod(c, 2)
                t = slice(64 * cp, 64 * cp + 64)
                total = WP[d][:, c, (C, 0)[d]:(C, 0)[d] + 1]
                if j:
                    e.wait_ge(rhs_done, 11 * q + j)
                    e.tensor_tensor(RH[t, :].rearrange("p (h v) -> p h v", h=2),
                                    pair(5).rearrange("p (h v) -> p h v", h=2)[t, :, 0:HD],
                                    LV[d][t, m, :].rearrange("p (h v) -> p h v", h=2), ALU.add).then_inc(rh_ready, 1)
                    if j < NCH - 1:
                        e.wait_ge(st_ready, 11 * q + j)
                        e.tensor_scalar(SW[:, :], SS[:, j % 2, :], total, None, ALU.mult).then_inc(sw_ready, 1)
                yield
                e.wait_ge(sa_done, 12 * q + j + 1)
                e.tensor_copy(SA[t, :], bank(5)[t, P:2 * P]).then_inc(sa_ready, 1)
                yield
                if j < NCH - 1:
                    e.wait_ge(st_done, 11 * q + j + 1)
                    if j:
                        e.wait_ge(sw_ready, 10 * q + j)
                        e.scalar_tensor_tensor(out=SS[:, (j + 1) % 2, :], in0=bank(6)[:, P:P + HD], scalar=total,
                                               in1=SW[:, :], op0=ALU.mult, op1=ALU.add).then_inc(st_ready, 1)
                    else:
                        e.tensor_scalar(SS[:, 1, :], bank(6)[:, P:P + HD], total, None, ALU.mult).then_inc(st_ready, 1)
                yield
            if d == 1:
                e.wait_ge(y_done, g + 1)
                e.tensor_copy(YC[:, :], bank(7)).then_inc(gn_sum, 1)
                yield
                e.wait_ge(gn_rksum, g + 1)
                e.tensor_tensor(YT[:, :], bank(6), VG[gp][:, TC:], ALU.mult).then_inc(gn_rkv, 1)
                e.wait_ge(gn_mean, g + 1)
                e.wait_ge(gn_sum, g + 2)
                e.scalar_tensor_tensor(out=YC[:, :], in0=bank(5), scalar=-1.0 / HD, in1=YC[:, :], op0=ALU.mult,
                                       op1=ALU.add).then_inc(gn_centred, 1)
                yield
                yield
                e.wait_ge(gn_rn, g + 1)
                e.wait_ge(gn_centred, g + 1)
                e.scalar_tensor_tensor(out=YC[:, :], in0=YC[:, :], scalar=par("ln_w"), in1=YQ[:, :], op0=ALU.mult,
                                       op1=ALU.mult).then_inc(gn_scaled, 1)
                e.wait_ge(gn_scaled, g + 1)
                e.wait_ge(gn_rkv, g + 1)
                e.scalar_tensor_tensor(out=YC[:, :], in0=YC[:, :], scalar=par("ln_b"), in1=YT[:, :], op0=ALU.add,
                                       op1=ALU.add).then_inc(gn_affine, 1)
                e.wait_ge(gn_affine, g + 1)
                e.wait_ge(gn_gate, g + 1)
                half = TX // 2
                e.tensor_tensor(X[:, bass.ds(g, 1), 0:half].rearrange("p a t -> p (a t)"), bank(6)[:, 0:half],
                                YC[:, 0:half], ALU.mult)
                e.tensor_tensor(OG[:, bass.ds(g, 1), :].rearrange("p a t -> p (a t)"), bank(6)[:, half:], YC[:, half:],
                                ALU.mult).then_inc(og_ready, 1)

        block = stack.enter_context(nc.Block())

        @block.sync
        def _(sp):
            sp.dma_start(CK[:, :], a["table"][:, 0:384]).then_inc(ld_const, 16)
            for n, r in list(ROWS_A.items()):
                v = a[PARAM[n]].rearrange("(r c) -> r c", c=P)
                sp.dma_start(ROWS[r:r + v.shape[0], 0, :], v).then_inc(ld_rows, 16)
            for n, r in list(ROWS_C.items()):
                v = a[n].rearrange("b (r c) -> (b r) c", c=P) if n == "c" else a[n].rearrange("(r c) -> r c", c=P)
                sp.dma_start(ROWS[r:r + 8, 2, :], v).then_inc(ld_rows, 16)
            for n, r in list(ROWS_B.items()):
                v = a[PARAM[n]]
                form = {"mu": "i (r c) -> (i r) c", "a0": "i (r c) -> (i r) c", "r_k": "(r h) c -> r (h c)"}
                v = v.rearrange(form.get(n, "(r c) -> r c"), **({"h": 2} if n == "r_k" else {"c": P}))
                sp.dma_start(ROWS[r:r + v.shape[0], 1, :], v).then_inc(ld_rows, 16)
            for h in range(2):
                sp.dma_start(QKG[64 * h:64 * h + 64, 0:1], a["l0_q_gain"].unsqueeze(1)).then_inc(ld_rows, 16)
                sp.dma_start(QKG[64 * h:64 * h + 64, 1:2], a["l0_k_gain"].unsqueeze(1)).then_inc(ld_rows, 16)
            for m in range(NTT):
                src = a["ctx"][0, m * P:(m + 1) * P, :] if m < 2 else a["x"][0, (m - 2) * P:(m - 1) * P, :]
                sp.dma_start(XT[:, m, :], src).then_inc(ld_x, 16)
            for i in range(4):
                sp.dma_start(ADA0[:, i], w_view(a["l0_ada_w"])[:, :, i * 512:(i + 1) * 512]).then_inc(ld_ada0[i], 16)
            with sp.Fori(0, 2) as i:
                for s in range(2):
                    load_unit(sp, U_IN + 2 * i + s, s,
                              [(RAW[:, s, :, 128 * r + 64 * h:128 * r + 64 * h + 64],
                                w_view(a["l0_w_in"])[:, :, bass.ds(512 * i + 256 * h + 128 * s + 64 * r, 64)])
                               for r in range(2) for h in range(2)])
            for s in range(2):
                load_unit(sp, U_IN + 4 + s, s, plain(a["l0_w_in"], D + UC * s, s))
            sp.wait_ge(ada0_done, 1)
            sp.wait_ge(xt_done, 12)
            sp.dma_start(ROPE[:, :, :].rearrange("p a b -> p (a b)"), a["table"][:, OFFSET["rope_cos"][0]:OFFSET["rope_cos"][0] + 2 * TX]).then_inc(ld_rope, 16)
            def load_out0(u):
                load_unit(sp, U_OUT0 + u, u % 2,
                          [(RAW[64 * h:64 * h + 64, u % 2, 4 * g:4 * g + 4, :],
                            a["l0_w_out"].rearrange("(g a r d) n -> g a d r n", g=2, a=2, r=4)[g, h][:, :, u * UC:(u + 1) * UC])
                           for h in range(2) for g in range(2)])

            load_out0(0)
            load_out0(1)
            with sp.Fori(0, 16) as n:
                load_ada(sp, n, 0, n * UC + 2048)
            with sp.Fori(0, 24) as n:
                load_ada(sp, n + 16, 1, n * UC)
            load_out0(2)
            load_out0(3)
            with sp.Fori(0, 4) as c:
                with sp.Fori(0, 2) as i:
                    for s in range(2):
                        load_unit(sp, U_MLP0 + 8 * c + 2 * i + s, s, plain(a["l0_mlp_up"], 1024 * c + 512 * i + 256 * s, s))
                with sp.Fori(0, 2) as i:
                    for s in range(2):
                        v = a["l0_mlp_down"][bass.ds(1024 * c, 1024), :]
                        load_unit(sp, U_MLP0 + 8 * c + 4 + 2 * i + s, s, plain(v, 512 * i + 256 * s, s))
            def load_rkv(j, w):
                load_unit(sp, U_RKV + j, j % 2, plain(a["l1_w_rkv"][w], UC * (j % 4), j % 2))

            def load_lora():
                load_unit(sp, U_LORA, 0, [(RAW[:, 0, :, 64 * (2 * i + d):64 * (2 * i + d) + 64], w_view(a[n][d]))
                                          for i, n in enumerate(("l1_w1", "l1_a1")) for d in range(2)])

            def load_gate():
                v = w_view(a["l1_g1"])
                load_unit(sp, U_LORA + 1, 1, [(RAW[:, 1, 4 * h:4 * h + 4, 0:P], v[:, 4 * h:4 * h + 4, :]) for h in range(2)])

            for j in range(2):
                load_rkv(j, 1)
            for j in range(12):
                if j < 10:
                    load_rkv(j + 2, (1, 2, 0)[(j + 2) // 4])
                elif j == 10:
                    load_lora()
                else:
                    load_gate()
                sp.wait_ge(evac_act, U_RKV + j + 3)
                sp.wait_ge(evac_dve, U_RKV + j + 3)
                for n in range(2):
                    sp.dma_start(SCR[j // 4, 2 * (j % 4) + n], STG[:, 2 * (j % 2) + n, :]).then_inc(stg_stored[j % 2], 16)
            for s in range(2):
                sp.wait_ge(stg_stored[s], 32 * 6)
            sp.wait_ge(w_used, U_LORA + 4)
            sp.dma_start(CT[:, :], a["table"][:, CORE_FIRST:]).then_inc(g_loaded, 16)
            with sp.Fori(0, KT // 2) as pair_of_groups:
                for gp in range(2):
                    g = 2 * pair_of_groups + gp
                    cols = bass.ds(P * g, P)
                    sp.wait_ge(kd_dir, 2 * g + 1)
                    for dst, src in ((KG[:, :], SCR[0, bass.ds(g, 1)].rearrange("a p t -> p (a t)")),
                                     (W2G[:, :], a["l1_w2"].rearrange("d r c -> (d r) c")[:, cols]),
                                     (A2G[:, :], a["l1_a2"].rearrange("d r c -> (d r) c")[:, cols]),
                                     (W0G[:, :, :], a["l1_w0"][:, cols].unsqueeze(0))):
                        sp.dma_start(dst, src).then_inc(g_loaded, 16)
                    sp.wait_ge(og_ready, g + 1)
                    for dst, src in ((VG[gp][:, :], SCR[1, bass.ds(g, 1)].rearrange("a p t -> p (a t)")),
                                     (RG[gp][:, :], SCR[2, bass.ds(g, 1), :, TC:].rearrange("a p t -> p (a t)")),
                                     (G2G[gp][:, :], a["l1_g2"][:, cols])):
                        sp.dma_start(dst, src).then_inc(g_loaded, 16)
            sp.wait_ge(og_ready, KT + 2)
            for s in range(2):
                load_unit(sp, U_OUT1 + s, s, plain(a["l1_w_out"], UC * s, s))
            for s in range(2):
                load_unit(sp, U_OUT1 + 2 + s, s, plain(a["l1_w_out"], UC * (2 + s), s))
            with sp.Fori(0, 4) as c:
                with sp.Fori(0, 2) as i:
                    for s in range(2):
                        load_unit(sp, U_MLP1 + 8 * c + 2 * i + s, s, plain(a["l1_mlp_up"], 1024 * c + 512 * i + 256 * s, s))
                with sp.Fori(0, 2) as i:
                    for s in range(2):
                        v = a["l1_mlp_down"][bass.ds(1024 * c, 1024), :]
                        load_unit(sp, U_MLP1 + 8 * c + 4 + 2 * i + s, s, plain(v, 512 * i + 256 * s, s))
            for i in range(2):
                sp.wait_ge(f_read, 4 * i + 4)
                sp.dma_start(out[0].rearrange("(m p) c -> p m c", p=P)[:, :, 512 * i:512 * i + 512],
                             OUTT[:, :, 512 * i:512 * i + 512]).then_inc(stored, 16)
            sp.wait_ge(stored, 32)

        @block.gpsimd
        def _(pool):
            pool.memset(ONES[:, :], 1.0).then_inc(ones_ready, 1)
            for j, v in enumerate((EPS, GN_EPS, 8 * math.log(2))):
                pool.memset(EPSC[:, j:j + 1], v).then_inc(ones_ready, 1)
            pool.sem_inc(w_split, 2)
            with pool.Fori(0, U_OUT0 // 2) as i:
                for s in range(2):
                    pool_split(pool, 2 * i + s, s)
            pool.wait_ge(ld_rope, 16)

            def rope_cos(idx, s):
                pool.wait_ge(hn_q, idx + 1)
                pool.tensor_tensor(HC[:, s, :], HN[:, s, TC:], ROPE[:, 0, :], ALU.mult).then_inc(hn_c, 1)

            with pool.Fori(0, 5) as i:
                for s in range(2):
                    rope_cos(2 * i + s, s)
            with pool.Fori(U_OUT0 // 2, U_OUT1 // 2) as i:
                for s in range(2):
                    pool_split(pool, 2 * i + s, s)
            pool.wait_ge(w_used, U_LORA + 4)
            pool.memset(WP[0][:, :, 0:1], 1.0).then_inc(pads_ready, 1)
            pool.memset(WP[1][:, :, C:C + 1], 1.0).then_inc(pads_ready, 1)
            for d in range(2):
                pool.memset(AZ[d][:, :, :, :], 0.0).then_inc(pads_ready, 1)
                pool.memset(RZ[d][:, :, :, :], 0.0).then_inc(pads_ready, 1)
            pool_build(pool, 0, 0)

            def pool_slots(g, last):
                for n in range(4):
                    if n < 3 or not last:
                        pool_build(pool, g + (n + 1) // 2, (n + 1) % 2)

            with pool.Fori(0, KT // 2 - 1) as i:
                pool_slots(2 * i, False)
            pool_slots(KT - 2, True)
            with pool.Fori(U_OUT1 // 2, UNITS // 2) as i:
                for s in range(2):
                    pool_split(pool, 2 * i + s, s)

        @block.scalar
        def _(act):
            act.wait_ge(par_ready, 3)
            act.activation(SV[:, :, :].rearrange("p k v -> p v k"), PAR[:, 256:272].rearrange("p (v k) -> p v k", v=2),
                           ACT.Exp, scale=-1.0).then_inc(silu_a, 1)
            act.sem_inc(evac_act, 2)
            for i in range(NTT):
                act.wait_ge(xt_done, 2 * i + 2)
                act.activation(X[:, 4:8, i * P:(i + 1) * P], bank((2 * i + 1) % 4).rearrange("p (k t) -> p k t", k=4),
                               ACT.Copy).then_inc(xv_act, 1)
            act.wait_ge(ones_ready, 4)
            act.wait_ge(xv_dve, NTT)
            act.wait_ge(xv_act, NTT)
            norm_act_stats(act, 0, 0)
            act.wait_ge(mod_ready, 1)
            norm_act_high(act, 0, 0, 0, 0, AH)
            act_split(act, 0, 0, LANDED[0])
            for i in range(3):
                for s in range(2):
                    u = 2 * i + s
                    act_split(act, u + 1, 1 - s, LANDED[u + 1])
                    act.wait_ge(w_used, u + 3)
                    act.activation(QKV[:, bass.ds(2 * u, 1), :].rearrange("p a t -> p (a t)"), tile_ps(4 * s),
                                   ACT.Copy).then_inc(evac_act, 1)
            def head_norm(tiles, idx):
                for s in range(2):
                    act.wait_ge(hn_done, idx + s + 1)
                    act.activation(HQ[:, s, :], tiles[s], ACT.Square).then_inc(hn_sq, 1)
                for s in range(2):
                    act.wait_ge(hn_stat, idx + s + 1)
                    act.activation(HR[:, s, :], tile_ps(2 * s), ACT.Ln, bias=EPSC[:, 0:1], scale=1.0 / HD).then_inc(hn_ln, 1)
                    act.wait_ge(hn_ln, idx + s + 1)
                    act.activation(HR[:, s, :], HR[:, s, :], ACT.Exp, scale=-0.5).then_inc(hn_rs, 1)

            act.wait_ge(evac_act, U_OUT0 + 2)
            act.wait_ge(evac_dve, U_OUT0 + 2)
            with act.Fori(0, 5) as i:
                head_norm([QKV[:, bass.ds(2 * i + s, 1), :].rearrange("p a t -> p (a t)") for s in range(2)], 2 * i)
            for p in range(2):
                act.wait_ge(v_t, p + 1)
                act.activation(VS[:, 2 * p:2 * p + 2, :, 0:HD].rearrange("p j l d -> p l j d"),
                               PS[:, 3072:3072 + T].rearrange("p (l j d) -> p l j d", l=NTT, j=2), ACT.Copy).then_inc(v_high, 1)
            act.wait_ge(hn_done, 12)
            for p in range(2):
                if p:
                    act.wait_ge(t_done, 48 + 2)
                for j in range(2):
                    for h in range(2):
                        act.activation(KH2[64 * h:64 * h + 64, j, :], QKV[64 * j:64 * j + 64, 8 + p, :],
                                       ACT.Copy).then_inc(k_high, 1)
                if not p:
                    act.sem_inc(e_done, 2)
                if p == 0:
                    split_high(act, 0, 0, 0)
                with act.Fori(4 * p, 4 * p + 4) as g:
                    attn_act(act, g)
            act.wait_ge(o_done, 49)
            for k in range(KT):
                act.activation(BH[:, k, :], OT[:, k, :], ACT.Copy).then_inc(ot_high, 1)
            for i in range(2):
                for s in range(2):
                    add_act(act, U_OUT0 + 2 * i + s, s, LANDED[U_OUT0 + 2 * i + s + 1])
            act.wait_ge(evac_dve, U_MLP0 + 2)
            norm_act_stats(act, 1, 0)
            norm_act_high(act, 1, 0, 1, 0, AH)
            with act.Fori(0, 4) as c:
                with act.Fori(0, 2) as i:
                    for s in range(2):
                        u = U_MLP0 + 8 * c + 2 * i + s
                        mlp_up_act(act, u, s, 4 * i + 2 * s, 8 * c + 4 * i + 2 * s, 0, LANDED[U_MLP0] + 4 * c + i + s)
                with act.Fori(0, 2) as i:
                    for s in range(2):
                        add_act(act, U_MLP0 + 8 * c + 4 + 2 * i + s, s, LANDED[U_MLP0] + 4 * c + 2 + i + s)
            act.wait_ge(evac_dve, U_RKV + 2)
            norm_act_stats(act, 2, 0)
            norm_act_high(act, 2, 1, 0, 0, U)
            mix_act(act, 0)
            for j in range(12):
                if j % 4 == 3:
                    mix_act(act, j // 4 + 1)
                act_split(act, U_RKV + j + 1, (j + 1) % 2, LANDED[U_RKV + j + 1])
                stage(act, j, 0, evac_act)
            act_split(act, U_LORA + 1, 1, LANDED[U_LORA + 1])
            mix_act(act, 4)
            mix_act(act, 5)
            act.wait_ge(w_used, U_LORA + 3)
            act.activation(LW[:, :], tile_ps(0), ACT.Tanh).then_inc(evac_act, 1)
            act.wait_ge(w_used, U_LORA + 4)
            act.activation(LG[:, :], tile_ps(4)[:, TC:], ACT.Tanh, scale=0.5).then_inc(lg_tanh, 1)
            act.wait_ge(lg_tanh, 1)
            act.sem_inc(evac_act, 1)
            act.wait_ge(pads_ready, 6)
            act.wait_ge(consts1, 2)
            act_build(act, 0, 0, 0, None)
            slots(act, act_chain, act_build)
            act.wait_ge(og_ready, KT + 2)
            for k in range(KT):
                act.activation(AH[:, k, TC:TC + TX // 2], X[:, k, 0:TX // 2], ACT.Copy)
                act.activation(AH[:, k, TC + TX // 2:], OG[:, k, :], ACT.Copy).then_inc(ot_high, 1)
            act_split(act, U_OUT1, 0, LANDED[U_OUT1])
            for j in range(4):
                add_act(act, U_OUT1 + j, j % 2, LANDED[U_OUT1 + j + 1])
            act.wait_ge(evac_dve, U_MLP1 + 2)
            norm_act_stats(act, 3, TC)
            norm_act_high(act, 3, 1, 1, TC, AH)

            def mlp_act(c, whole):
                with act.Fori(0, 2) as i:
                    for s in range(2):
                        mlp_up_act(act, U_MLP1 + 8 * c + 2 * i + s, s, 4 * i + 2 * s, 32 + 8 * c + 4 * i + 2 * s, TC,
                                   LANDED[U_MLP1 + 1 + s] + 4 * c + i)
                with act.Fori(0, 2 if whole else 1) as i:
                    for s in range(2):
                        add_act(act, U_MLP1 + 8 * c + 4 + 2 * i + s, s, LANDED[U_MLP1 + 1 + s] + 4 * c + 2 + i)

            with act.Fori(0, 3) as c:
                mlp_act(c, True)
            mlp_act(3, False)
            add_act(act, UNITS - 2, 0, LANDED[UNITS - 1])
            add_act(act, UNITS - 1, 1, None)
            act.wait_ge(evac_dve, UNITS + 2)
            norm_act_stats(act, 4, TC)
            for k in range(KT):
                act.wait_ge(f_done, k + 1)
                act.activation(OUTT[:, :, k * P:(k + 1) * P], bank(2 + k % 4).rearrange("p (m c) -> p m c", c=P),
                               ACT.Copy).then_inc(f_read, 1)

        @block.tensor
        def _(pe):
            pe.sem_inc(w_used, 2)
            pe.sem_inc(ada_used, 1)
            pe.wait_ge(ld_const, 16)
            pe.wait_ge(ld_rows, 16 * ROW_LOADS)
            for b in range(3):
                n = (P, 112, 16)[b]
                pe.transpose(bank(7)[:, b * P:b * P + n], ROWS[0:n, b, :], IDN[0:n, 0:n]).then_inc(par_t, 1)
            pe.wait_ge(ld_x, 16 * NTT)
            for i in range(2 * NTT):
                if i >= 4:
                    pe.wait_ge((xv_dve, xv_act)[i % 2], i // 2 - 1)
                for k in range(4):
                    kk = 4 * (i % 2) + k
                    mm = pe.transpose(bank(i % 4)[:, k * P:(k + 1) * P], XT[:, i // 2, kk * P:(kk + 1) * P], IDN)
                mm.then_inc(xt_done, 1)
            pe.wait_ge(sv_ready, 1)
            for i in range(4):
                pe.wait_ge(ld_ada0[i], 16)
                for n in range(4):
                    for k in range(KT):
                        mm = pe.matmul(bank(4)[:, 8 * i + 2 * n:8 * i + 2 * n + 2], ADA0[:, i, k, n * P:(n + 1) * P],
                                       SV[:, k, :], start=(k == 0), stop=(k == KT - 1), skip_group_check=True)
            mm.then_inc(ada0_done, 1)
            pe.wait_ge(ones_ready, 4)
            pe.wait_ge(xv_act, NTT)
            pe.wait_ge(xv_dve, NTT)
            norm_pe_stats(pe, 0, 0)
            with pe.Fori(0, 3) as i:
                for s in range(2):
                    pe_unit(pe, 2 * i + s, s, AH, AL, k_ready=after_norm(0))
            pe.wait_ge(evac_act, U_OUT0 + 2)
            pe.wait_ge(evac_dve, U_OUT0 + 2)

            def head_norm(idx):
                for s in range(2):
                    pe.wait_ge(hn_sq, idx + s + 1)
                    for a0, a1 in STREAMS:
                        mm = pe.matmul(tile_ps(2 * s)[:, a0:a1], HEAD1, HQ[:, s, a0:a1], start=True, stop=True,
                                       skip_group_check=True)
                    mm.then_inc(hn_stat, 1)
                for s in range(2):
                    pe.wait_ge(hn_q, idx + s + 1)
                    pe.matmul(bank(4 + s), SWAP, HN[:, s, TC:], start=True, stop=True).then_inc(hn_sw, 1)

            with pe.Fori(0, 5) as i:
                head_norm(2 * i)
            for p in range(2):
                if p:
                    pe.wait_ge(v_low, 1)
                for l in range(NTT):
                    mm = pe.transpose(PS[:, 3072 + l * P:3072 + (l + 1) * P], QKV[:, 10 + p, l * P:(l + 1) * P], IDN)
                mm.then_inc(v_t, 1)
            pe.wait_ge(hn_done, 12)
            pe.wait_ge(v_low, 2)
            pe.sem_inc(t_done, 2)
            pe.sem_inc(s_done, 1)
            for p in range(2):
                pe.wait_ge(k_low, 4 * p + 4)
                with pe.Fori(4 * p, 4 * p + 4) as g:
                    attn_pe(pe, g, p)
            pe.wait_ge(o_done, 49)

            def ot_ready(e, k):
                e.wait_ge(ot_low, k + 1)

            with pe.Fori(0, 2) as i:
                for s in range(2):
                    pe_unit(pe, U_OUT0 + 2 * i + s, s, BH, BL, k_ready=ot_ready)
            pe.wait_ge(evac_dve, U_MLP0 + 2)
            norm_pe_stats(pe, 1, 0)
            pe.wait_ge(n_ln, 2)
            with pe.Fori(0, 4) as c:
                with pe.Fori(0, 2) as i:
                    for s in range(2):
                        pe_unit(pe, U_MLP0 + 8 * c + 2 * i + s, s, AH, AL, k_ready=after_norm(1))

                def hidden_ready(e, k):
                    e.wait_ge(h_low, 8 * c + k + 3)

                with pe.Fori(0, 2) as i:
                    for s in range(2):
                        pe_unit(pe, U_MLP0 + 8 * c + 4 + 2 * i + s, s, BH, BL, k_ready=hidden_ready)
            pe.wait_ge(evac_act, U_RKV + 2)
            pe.wait_ge(evac_dve, U_RKV + 2)
            norm_pe_stats(pe, 2, 0)
            pe.wait_ge(n_ln, 3)
            for n in range(2):
                for i in range(4):
                    pe_unit(pe, U_RKV + 4 * n + i, i % 2, AH, AL, k_ready=mix_ready(n), k_used=mx_used)
            for i in range(4):
                pe_unit(pe, U_RKV + 8 + i, i % 2, AH, AL, streams=(1,), k_ready=mix_ready(2), k_used=mx_used)
            pe_unit(pe, U_LORA, 0, AH, AL, ntiles=(0,), k_ready=mix_ready(3), k_used=mx_used, done=lora_done)
            pe_unit(pe, U_LORA, 0, AH, AL, ntiles=(1,), k_ready=mix_ready(4), k_used=mx_used)
            pe_unit(pe, U_LORA + 1, 1, AH, AL, streams=(1,), ntiles=(0,), k_ready=mix_ready(5))
            pe.wait_ge(lora_ready, 1)
            pe.wait_ge(evac_act, U_OUT1 + 2)
            pe.wait_ge(evac_dve, U_OUT1 + 2)
            pe.wait_ge(pads_ready, 6)
            pe_build(pe, 0, 0, 0, None)
            slots(pe, pe_chain, pe_build)

            def og_split(e, k):
                e.wait_ge(ot_low, KT + k + 1)

            with pe.Fori(0, 2) as i:
                for s in range(2):
                    pe_unit(pe, U_OUT1 + 2 * i + s, s, AH, AL, streams=(1,), k_ready=og_split)
            pe.wait_ge(evac_act, U_MLP1 + 2)
            pe.wait_ge(evac_dve, U_MLP1 + 2)
            norm_pe_stats(pe, 3, TC)
            pe.wait_ge(n_ln, 4)
            with pe.Fori(0, 4) as c:
                with pe.Fori(0, 2) as i:
                    for s in range(2):
                        pe_unit(pe, U_MLP1 + 8 * c + 2 * i + s, s, AH, AL, streams=(1,), k_ready=after_norm(2))

                def hidden1_ready(e, k):
                    e.wait_ge(h_low, 32 + 8 * c + k + 3)

                with pe.Fori(0, 2) as i:
                    for s in range(2):
                        pe_unit(pe, U_MLP1 + 8 * c + 4 + 2 * i + s, s, BH, BL, streams=(1,), k_ready=hidden1_ready)
            pe.wait_ge(evac_act, UNITS + 2)
            pe.wait_ge(evac_dve, UNITS + 2)
            norm_pe_stats(pe, 4, TC)
            for k in range(KT):
                pe.wait_ge(n_t, KT * 4 + k + 1)
                if k >= 4:
                    pe.wait_ge(f_read, k - 3)
                for m in range(4):
                    mm = pe.transpose(bank(2 + k % 4)[:, m * P:(m + 1) * P], TN[:, k % 2, TC + m * P:TC + (m + 1) * P], IDN)
                mm.then_inc(f_done, 1)

        @block.vector
        def _(dve):
            dve.sem_inc(evac_dve, 2)
            dve.sem_inc(ada_read, 1)
            dve.sem_inc(hn_done, 2)
            dve.sem_inc(h_low, 2)
            dve.wait_ge(par_t, 3)
            dve.tensor_copy(PAR[:, 0:240], bank(7)[:, 0:240]).then_inc(par_ready, 1)
            dve.tensor_copy(PAR[:, 256:272], bank(7)[:, 256:272]).then_inc(par_ready, 2)
            dve.wait_ge(silu_a, 1)
            dve.tensor_scalar(SV[:, :, :], SV[:, :, :], 1.0, None, ALU.add).then_inc(sv_step, 1)
            dve.wait_ge(sv_step, 1)
            dve.reciprocal(SV[:, :, :], SV[:, :, :]).then_inc(sv_step, 1)
            dve.wait_ge(sv_step, 2)
            dve.tensor_tensor(SV[:, :, :], SV[:, :, :], PAR[:, 256:272].rearrange("p (v k) -> p k v", v=2),
                              ALU.mult).then_inc(sv_ready, 1)
            dve.wait_ge(par_ready, 3)
            dve.tensor_scalar(A0H[:, :], col(1, ROWS_B["a0"], 16), 0.5, None, ALU.mult).then_inc(consts1, 1)
            dve.tensor_scalar(KA1[:, :], col(1, ROWS_B["k_a"], KT), -1.0, 1.0, ALU.mult, ALU.add).then_inc(consts1, 1)
            for i in range(NTT):
                dve.wait_ge(xt_done, 2 * i + 1)
                dve.tensor_copy(X[:, 0:4, i * P:(i + 1) * P], bank((2 * i) % 4).rearrange("p (k t) -> p k t", k=4))\
                   .then_inc(xv_dve, 1)
            dve.wait_ge(ada0_done, 1)
            dve.tensor_tensor(MOD[:, 0, 0:16, :], bank(4)[:, 0:32].rearrange("p (n v) -> p n v", v=2),
                              PAR[:, 0:16].unsqueeze(2).to_broadcast([P, 16, 2]), ALU.add).then_inc(mod_ready, 1)
            dve.wait_ge(mod_ready, 1)
            dve.wait_ge(xv_act, NTT)
            dve.wait_ge(xv_dve, NTT)
            norm_dve(dve, 0, 0, 0, 0, 0)
            with dve.Fori(0, 3) as i:
                for s in range(2):
                    u = 2 * i + s
                    dve.wait_ge(w_used, u + 3)
                    dve.tensor_copy(QKV[:, bass.ds(2 * u + 1, 1), :].rearrange("p a t -> p (a t)"), tile_ps(4 * s + 2))\
                       .then_inc(evac_dve, 1)
            dve.wait_ge(evac_act, U_OUT0 + 2)
            dve.wait_ge(evac_dve, U_OUT0 + 2)

            def head_norm(tiles, idx, gain):
                for s in range(2):
                    dve.wait_ge(hn_rs, idx + s + 1)
                    dve.scalar_tensor_tensor(out=HN[:, s, :], in0=tiles[s], scalar=QKG[:, gain:gain + 1],
                                             in1=HR[:, s, :], op0=ALU.mult, op1=ALU.mult).then_inc(hn_q, 1)
                for s in range(2):
                    dve.wait_ge(hn_sw, idx + s + 1)
                    dve.tensor_tensor(HQ[:, s, 0:TX], bank(4 + s), ROPE[:, 1, :], ALU.mult).then_inc(hn_s, 1)
                    dve.tensor_copy(tiles[s][:, 0:TC], HN[:, s, 0:TC])
                    dve.wait_ge(hn_s, idx + s + 1)
                    dve.wait_ge(hn_c, idx + s + 1)
                    dve.tensor_tensor(tiles[s][:, TC:], HC[:, s, :], HQ[:, s, 0:TX], ALU.add).then_inc(hn_done, 1)

            dve.wait_ge(ld_rope, 16)
            with dve.Fori(0, 4) as i:
                head_norm([QKV[:, bass.ds(2 * i + s, 1), :].rearrange("p a t -> p (a t)") for s in range(2)], 2 * i, 0)
            head_norm([QKV[:, 8 + s, :] for s in range(2)], 8, 1)
            dve.sem_inc(ptl, 1)
            dve.sem_inc(ptl_first, 1)
            dve.sem_inc(ob_done, 1)
            dve.sem_inc(o_done, 1)
            for p in range(2):
                dve.wait_ge(v_high, p + 1)
                dve.tensor_tensor(VS[:, 2 * p:2 * p + 2, :, HD:].rearrange("p j l d -> p l j d"),
                                  PS[:, 3072:3072 + T].rearrange("p (l j d) -> p l j d", l=NTT, j=2),
                                  VS[:, 2 * p:2 * p + 2, :, 0:HD].rearrange("p j l d -> p l j d"),
                                  ALU.subtract).then_inc(v_low, 1)
            dve.wait_ge(hn_done, 12)
            for p in range(2):
                dve.wait_ge(k_high, 4 * p + 4)
                for j in range(2):
                    for h in range(2):
                        dve.tensor_tensor(KL2[64 * h:64 * h + 64, j, :], QKV[64 * j:64 * j + 64, 8 + p, :],
                                          KH2[64 * j:64 * j + 64, j, :], ALU.subtract).then_inc(k_low, 1)
                if p == 0:
                    split_low(dve, 0, 0)
                with dve.Fori(4 * p, 4 * p + 4) as g:
                    attn_dve(dve, g)
            dve.wait_ge(o_done, 49)
            for k in range(KT):
                dve.wait_ge(ot_high, k + 1)
                dve.tensor_tensor(BL[:, k, :], OT[:, k, :], BH[:, k, :], ALU.subtract).then_inc(ot_low, 1)
            with dve.Fori(0, 2) as i:
                for s in range(2):
                    add_dve(dve, U_OUT0 + 2 * i + s, s, 4 * i + 2 * s, 0, 2, 0)
            dve.wait_ge(evac_dve, U_MLP0 + 2)
            norm_dve(dve, 1, 0, 1, 0, 1)
            with dve.Fori(0, 4) as c:
                with dve.Fori(0, 2) as i:
                    for s in range(2):
                        mlp_up_dve(dve, U_MLP0 + 8 * c + 2 * i + s, 4 * i + 2 * s, 8 * c + 4 * i + 2 * s, 0)
                with dve.Fori(0, 2) as i:
                    for s in range(2):
                        add_dve(dve, U_MLP0 + 8 * c + 4 + 2 * i + s, s, 4 * i + 2 * s, 0, 5, 0)
            dve.wait_ge(evac_dve, U_RKV + 2)
            norm_dve(dve, 2, 1, 0, 0, None)
            dve.wait_ge(n_h, KT * 3)
            dve.tensor_copy(XX[:, :, 0:TC + 1:TC], U[:, :, 1:TC + 2:TC]).then_inc(xx_step, 1)
            dve.tensor_copy(XX[:, :, TC - 1:T:TX], U[:, :, TC - 2:T - 1:TX]).then_inc(xx_step, 1)
            for k in range(KT):
                for a0, a1 in STREAMS:
                    dve.tensor_tensor(XX[:, k, a0 + 1:a1 - 1], U[:, k, a0:a1 - 2], U[:, k, a0 + 2:a1], ALU.add)\
                       .then_inc(xx_step, 1)
                dve.wait_ge(xx_step, 2 * k + 4)
                dve.scalar_tensor_tensor(out=XX[:, k, :], in0=XX[:, k, :], scalar=0.5, in1=U[:, k, :], op0=ALU.mult,
                                         op1=ALU.subtract).then_inc(xx_ready, 1)
            mix_dve(dve, 0)
            for j in range(12):
                if j % 4 == 3:
                    mix_dve(dve, j // 4 + 1)
                stage(dve, j, 1, evac_dve)
            mix_dve(dve, 4)
            mix_dve(dve, 5)
            dve.wait_ge(w_used, U_LORA + 3)
            dve.tensor_copy(LA[:, :], tile_ps(2)).then_inc(evac_dve, 1)
            dve.wait_ge(lg_tanh, 1)
            dve.tensor_scalar(LG[:, :], LG[:, :], 0.5, 0.5, ALU.mult, ALU.add).then_inc(lora_ready, 1)
            dve.sem_inc(evac_dve, 1)
            dve.sem_inc(og_ready, 2)
            dve.sem_inc(kd_dir, 1)
            dve.sem_inc(gn_sum, 1)
            dve.wait_ge(pads_ready, 6)
            dve.wait_ge(consts1, 2)
            dve_build(dve, 0, 0, 0, None)
            slots(dve, dve_chain, dve_build)
            for k in range(KT):
                dve.wait_ge(ot_high, KT + k + 1)
                dve.tensor_tensor(AL[:, k, TC:TC + TX // 2], X[:, k, 0:TX // 2], AH[:, k, TC:TC + TX // 2], ALU.subtract)
                dve.tensor_tensor(AL[:, k, TC + TX // 2:], OG[:, k, :], AH[:, k, TC + TX // 2:],
                                  ALU.subtract).then_inc(ot_low, 1)
            with dve.Fori(0, 2) as i:
                for s in range(2):
                    add_dve(dve, U_OUT1 + 2 * i + s, s, 4 * i + 2 * s, 1, 2, TC)
            dve.wait_ge(evac_dve, U_MLP1 + 2)
            norm_dve(dve, 3, 1, 1, TC, 2)
            with dve.Fori(0, 4) as c:
                with dve.Fori(0, 2) as i:
                    for s in range(2):
                        mlp_up_dve(dve, U_MLP1 + 8 * c + 2 * i + s, 4 * i + 2 * s, 32 + 8 * c + 4 * i + 2 * s, TC)
                with dve.Fori(0, 2) as i:
                    for s in range(2):
                        add_dve(dve, U_MLP1 + 8 * c + 4 + 2 * i + s, s, 4 * i + 2 * s, 1, 5, TC)
            dve.wait_ge(evac_dve, UNITS + 2)
            dve.wait_ge(n_rs, 5)
            for k in range(KT):
                if k >= 2:
                    dve.wait_ge(f_done, k - 1)
                dve.scalar_tensor_tensor(out=TN[:, k % 2, TC:], in0=X[:, k, TC:], scalar=col(1, ROWS_B["final"] + k),
                                         in1=RS[:, TC:], op0=ALU.mult, op1=ALU.mult).then_inc(n_t, 1)


_INS = ["x", "c", "ctx", "c_ctx", "l0_ada_w", "l0_ada_b", "l0_norm1", "l0_w_in", "l0_q_gain", "l0_k_gain", "l0_w_out",
        "l0_norm2", "l0_mlp_up", "l0_mlp_down", "l1_ada_w", "l1_ada_b", "l1_norm1", "l1_mu", "l1_w_rkv", "l1_w0",
        "l1_w1", "l1_w2", "l1_a0", "l1_a1", "l1_a2", "l1_g1", "l1_g2", "l1_k_k", "l1_k_a", "l1_r_k", "l1_ln_w",
        "l1_ln_b", "l1_w_out", "l1_norm2", "l1_mlp_up", "l1_mlp_down", "final_norm"]


def kernel(**inputs):
    import numpy as _np
    import concourse.bacc as _bacc
    from concourse import mybir as _mybir
    from concourse.bass_utils import run_bass_kernel_spmd as _run

    nc = _bacc.Bacc("TRN2", target_bir_lowering=False, num_devices=1)
    arrays = {name: _np.ascontiguousarray(inputs[name]) for name in _INS}
    arrays["table"] = _np.ascontiguousarray(_np.concatenate(list(TABLE.values()), 1))
    args = {name: nc.dram_tensor(name, v.shape, _mybir.dt.from_np(v.dtype), kind="ExternalInput").ap()
            for name, v in arrays.items()}
    out = nc.dram_tensor("out", (1, TX, D), _mybir.dt.float32, kind="ExternalOutput").ap()
    build(nc, args, out)
    r = _run(nc, [arrays], core_ids=[0])
    return r.results[0]["out"]
```
